# Optimizing a Trainium2 kernel written in Bass

```python
import math
import jax, jax.numpy as jnp
from jax import lax
import numpy as np

D_MODEL = 2048
BATCH = 1
SEQ = 512
DEPTH = 2
DEC_BATCH = 1
DEC_SEQ = 32
PAST_LEN = 1024

CHUNK = 64
N_META = 16
N_A_LAYERS = DEPTH // 2
N_B_LAYERS = DEPTH - N_A_LAYERS
DN_HEAD_DIM = 128
DN_QK_HEADS = D_MODEL // 128
DN_V_HEADS = 2 * DN_QK_HEADS
DN_QK_W = DN_QK_HEADS * DN_HEAD_DIM
DN_V_W = DN_V_HEADS * DN_HEAD_DIM
CONV_W = 4
CONV_DIM = 2 * DN_QK_W + DN_V_W
DN_IN = CONV_DIM + DN_V_W + 2 * DN_V_HEADS
FX_HEAD_DIM = 128
FX_HEADS = D_MODEL // FX_HEAD_DIM
FX_W = FX_HEADS * FX_HEAD_DIM
FX_Q_BLOCK = 128
KV_IN = 2 * FX_W + FX_HEADS
EPS = 1e-6

kernel_name = 'yoco_deltanet_fox_stream_step'

def rms_norm(x, g):
    xf = x.astype(jnp.float32)
    y = xf * lax.rsqrt(jnp.mean(xf * xf, axis=-1, keepdims=True) + EPS)
    return (y * g.astype(jnp.float32)).astype(x.dtype)

def l2_norm(x):
    xf = x.astype(jnp.float32)
    return xf * lax.rsqrt(jnp.sum(xf * xf, axis=-1, keepdims=True) + EPS)

def short_conv(xp, w):
    return lax.conv_general_dilated(
        xp, w[:, None, :].astype(xp.dtype), window_strides=(1,), padding='VALID',
        dimension_numbers=('NWC', 'WIO', 'NWC'), feature_group_count=xp.shape[-1])

def gated_delta_rule(q, k, v, g, beta, s0):
    B, T, HK, DK = q.shape
    HV, DV = v.shape[2], v.shape[3]
    rep = HV // HK
    n = -(-T // CHUNK)
    pad = n * CHUNK - T

    def blocks(a):
        a = jnp.pad(a, [(0, 0), (0, pad)] + [(0, 0)] * (a.ndim - 2))
        a = a.reshape((B, n, CHUNK) + a.shape[2:])
        return jnp.swapaxes(jnp.moveaxis(a, 1, 0), 2, 3)

    idx = jnp.arange(CHUNK)
    incl = idx[:, None] >= idx[None, :]
    strict = idx[:, None] > idx[None, :]
    eye = jnp.eye(CHUNK, dtype=jnp.float32)

    def step(S, inp):
        qc, kc, vc, gc, bc = inp
        qc = jnp.repeat(qc, rep, axis=1)
        kc = jnp.repeat(kc, rep, axis=1)
        G = jnp.cumsum(gc, axis=-1)
        decay = jnp.exp(jnp.where(incl, G[..., :, None] - G[..., None, :], -jnp.inf))
        kk = jnp.einsum('bhik,bhjk->bhij', kc, kc)
        m = jnp.where(strict, bc[..., :, None] * kk * decay, 0.0)
        rhs = jnp.concatenate([vc * bc[..., None], kc * (bc * jnp.exp(G))[..., None]], axis=-1)
        sol = lax.linalg.triangular_solve(m + eye, rhs, left_side=True, lower=True,
                                          unit_diagonal=True)
        u, w = sol[..., :DV], sol[..., DV:]
        v_new = u - jnp.einsum('bhck,bhkv->bhcv', w, S)
        qk = jnp.einsum('bhik,bhjk->bhij', qc, kc) * decay
        o = (jnp.einsum('bhck,bhkv->bhcv', qc * jnp.exp(G)[..., None], S)
             + jnp.einsum('bhij,bhjv->bhiv', qk, v_new))
        g_last = G[..., -1]
        S = (S * jnp.exp(g_last)[..., None, None]
             + jnp.einsum('bhck,bhcv->bhkv', kc * jnp.exp(g_last[..., None] - G)[..., None], v_new))
        return S, o

    s_fin, o = lax.scan(step, s0, (blocks(q), blocks(k), blocks(v), blocks(g), blocks(beta)))
    o = jnp.moveaxis(jnp.swapaxes(o, 2, 3), 0, 1).reshape(B, n * CHUNK, HV, DV)[:, :T]
    return o, s_fin

def delta_layer(h, conv_prev, s0, norm_g, w_in, conv_w, a_log, dt_bias, out_norm_g, w_out):
    f32 = jnp.float32
    B, L, _ = h.shape
    u = rms_norm(h, norm_g) @ w_in
    qkv = u[..., :CONV_DIM]
    z = u[..., CONV_DIM:CONV_DIM + DN_V_W]
    b = u[..., CONV_DIM + DN_V_W:CONV_DIM + DN_V_W + DN_V_HEADS]
    a = u[..., CONV_DIM + DN_V_W + DN_V_HEADS:]
    xp = jnp.concatenate([conv_prev.astype(qkv.dtype), qkv], axis=1)
    conv_state = xp[:, xp.shape[1] - (CONV_W - 1):]
    c = jax.nn.silu(short_conv(xp, conv_w))
    q = l2_norm(c[..., :DN_QK_W].reshape(B, L, DN_QK_HEADS, DN_HEAD_DIM)) * (DN_HEAD_DIM ** -0.5)
    k = l2_norm(c[..., DN_QK_W:2 * DN_QK_W].reshape(B, L, DN_QK_HEADS, DN_HEAD_DIM))
    v = c[..., 2 * DN_QK_W:].reshape(B, L, DN_V_HEADS, DN_HEAD_DIM).astype(f32)
    beta = jax.nn.sigmoid(b.astype(f32))
    g = -jnp.exp(a_log.astype(f32)) * jax.nn.softplus(a.astype(f32) + dt_bias.astype(f32))
    o, s_new = gated_delta_rule(q, k, v, g, beta, s0)
    o = rms_norm(o, out_norm_g) * jax.nn.silu(z.astype(f32)).reshape(B, L, DN_V_HEADS, DN_HEAD_DIM)
    return h + o.reshape(B, L, DN_V_W).astype(h.dtype) @ w_out, conv_state, s_new

def kv_side(h, kv_norm_g, kv_w, f_bias, k_norm_g):
    B, L, _ = h.shape
    u = rms_norm(h, kv_norm_g) @ kv_w
    k = rms_norm(u[..., :FX_W].reshape(B, L, FX_HEADS, FX_HEAD_DIM), k_norm_g)
    v = u[..., FX_W:2 * FX_W].reshape(B, L, FX_HEADS, FX_HEAD_DIM)
    logf = jax.nn.log_sigmoid(u[..., 2 * FX_W:].astype(jnp.float32) + f_bias.astype(jnp.float32))
    return k, v, logf

def fox_queries(h, norm_g, w_in, q_norm_g):
    B, L, _ = h.shape
    u = rms_norm(h, norm_g) @ w_in
    q = rms_norm(u[..., :FX_W].reshape(B, L, FX_HEADS, FX_HEAD_DIM), q_norm_g)
    return q, u[..., FX_W:]

def fox_attend(q, k, v, fq, fk, q_pos, k_pos):
    s = jnp.einsum('bqhd,bkhd->bhqk', q, k).astype(jnp.float32) * (FX_HEAD_DIM ** -0.5)
    s = s + jnp.swapaxes(fq, 1, 2)[..., :, None] - jnp.swapaxes(fk, 1, 2)[..., None, :]
    s = jnp.where(k_pos[None, :] <= q_pos[:, None], s, -jnp.inf)
    p = jax.nn.softmax(s, axis=-1)
    return jnp.einsum('bhqk,bkhd->bqhd', p.astype(v.dtype), v)

def fox_prompt_attend(q, k, v, f):
    B, L, H, d = q.shape
    nb = -(-L // FX_Q_BLOCK)
    pad = nb * FX_Q_BLOCK - L
    qb = jnp.swapaxes(jnp.pad(q, ((0, 0), (0, pad), (0, 0), (0, 0))).reshape(B, nb, FX_Q_BLOCK, H, d), 0, 1)
    fb = jnp.swapaxes(jnp.pad(f, ((0, 0), (0, pad), (0, 0))).reshape(B, nb, FX_Q_BLOCK, H), 0, 1)
    pb = jnp.arange(nb * FX_Q_BLOCK).reshape(nb, FX_Q_BLOCK)
    k_pos = jnp.arange(L)
    o = lax.map(lambda a: fox_attend(a[0], k, v, a[1], f, a[2], k_pos), (qb, fb, pb))
    return jnp.swapaxes(o, 0, 1).reshape(B, nb * FX_Q_BLOCK, H, d)[:, :L]

def fox_out(h, o, z, w_out):
    B, L, _ = h.shape
    return h + (o.reshape(B, L, FX_W) * jax.nn.silu(z)).astype(h.dtype) @ w_out

def setup_inputs(seed: int = 0) -> dict:
    key = jax.random.key(seed)
    ks = jax.random.split(key, 24)
    f32 = jnp.float32

    def nrm(k, shape, scale):
        return jax.random.normal(k, shape, f32) * scale

    dt = jnp.exp(jax.random.uniform(ks[12], (N_A_LAYERS, DN_V_HEADS), f32,
                                    math.log(1e-3), math.log(1e-1)))
    return {
        'x_prompt': nrm(ks[0], (BATCH, SEQ, D_MODEL), 1.0),
        'x_sample': nrm(ks[1], (DEC_BATCH, DEC_SEQ, D_MODEL), 1.0),
        'cache_k': nrm(ks[2], (DEC_BATCH, PAST_LEN, FX_HEADS, FX_HEAD_DIM), 1.0),
        'cache_v': nrm(ks[3], (DEC_BATCH, PAST_LEN, FX_HEADS, FX_HEAD_DIM), 1.0),
        'cache_logf': jax.nn.log_sigmoid(2.5 + nrm(ks[4], (DEC_BATCH, PAST_LEN, FX_HEADS), 1.0)),
        'state_delta': nrm(ks[5], (N_A_LAYERS, DEC_BATCH, DN_V_HEADS, DN_HEAD_DIM, DN_HEAD_DIM),
                           DN_HEAD_DIM ** -0.5),
        'state_conv': nrm(ks[6], (N_A_LAYERS, DEC_BATCH, CONV_W - 1, CONV_DIM), 1.0),
        'meta_tokens': nrm(ks[7], (N_META, D_MODEL), 1.0),
        'a_norm_g': 1.0 + nrm(ks[8], (N_A_LAYERS, D_MODEL), 0.02),
        'a_w_in': nrm(ks[9], (N_A_LAYERS, D_MODEL, DN_IN), D_MODEL ** -0.5),
        'a_conv_w': nrm(ks[10], (N_A_LAYERS, CONV_W, CONV_DIM), CONV_W ** -0.5),
        'a_a_log': jnp.log(jax.random.uniform(ks[11], (N_A_LAYERS, DN_V_HEADS), f32, 1.0, 16.0)),
        'a_dt_bias': dt + jnp.log(-jnp.expm1(-dt)),
        'a_out_norm_g': 1.0 + nrm(ks[13], (N_A_LAYERS, DN_HEAD_DIM), 0.02),
        'a_w_out': nrm(ks[14], (N_A_LAYERS, DN_V_W, D_MODEL), DN_V_W ** -0.5),
        'kv_norm_g': 1.0 + nrm(ks[15], (D_MODEL,), 0.02),
        'kv_w': nrm(ks[16], (D_MODEL, KV_IN), D_MODEL ** -0.5),
        'kv_f_bias': jax.random.uniform(ks[17], (FX_HEADS,), f32, 1.0, 4.0),
        'kv_k_norm_g': 1.0 + nrm(ks[18], (FX_HEAD_DIM,), 0.02),
        'b_norm_g': 1.0 + nrm(ks[19], (N_B_LAYERS, D_MODEL), 0.02),
        'b_w_in': nrm(ks[20], (N_B_LAYERS, D_MODEL, 2 * FX_W), D_MODEL ** -0.5),
        'b_q_norm_g': 1.0 + nrm(ks[21], (N_B_LAYERS, FX_HEAD_DIM), 0.02),
        'b_w_out': nrm(ks[22], (N_B_LAYERS, FX_W, D_MODEL), FX_W ** -0.5),
    }

def reference(x_prompt, x_sample, cache_k, cache_v, cache_logf, state_delta, state_conv,
              meta_tokens, a_norm_g, a_w_in, a_conv_w, a_a_log, a_dt_bias, a_out_norm_g, a_w_out,
              kv_norm_g, kv_w, kv_f_bias, kv_k_norm_g, b_norm_g, b_w_in, b_q_norm_g, b_w_out):
    f32 = jnp.float32
    bp = x_prompt.shape[0]
    n_new = x_sample.shape[1]
    past = cache_k.shape[1]
    meta = jnp.broadcast_to(meta_tokens.astype(x_prompt.dtype)[None], (bp, N_META, D_MODEL))
    hp = jnp.concatenate([meta, x_prompt], axis=1)
    hs = x_sample
    conv0 = jnp.zeros((bp, CONV_W - 1, CONV_DIM), hp.dtype)
    s0 = jnp.zeros((bp, DN_V_HEADS, DN_HEAD_DIM, DN_HEAD_DIM), f32)
    q_pos_s = past + jnp.arange(n_new)
    k_pos_s = jnp.arange(past + n_new)
    delta_p, conv_p, delta_s, conv_s = [], [], [], []
    for layer in range(DEPTH):
        if layer < N_A_LAYERS:
            wa = (a_norm_g[layer], a_w_in[layer], a_conv_w[layer], a_a_log[layer],
                  a_dt_bias[layer], a_out_norm_g[layer], a_w_out[layer])
            hp, c_st, d_st = delta_layer(hp, conv0, s0, *wa)
            conv_p.append(c_st)
            delta_p.append(d_st)
            hs, c_st, d_st = delta_layer(hs, state_conv[layer], state_delta[layer].astype(f32), *wa)
            conv_s.append(c_st)
            delta_s.append(d_st)
        else:
            if layer == N_A_LAYERS:
                k_p, v_p, logf_p = kv_side(hp, kv_norm_g, kv_w, kv_f_bias, kv_k_norm_g)
                f_p = jnp.cumsum(logf_p, axis=1)
                k_s, v_s, logf_s = kv_side(hs, kv_norm_g, kv_w, kv_f_bias, kv_k_norm_g)
                k_all = jnp.concatenate([cache_k.astype(k_s.dtype), k_s], axis=1)
                v_all = jnp.concatenate([cache_v.astype(v_s.dtype), v_s], axis=1)
                f_all = jnp.cumsum(jnp.concatenate([cache_logf.astype(f32), logf_s], axis=1), axis=1)
                f_q_s = f_all[:, past:]
            j = layer - N_A_LAYERS
            q, z = fox_queries(hp, b_norm_g[j], b_w_in[j], b_q_norm_g[j])
            hp = fox_out(hp, fox_prompt_attend(q, k_p, v_p, f_p), z, b_w_out[j])
            q, z = fox_queries(hs, b_norm_g[j], b_w_in[j], b_q_norm_g[j])
            hs = fox_out(hs, fox_attend(q, k_all, v_all, f_q_s, f_all, q_pos_s, k_pos_s), z, b_w_out[j])
    y_prompt = hp[:, N_META:]
    return (y_prompt, hs,
            jnp.stack(delta_p).astype(x_prompt.dtype), jnp.stack(conv_p), k_p, v_p,
            logf_p.astype(x_prompt.dtype),
            jnp.stack(delta_s).astype(state_delta.dtype), jnp.stack(conv_s).astype(state_conv.dtype),
            k_s, v_s, logf_s.astype(cache_logf.dtype))


_drawn_inputs = setup_inputs


def setup_inputs(seed=0):
    import zlib

    import numpy as np

    out = dict(_drawn_inputs(seed))
    spreads = {}
    factors = {'cache_logf': 3.528,
     'a_out_norm_g': 5.21,
     'kv_norm_g': 2.737,
     'kv_k_norm_g': 3.001,
     'b_norm_g': 8.0,
     'b_q_norm_g': 8.0}
    for name, (base, spread) in spreads.items():
        noise = np.random.default_rng([zlib.crc32(name.encode()), seed]).standard_normal(out[name].shape)
        drawn = base * np.exp(spread * noise) if base else spread * noise
        out[name] = __import__('jax').numpy.asarray(drawn.astype(out[name].dtype))
    for name, factor in factors.items():
        out[name] = (out[name] * factor).astype(out[name].dtype)
    return out
```

```python
from contextlib import ExitStack

import concourse.bass as bass
from concourse import mybir

ALU = mybir.AluOpType
ACT = mybir.ActivationFunctionType
AX = mybir.AxisListType
F32 = mybir.dt.float32
F32R = mybir.dt.float32r

P = 128
D = 2048
KT = D // P
N_META = 16
SEQ = 512
PROMPT = N_META + SEQ
SAMPLE = 32
NTOK = PROMPT + SAMPLE
HALF = NTOK // 2
PAST = 1024
EPS = 1e-6

HD = 128
PAIRS = 16
VH = 2 * PAIRS
CONV_W = 4
CONV_TILES = 4 * PAIRS
CONV_DIM = CONV_TILES * P
V_W = VH * HD
OFF_K, OFF_V, OFF_Z, OFF_B = D, 2 * D, CONV_DIM, CONV_DIM + V_W

C = 64
UNITS = 10
NPAD = UNITS * C
TAIL, SAMP = 8, 9
TAIL_N = PROMPT - TAIL * C
SAMP0 = SAMP * C
LEVELS = 6
HIST = CONV_W - 1

FH = 16
KSUB = 8
SUBS = 12
RAW_RING, SPLIT_RING = 3, 2

NEG = -1e30

_at = 0
CONST = {}
for _name, _n in (("ident", P), ("ones", P), ("eye64", C), ("level", LEVELS * C), ("incl", C), ("strict", C),
                  ("causal", P), ("scan", NPAD)):
    CONST[_name] = (_at, _at + _n)
    _at += _n
NCONST = _at


def constants():
    import numpy as np
    c = np.zeros((P, NCONST), np.float32)

    def put(name, a):
        lo, hi = CONST[name]
        c[:, lo:hi] = a
    put("ident", np.eye(P))
    put("ones", 1.0)
    row = np.arange(P)[:, None]
    j = row % C
    i = np.arange(C)[None, :]
    put("eye64", j == i)
    put("level", np.concatenate([((j >> l) % 2 == 1) & ((i >> l) == (j >> l) - 1) for l in range(LEVELS)], 1))
    put("incl", np.where(j <= i, 0.0, NEG))
    put("strict", j < i)
    put("causal", np.where(np.arange(P)[None, :] <= row, 0.0, NEG))
    put("scan", np.broadcast_to((np.arange(NPAD) % C != 0)[None, :], (P, NPAD)))
    return c


class Order:

    def __init__(self, steps, ahead, subs):
        self.steps = steps
        self.subs = subs
        self.ahead = ahead
        self.index, self.count = {}, {}
        for s in steps:
            self.index[s] = self.count.get(s[0], 0)
            self.count[s[0]] = self.index[s] + 1


class Turn:

    def __init__(self, order, p, front=True, behind=True, split=True):
        self.order, self.p, self.front, self.behind, self.split = order, p, front, behind, split
        self.fixed = isinstance(p, int)

    def has(self, kind):
        return self.front if kind in self.order.ahead else self.behind

    def steps(self):
        def runs(s):
            if s[0] in ("scale", "split") and s[1] < 2:
                return self.fixed and self.p == 0
            if s[0] in ("scale", "split") and s[1] >= self.order.subs:
                return self.front and self.split
            return self.has(s[0])
        return [s for s in self.order.steps if runs(s)]

    def turns_before(self, kind):
        return self.p if kind in self.order.ahead else self.p - 1


class Signal:

    def __init__(self, sem, kind, per=1):
        self.sem, self.kind, self.per = sem, kind, per

    def after(self, turn, *args, n=None, ago=0, back=0):
        i = turn.order.index[(self.kind, *args)] - back
        each = turn.order.count[self.kind] * self.per
        value = (turn.turns_before(self.kind) - ago) * each + i * self.per + (self.per if n is None else n)
        return None if turn.fixed and value <= 0 else (self.sem, value)


class Bank:

    def __init__(self, taken):
        self.taken = taken

    def uses(self, s):
        return s[0] in self.taken and self.taken[s[0]][0](*s[1:])

    def free(self, turn, step):
        now = turn.steps()
        for s in reversed(now[:now.index(step)]):
            if self.uses(s):
                return self.taken[s[0]][1].after(turn, *s[1:])
        if turn.fixed and turn.p == 0:
            return None
        before = [s for s in turn.order.steps if s[0] in turn.order.ahead or not (turn.fixed and turn.p == 1)]
        for s in reversed(before):
            if self.uses(s):
                return self.taken[s[0]][1].after(turn, *s[1:], ago=1)
        return None


class Semaphores:

    def __init__(self, nc):
        self.nc, self.held = nc, []

    def semaphore(self, name):
        self.held.append(self.nc.alloc_semaphore(name=name))
        return self.held[-1]

    def retire(self):
        self.nc.all_engine_barrier()
        self.nc.clear_and_free_semaphores(self.held)
        self.nc.all_engine_barrier()
        self.held = []


def wait(engine, point):
    if point is not None:
        engine.wait_ge(*point)


def pair_order():
    at = {k: [] for k in range(SUBS * KSUB + 1)}
    for n in range(SUBS + 2):
        at[max(0, KSUB * (n - SPLIT_RING + 1))].append(("split", n))
    for t in range(4):
        end = (2 * t + 2) * KSUB
        at[end] += [("evac", t), ("conv", t), ("silu", t)]
        if t < 2:
            at[end] += [("square", t)]
            at[end + 4] += [("sumsq", t), ("root", t)]
    for t in (4, 5):
        at[(2 * t + 2) * KSUB].append(("zevac", t))
    at[0] += [("tab",), ("decay",), ("kqn",)]
    k = 2
    for g in range(3):
        for kind in ("kkq", "knat", "vnat"):
            at[k].append((kind, g))
            k += 1
    k0 = 11
    inverse = []
    for b in range(2):
        for l in range(LEVELS):
            inverse += [[("inv1", b, l)], [("inv2", b, l)]]
    for i, s in enumerate(inverse[:12]):
        at[k0 + int(i * 2)] += s
    for i, s in enumerate(inverse[12:]):
        at[k0 + 24 + i * 2] += s
    k1 = k0 + 24
    seq = [(kind, c) for c in (0, 1, 2, 3, 4, 5, 6, 7, 8, 9) for kind in ("seq1", "seq2", "seq3")]
    for i, s in enumerate(seq):
        at[min(k1 + 1 + int(i * 1.9), 93)].append(s)
    at[94] += [("states",), ("osq",)]
    at[40].append(("fetch",))
    for g in range(3):
        at[96].append(("otr", g))
    at[96].append(("put",))
    steps = []
    for k in range(SUBS * KSUB + 1):
        steps += at[k]
        if k < SUBS * KSUB:
            steps.append(("kstep", k // KSUB, k % KSUB))
    return Order(steps, {"split", "kstep", "evac", "conv", "silu", "square", "sumsq", "root", "zevac",
                         "fetch"}, SUBS)


def group(g):
    return list(range(4 * g, min(4 * g + 4, UNITS)))


def norm_and_gates(nc, top, io, keep, scratch):
    with ExitStack() as ctx:
        def sb(name, shape, dt=F32):
            return ctx.enter_context(nc.sbuf_tensor(name, shape, dt))

        def sem(name):
            return top.semaphore(name)

        banks = [ctx.enter_context(nc.psum_tensor(f"p1_bank{i}", [P, 512], F32)) for i in range(8)]
        const, xh, xl = keep["const"], keep["xh"], keep["xl"]
        ident, ones = const["ident"], const["ones"]
        hT = sb("hT", [P, KT, NTOK])
        rows = sb("rows", [P, 2, D])
        vec_rows = sb("vec_rows", [51, P])
        cw_rows = sb("cw_rows", [P, 2, P])
        hist_rows = sb("hist_rows", [96, 2, P])
        wab = sb("wab", [P, KT, 2 * VH])
        gate_in = sb("gate_in", [64, 2])
        sq = sb("sq", [P, 2, NTOK])
        xn = sb("xn", [P, 2, NTOK])
        rt = sb("rt", [P, NTOK])
        rb = sb("rb", [P, NTOK])
        eps = sb("eps", [P, 1])
        gat = sb("gat", [64, 4, NTOK])
        decay_rate = sb("decay_rate", [64, 1])
        GT = sb("GT", [64, NPAD])
        BT = sb("BT", [32, NPAD])
        twice = sb("twice", [64, UNITS, 2, C])
        glast_in = sb("glast_in", [64, UNITS, VH])
        Gs = sb("Gs", [P, 4, PAIRS, UNITS])
        tabs = keep["tabs"]

        row_in = [sem(f"row_in{i}") for i in range(2)]
        small_in = sem("small_in")
        wab_in = sem("wab_in")
        turned = sem("turned")
        took_a = sem("took_a")
        took_v = sem("took_v")
        took_small = sem("took_small")
        squared = sem("squared")
        summed = sem("summed")
        rooted = sem("rooted")
        inverted = sem("inverted")
        normed = sem("normed")
        high = sem("high")
        low = sem("low")
        ab_step = sem("ab_step")
        gate_a = sem("gate_a")
        gate_v = sem("gate_v")
        gate_p = sem("gate_p")
        stored = sem("p1_stored")
        block = ctx.enter_context(nc.Block())

        x_p = io["x_prompt"].rearrange("b t d -> (b t) d")
        x_s = io["x_sample"].rearrange("b t d -> (b t) d")
        tiles = [(P, [(io["meta_tokens"], 0, N_META, 0), (x_p, 0, P - N_META, N_META)])]
        tiles += [(P, [(x_p, P * i - N_META, P, 0)]) for i in range(1, 4)]
        tiles += [(N_META + SAMPLE, [(x_p, SEQ - N_META, N_META, 0), (x_s, 0, SAMPLE, N_META)])]

        @block.sync
        def _(sp):
            sp.dma_start(keep["const_all"][:], io["consts"]).then_inc(small_in, 16)
            for n, name in enumerate(("a_norm_g", "kv_norm_g", "b_norm_g")):
                src = io[name] if name == "kv_norm_g" else io[name].rearrange("l d -> (l d)")
                sp.dma_start(vec_rows[16 * n:16 * n + 16, :], src.rearrange("(k p) -> k p", p=P)).then_inc(small_in, 16)
            for n, name in enumerate(("a_out_norm_g", "kv_k_norm_g", "b_q_norm_g")):
                src = io[name].rearrange("(l d) -> l d", l=1) if name == "kv_k_norm_g" else io[name]
                sp.dma_start(vec_rows[48 + n:49 + n, :], src).then_inc(small_in, 16)
            cw = io["a_conv_w"].rearrange("l w (t p) -> (l w t) p", p=P)
            for n in range(2):
                sp.dma_start(cw_rows[:, n, :], cw[P * n:P * n + P, :]).then_inc(small_in, 16)
            hist = io["state_conv"].rearrange("l b w (t p) -> (l b w t) p", p=P)
            for n in range(2):
                sp.dma_start(hist_rows[:, n, :], hist[96 * n:96 * n + 96, :]).then_inc(small_in, 16)
            sp.dma_start(gate_in[32:64, 0:1], io["a_a_log"].rearrange("l h -> h l")).then_inc(small_in, 16)
            sp.dma_start(gate_in[32:64, 1:2], io["a_dt_bias"].rearrange("l h -> h l")).then_inc(small_in, 16)
            for i, (_, parts) in enumerate(tiles):
                if i >= 2:
                    sp.wait_ge(turned, 2 + 4 * (i - 1))
                for n, (src, r0, nr, at) in enumerate(parts):
                    d = sp.dma_start(rows[at:at + nr, i % 2, :], src[r0:r0 + nr, :])
                    d.then_inc(row_in[i % 2], 16)
                if i == 0:
                    sp.dma_start(wab[:], io["a_w_in"].rearrange("l (k p) n -> p (l k) n", p=P)[:, :, OFF_B:OFF_B + 2 * VH]
                                 ).then_inc(wab_in, 16)
            sp.wait_ge(took_a, 10)
            sp.wait_ge(took_v, 10)
            sp.dma_start(scratch["h0"].rearrange("k p t -> p k t"), hT[:]).then_inc(stored, 16)
            sp.wait_ge(gate_v, 9)
            sp.dma_start(scratch["G"], GT[32:64, :]).then_inc(stored, 16)
            sp.dma_start(scratch["beta"], BT[:]).then_inc(stored, 16)
            sp.wait_ge(stored, 48)

        SMALL = 13 * 16

        @block.tensor
        def _(pe):
            pe.wait_ge(small_in, SMALL)
            nc.tensor.transpose(banks[6][:, 0:51], vec_rows[:, :], ident[0:51, 0:51])
            for n in range(2):
                nc.tensor.transpose(banks[6][:, 64 + 96 * n:160 + 96 * n], hist_rows[:, n, :], ident[0:96, 0:96])
            for n in range(2):
                m = nc.tensor.transpose(banks[7][:, P * n:P * n + P], cw_rows[:, n, :], ident[:, :])
            m.then_inc(turned, 2)
            per_slot = [0, 0]
            for i, (nr, parts) in enumerate(tiles):
                per_slot[i % 2] += 16 * len(parts)
                pe.wait_ge(row_in[i % 2], per_slot[i % 2])
                for q in range(4):
                    b = (4 * i + q) % 4
                    if 4 * i + q >= 4:
                        pe.wait_ge(took_a if b % 2 == 0 else took_v, 2 * (i - 1) + q // 2 + 1)
                    for k in range(4):
                        m = nc.tensor.transpose(banks[b][:, P * k:P * k + nr],
                                                rows[0:nr, i % 2, P * (4 * q + k):P * (4 * q + k) + P],
                                                ident[0:nr, 0:nr])
                    m.then_inc(turned, 1)
            for k in range(KT):
                pe.wait_ge(squared, k + 1)
                for h in range(2):
                    m = nc.tensor.matmul(banks[4 + h][:, 0:HALF], ones[:, :], sq[:, k % 2, h * HALF:(h + 1) * HALF],
                                         start=(k == 0), stop=(k == KT - 1))
                m.then_inc(summed, 1)
            pe.wait_ge(took_a, 10)
            pe.wait_ge(took_v, 10)
            pe.wait_ge(wab_in, 16)
            for k in range(KT):
                pe.wait_ge(normed, k + 1)
                for h in range(2):
                    m = nc.tensor.matmul(banks[h][0:64, 0:HALF], wab[:, k, :], xn[:, k % 2, h * HALF:(h + 1) * HALF],
                                         start=(k == 0), stop=(k == KT - 1))
                m.then_inc(ab_step, 1)
            pe.wait_ge(gate_v, 10)
            pe.wait_ge(took_small, 1)
            for u in range(UNITS):
                for r, b in ((slice(32, 64), 2), (slice(0, 32), 3)):
                    m = nc.tensor.transpose(banks[b][:, 32 * u:32 * u + 32], twice[r, u].rearrange("h c t -> h (c t)"),
                                            ident[r, r])
            m.then_inc(gate_p, 1)
            nc.tensor.matmul(banks[6][:, 0:32 * UNITS], ones[32:64, :], glast_in[32:64].rearrange("h u g -> h (u g)"),
                             start=True, stop=True).then_inc(gate_p, 1)

        @block.scalar
        def _(act):
            act.wait_ge(turned, 2)
            nc.scalar.activation(keep["vec"][:], banks[6][:, 0:51], ACT.Copy)
            nc.scalar.activation(keep["hist"][:].rearrange("p w t -> p (w t)"), banks[6][:, 64:256], ACT.Copy)
            nc.scalar.activation(keep["cw"][:].rearrange("p w t -> p (w t)"), banks[7][:, 0:256], ACT.Copy,
                                 scale=0.5).then_inc(took_small, 1)
            col = 0
            for i, (nr, _) in enumerate(tiles):
                for q in (0, 2):
                    act.wait_ge(turned, 2 + 4 * i + q + 1)
                    nc.scalar.activation(hT[:, 4 * q:4 * q + 4, col:col + nr],
                                         banks[q].rearrange("p (k t) -> p k t", k=4)[:, :, 0:nr],
                                         ACT.Copy).then_inc(took_a, 1)
                col += nr
            act.wait_ge(took_v, 10)
            act.wait_ge(took_a, 10)
            for k in range(KT):
                if k >= 2:
                    act.wait_ge(summed, k - 1)
                nc.scalar.activation(sq[:, k % 2, :], hT[:, k, :], ACT.Square).then_inc(squared, 1)
            act.wait_ge(summed, KT)
            act.wait_ge(gate_v, 1)
            for h in range(2):
                m = nc.scalar.activation(rt[:, h * HALF:(h + 1) * HALF], banks[4 + h][:, 0:HALF], ACT.Sqrt,
                                         bias=eps[:, 0:1], scale=1.0 / D)
            m.then_inc(rooted, 1)
            for k in range(KT):
                act.wait_ge(normed, k + 1)
                nc.scalar.activation(xh[:, k, :], xn[:, k % 2, :], ACT.Copy).then_inc(high, 1)
            act.wait_ge(ab_step, KT)
            for h in range(2):
                s = slice(h * HALF, (h + 1) * HALF)
                nc.scalar.activation(gat[0:32, 0, s], banks[h][0:32, 0:HALF], ACT.Exp, scale=-1.0)
                nc.scalar.activation(gat[32:64, 0, s], banks[h][32:64, 0:HALF], ACT.Identity, bias=gate_in[32:64, 1:2])
                m = nc.scalar.activation(gat[32:64, 1, s], banks[h][32:64, 0:HALF], ACT.Abs, bias=gate_in[32:64, 1:2])
            m.then_inc(gate_a, 1)
            act.wait_ge(gate_a, 1)
            nc.scalar.activation(gat[32:64, 2, :], gat[32:64, 1, :], ACT.Exp, scale=-1.0).then_inc(gate_a, 1)
            nc.scalar.activation(decay_rate[32:64, :], gate_in[32:64, 0:1], ACT.Exp).then_inc(gate_a, 1)
            act.wait_ge(gate_a, 2)
            nc.scalar.activation(gat[32:64, 3, :], gat[32:64, 2, :], ACT.Ln, bias=1.0).then_inc(gate_a, 1)
            act.wait_ge(gate_v, 12)
            nc.scalar.activation(Gs[:, 1], tabs[:, :, 0:10], ACT.Exp)
            nc.scalar.activation(tabs[:, :, 40:50], Gs[:, 0], ACT.Exp)
            nc.scalar.activation(tabs[:, :, 20:30], Gs[:, 2], ACT.Exp).then_inc(gate_a, 1)
            act.wait_ge(gate_p, 2)
            glast = banks[6][:, 0:32 * UNITS].rearrange("p (u q h) -> p h q u", q=PAIRS, h=2)
            for h in range(2):
                m = nc.scalar.activation(tabs[:, :, 50 + 10 * h:60 + 10 * h], glast[:, h], ACT.Exp)
            m.then_inc(gate_a, 1)

        @block.vector
        def _(dve):
            nc.vector.memset(eps[:], EPS).then_inc(gate_v, 1)
            col = 0
            for i, (nr, _) in enumerate(tiles):
                for q in (1, 3):
                    dve.wait_ge(turned, 2 + 4 * i + q + 1)
                    nc.vector.tensor_copy(hT[:, 4 * q:4 * q + 4, col:col + nr],
                                          banks[q].rearrange("p (k t) -> p k t", k=4)[:, :, 0:nr]).then_inc(took_v, 1)
                col += nr
            nc.vector.memset(GT[:], 0.0)
            nc.vector.memset(BT[:], 0.0).then_inc(gate_v, 1)
            dve.wait_ge(rooted, 1)
            nc.vector.reciprocal(rb[:], rt[:]).then_inc(inverted, 1)
            dve.wait_ge(took_small, 1)
            dve.wait_ge(inverted, 1)
            dve.wait_ge(took_a, 10)
            for k in range(KT):
                if k >= 2:
                    dve.wait_ge(high, k - 1)
                    dve.wait_ge(low, k - 1)
                    dve.wait_ge(ab_step, k - 1)
                nc.vector.scalar_tensor_tensor(out=xn[:, k % 2, :], in0=hT[:, k, :], scalar=keep["vec"][:, k:k + 1],
                                               in1=rb[:], op0=ALU.mult, op1=ALU.mult).then_inc(normed, 1)
                dve.wait_ge(high, k + 1)
                nc.vector.tensor_tensor(xl[:, k, :], xn[:, k % 2, :], xh[:, k, :].bitcast(F32),
                                        ALU.subtract).then_inc(low, 1)
            dve.wait_ge(gate_a, 1)
            b = gat[0:32]
            nc.vector.tensor_scalar(b[:, 1, :], b[:, 0, :], 1.0, None, ALU.add).then_inc(gate_v, 1)
            dve.wait_ge(gate_v, 3)
            for dst, src in ((slice(0, PROMPT), slice(0, PROMPT)), (slice(SAMP0, SAMP0 + SAMPLE), slice(PROMPT, NTOK))):
                m = nc.vector.reciprocal(BT[:, dst], b[:, 1, src])
            m.then_inc(gate_v, 1)
            a = gat[32:64]
            dve.wait_ge(gate_a, 4)
            nc.vector.scalar_tensor_tensor(out=a[:, 1, :], in0=a[:, 0, :], scalar=0.0, in1=a[:, 3, :],
                                           op0=ALU.max, op1=ALU.add).then_inc(gate_v, 1)
            dve.wait_ge(gate_v, 5)
            nc.vector.tensor_scalar(a[:, 2, :], a[:, 1, :], decay_rate[32:64, 0:1], -1.0,
                                    ALU.mult, ALU.mult).then_inc(gate_v, 1)
            dve.wait_ge(gate_v, 6)
            nc.vector.tensor_copy(GT[32:64, 0:PROMPT], a[:, 2, 0:PROMPT])
            nc.vector.tensor_copy(GT[32:64, SAMP0:SAMP0 + SAMPLE], a[:, 2, PROMPT:NTOK]).then_inc(gate_v, 1)
            dve.wait_ge(gate_v, 7)
            nc.vector.tensor_tensor_scan(GT[32:64, :], const["scan"][32:64, :], GT[32:64, :], 0.0,
                                         ALU.mult, ALU.add).then_inc(gate_v, 2)
            dve.wait_ge(gate_v, 9)
            for r, x in ((slice(32, 64), GT), (slice(0, 32), BT)):
                nc.vector.tensor_copy(twice[r], x[r].rearrange("h (u c) -> h u c", c=C)[:, :, None, :].broadcast_to([32, UNITS, 2, C]))
            last = GT[32:64].rearrange("h (u c) -> h u c", c=C)[:, :, C - 1:C].broadcast_to([32, UNITS, VH])
            nc.vector.tensor_tensor(glast_in[32:64], last, ident[32:64, None, 32:64].broadcast_to([32, UNITS, VH]),
                                    ALU.mult).then_inc(gate_v, 1)
            dve.wait_ge(gate_p, 2)
            G = banks[2][:, 0:32 * UNITS].rearrange("p (u q h) -> p h q u", q=PAIRS, h=2)
            Bt = banks[3][:, 0:32 * UNITS].rearrange("p (u q h) -> p h q u", q=PAIRS, h=2)
            gl = banks[6][:, 0:32 * UNITS].rearrange("p (u q h) -> p h q u", q=PAIRS, h=2)
            for h in range(2):
                r = slice(64 * h, 64 * h + 64)
                nc.vector.tensor_copy(tabs[r, :, 0:10], G[r, h])
                nc.vector.tensor_copy(Gs[r, 0], G[r, 1 - h])
                nc.vector.tensor_copy(Gs[r, 3], gl[r, h])
                m = nc.vector.tensor_copy(tabs[r, :, 30:40], Bt[r, h])
            m.then_inc(gate_v, 1)
            dve.wait_ge(gate_v, 11)
            nc.vector.tensor_tensor(Gs[:, 2], Gs[:, 3], tabs[:, :, 0:10], ALU.subtract).then_inc(gate_v, 1)
            dve.wait_ge(gate_a, 5)
            nc.vector.scalar_tensor_tensor(out=tabs[:, :, 10:20], in0=Gs[:, 1], scalar=-1.0, in1=tabs[:, :, 30:40],
                                           op0=ALU.mult, op1=ALU.mult).then_inc(gate_v, 1)
            dve.wait_ge(gate_v, 13)
            nc.vector.tensor_scalar(keep["vec"][:, 48:49], keep["vec"][:, 48:49], 0.5, None, ALU.mult)



def delta_layer(nc, top, io, keep, scratch):
    order = pair_order()
    with ExitStack() as ctx:
        def sb(name, shape, dt=F32):
            return ctx.enter_context(nc.sbuf_tensor(name, shape, dt))

        def sem(name):
            return top.semaphore(name)

        def signal(name, kind, per=1):
            return Signal(sem(name), kind, per)

        main = [ctx.enter_context(nc.psum_tensor(f"main{i}", [P, 512], F32)) for i in range(4)]
        E = [ctx.enter_context(nc.psum_tensor(f"E{i}", [P, 512], F32)) for i in range(2)]
        F = [ctx.enter_context(nc.psum_tensor(f"F{i}", [P, 512], F32)) for i in range(2)]
        const, xh, xl, tabs = keep["const"], keep["xh"], keep["xl"], keep["tabs"]
        ident, ones, eye64 = const["ident"], const["ones"], const["eye64"]
        vec, cw, hist = keep["vec"], keep["cw"], keep["hist"]

        w_raw = sb("w_raw", [P, RAW_RING, KSUB, P])
        w_hi = sb("w_hi", [P, SPLIT_RING, KSUB, P], F32R)
        w_lo = sb("w_lo", [P, SPLIT_RING, KSUB, P], F32R)
        xp = sb("xp", [P, 2, NPAD + 8])
        y = sb("y", [P, NPAD])
        th = sb("th", [P, NPAD])
        cqk = sb("cqk", [P, 2, NPAD])
        cv = sb("cv", [P, UNITS, 2, C])
        sq = sb("sq2", [P, NPAD])
        root = sb("root", [P, NPAD])
        rqk = sb("rqk", [P, 2, NPAD])
        zt = sb("zt", [P, NTOK])
        znew = sb("znew", [P, 2, NTOK])
        zs = sb("zs", [P, 2, NTOK])
        kqk = sb("kqk", [P, UNITS, 4, C])
        kc = sb("kc", [P, UNITS, P])
        bv = sb("bv", [P, UNITS, P])
        dec = sb("dec", [P, NPAD])
        bdec = sb("bdec", [P, NPAD])
        MT = sb("MT", [P, UNITS, P])
        QK = sb("QK", [P, UNITS, P])
        Tc = sb("Tc", [P, UNITS, C])
        TTc = sb("TTc", [P, UNITS, C])
        TT = sb("TT", [P, UNITS, P])
        Yc = sb("Yc", [P, 5, C])
        Y = sb("Y", [P, 5, P])
        S = sb("S", [P, 2, 2, HD])
        Rr = sb("Rr", [P, HD])
        oq = sb("oq", [P, HD])
        vn = sb("vn", [P, HD])
        vnd = sb("vnd", [P, 2, HD])
        on = sb("on", [P, UNITS, HD])
        osum = sb("osum", [P, 3, UNITS])
        ot = sb("ot", [P, 2, NTOK])
        ptab = sb("ptab", [P, 70])
        cout = keep["cout"]
        eps = sb("eps2", [P, 1])

        w_in = [sem(f"w_in{i}") for i in range(RAW_RING)]
        hi_made, lo_made, sub_used = sem("hi_made"), sem("lo_made"), sem("sub_used")
        ready = sem("p2_ready")
        xp_made = signal("xp_made", "evac")
        taps = signal("taps", "conv", CONV_W)
        kept = signal("kept", "conv")
        tanh_y = signal("tanh_y", "conv")
        silu = signal("silu", "silu")
        z_tanh = signal("z_tanh", "zevac")
        z_made = signal("z_made", "zevac")
        square = signal("square", "square")
        sumsq = signal("sumsq", "sumsq")
        rooted = signal("rooted2", "root")
        inverted = signal("inverted2", "root")
        tables = signal("tables", "tab")
        g_in, b_in = signal("g_in", "fetch", 32), signal("b_in", "fetch", 32)
        s_in = signal("s_in", "tab", 16)
        s_zero = signal("s_zero", "tab")
        z_moved = signal("z_moved", "tab")
        g_sum = signal("g_sum", "decay", 2)
        dec_made = signal("dec_made", "decay")
        bdec_made = signal("bdec_made", "decay", 2)
        kq_made = signal("kq_made", "kqn", 3)
        kkq_sum, kkq_took = signal("kkq_sum", "kkq"), signal("kkq_took", "kkq")
        knat_t, kc_made = signal("knat_t", "knat"), signal("kc_made", "knat")
        vnat_t, bv_made = signal("vnat_t", "vnat"), signal("bv_made", "vnat")
        mt_sum, y_made, y_spread = signal("mt_sum", "inv1"), signal("y_made", "inv1"), signal("y_spread", "inv1")
        ty_sum, t_made, tt_spread = signal("ty_sum", "inv2"), signal("t_made", "inv2", 2), signal("tt_spread", "inv2")
        ks_sum, r_made, oq_made = signal("ks_sum", "seq1"), signal("r_made", "seq1"), signal("oq_made", "seq1")
        vn_sum, vn_made = signal("vn_sum", "seq2"), signal("vn_made", "seq2")
        os_sum, s_made = signal("os_sum", "seq3"), signal("s_made", "seq3")
        o_squared, o_summed = signal("o_squared", "osq"), signal("o_summed", "osq")
        o_rooted, o_normed = signal("o_rooted", "osq"), signal("o_normed", "osq", 2)
        o_turned, o_gated = signal("o_turned", "otr"), signal("o_gated", "otr")
        o_out = signal("o_out", "put", 16)
        s_out = signal("s_out", "states", 32)

        bank_e = [
            Bank({"kkq": (lambda g: g % 2 == 0, kkq_took), "knat": (lambda g: g % 2 == 1, kc_made),
                  "vnat": (lambda g: g % 2 == 0, bv_made), "inv1": (lambda b, l: True, y_made),
                  "inv2": (lambda b, l: 0 < l < LEVELS - 1, t_made), "otr": (lambda g: g % 2 == 0, o_gated),
                  "sumsq": (lambda t: True, rooted)}),
            Bank({"kkq": (lambda g: g % 2 == 1, kkq_took), "knat": (lambda g: g % 2 == 0, kc_made),
                  "vnat": (lambda g: g % 2 == 1, bv_made), "inv2": (lambda b, l: True, t_made),
                  "otr": (lambda g: g % 2 == 1, o_gated), "sumsq": (lambda t: True, rooted)}),
        ]


        def turns(engine, body):
            body(Turn(order, 0, behind=False))
            body(Turn(order, 1))
            with engine.Fori(2, PAIRS - 1) as p:
                body(Turn(order, p))
            body(Turn(order, PAIRS - 1, split=False))
            body(Turn(order, PAIRS, front=False))

        block = ctx.enter_context(nc.Block())

        @block.sync
        def _(sp):
            w = io["a_w_in"].rearrange("l (k p) n -> p (l k) n", p=P)

            def body(turn):
                if not turn.front:
                    return
                p = turn.p
                column = [P * p, OFF_K + P * p, OFF_V + 2 * P * p, OFF_V + 2 * P * p + P,
                          OFF_Z + 2 * P * p, OFF_Z + 2 * P * p + P]
                for n in range(SUBS):
                    if not (turn.fixed and SUBS * p + n < RAW_RING):
                        sp.wait_ge(lo_made, SUBS * p + n - RAW_RING + 1)
                    k0 = KSUB * (n % 2)
                    sp.dma_start(w_raw[:, n % RAW_RING], w[:, k0:k0 + KSUB, bass.ds(column[n // 2], P)]
                                 ).then_inc(w_in[n % RAW_RING], 16)
            turns(sp, body)

        @block.gpsimd
        def _(pool):
            nc.gpsimd.memset(MT[:], 0.0)
            nc.gpsimd.memset(QK[:], 0.0)
            nc.gpsimd.memset(TT[:], 0.0)
            nc.gpsimd.memset(Y[:], 0.0)
            nc.gpsimd.memset(vnd[:], 0.0)
            nc.gpsimd.memset(zt[:], 0.0)
            nc.gpsimd.memset(xp[:], 0.0).then_inc(ready, 1)

        @block.tensor
        def _(pe):
            pe.wait_ge(ready, 1)

            def body(turn):
                p = turn.p
                for step in turn.steps():
                    what, *a = step
                    if what == "kstep":
                        n, k = a
                        t = n // 2
                        if k == 0:
                            pe.wait_ge(lo_made, SUBS * p + n + 1)
                            if n % 2 == 0 and not (turn.fixed and p == 0 and t < 2):
                                wait(pe, z_made.after(turn, 4 + t, ago=1) if t < 2 else xp_made.after(turn, t - 2))
                        for hi, x in ((w_hi, xh), (w_hi, xl), (w_lo, xh)):
                            for h in range(2):
                                m = nc.tensor.matmul(main[2 * (t % 2) + h][:, 0:HALF], hi[:, n % SPLIT_RING, k, :],
                                                     x[:, KSUB * (n % 2) + k, h * HALF:(h + 1) * HALF],
                                                     start=(n % 2 == 0 and k == 0 and hi is w_hi and x is xh),
                                                     stop=(n % 2 == 1 and k == KSUB - 1 and hi is w_lo))
                        if k == KSUB - 1:
                            m.then_inc(sub_used, 1)
                    elif what == "sumsq":
                        t, = a
                        wait(pe, square.after(turn, t))
                        for e in range(2):
                            wait(pe, bank_e[e].free(turn, step))
                        for e in range(2):
                            m = nc.tensor.matmul(E[e][:, 0:NPAD // 2], ones[:, :], sq[:, e * NPAD // 2:(e + 1) * NPAD // 2],
                                                 start=True, stop=True)
                        m.then_inc(sumsq.sem, 1)
                    elif what == "kkq":
                        g, = a
                        wait(pe, kq_made.after(turn))
                        wait(pe, bank_e[g % 2].free(turn, step))
                        for i, u in enumerate(group(g)):
                            m = nc.tensor.matmul(E[g % 2][:, P * i:P * i + P], kqk[:, u, 0:2, :].rearrange("p s c -> p (s c)"),
                                                 kqk[:, u, 1:3, :], start=True, stop=True)
                        m.then_inc(kkq_sum.sem, 1)
                    elif what == "knat":
                        g, = a
                        wait(pe, bank_e[1 - g % 2].free(turn, step))
                        for i, u in enumerate(group(g)):
                            m = nc.tensor.transpose(E[1 - g % 2][:, P * i:P * i + P], kqk[:, u, 0:2, :].rearrange("p s c -> p (s c)"), ident[:, :])
                        m.then_inc(knat_t.sem, 1)
                    elif what == "vnat":
                        g, = a
                        wait(pe, bank_e[g % 2].free(turn, step))
                        for i, u in enumerate(group(g)):
                            m = nc.tensor.transpose(E[g % 2][:, P * i:P * i + P], cv[:, u].rearrange("p s c -> p (s c)"), ident[:, :])
                        m.then_inc(vnat_t.sem, 1)
                    elif what == "inv1":
                        b, l = a
                        wait(pe, bank_e[0].free(turn, step))
                        wait(pe, t_made.after(turn, b, l - 1) if l else kkq_took.after(turn, 2))
                        for i in range(5):
                            u = 5 * b + i
                            m = nc.tensor.matmul(E[0][:, C * i:C * i + C], MT[:, u, :],
                                                 Tc[:, u, :] if l else eye64[:, :], start=True, stop=True)
                        m.then_inc(mt_sum.sem, 1)
                    elif what == "inv2":
                        b, l = a
                        wait(pe, bank_e[1].free(turn, step))
                        wait(pe, y_spread.after(turn, b, l))
                        if l:
                            wait(pe, tt_spread.after(turn, b, l - 1))
                        if 0 < l < LEVELS - 1:
                            wait(pe, bank_e[0].free(turn, step))
                        for i in range(5):
                            u = 5 * b + i
                            if 0 < l < LEVELS - 1:
                                nc.tensor.matmul(E[0][:, C * i:C * i + C], TT[:, u, :], Yc[:, i, :],
                                                 start=True, stop=True)
                            m = nc.tensor.matmul(E[1][:, C * i:C * i + C], Y[:, i, :],
                                                 TTc[:, u, :] if l else eye64[:, :], start=True, stop=True)
                        m.then_inc(ty_sum.sem, 1)
                    elif what == "seq1":
                        c, = a
                        if c == 0 or c == SAMP:
                            wait(pe, s_zero.after(turn))
                            wait(pe, s_in.after(turn))
                        if c > 0:
                            wait(pe, s_made.after(turn, c - 1))
                        elif not (turn.fixed and p == 1):
                            wait(pe, s_made.after(turn, SAMP, ago=1))
                        s = S[:, 1 if c == SAMP else 0]
                        nc.tensor.matmul(F[0][:, 0:HD], kqk[:, c, 1:3, :].rearrange("p s c -> p (s c)"), s[:, 0, :], start=True, stop=True)
                        nc.tensor.matmul(F[0][:, HD:2 * HD], kqk[:, c, 2:4, :].rearrange("p s c -> p (s c)"), s[:, 1, :], start=True, stop=True
                                         ).then_inc(ks_sum.sem, 1)
                    elif what == "seq2":
                        c, = a
                        wait(pe, r_made.after(turn, c))
                        wait(pe, tt_spread.after(turn, c // 5, LEVELS - 1))
                        nc.tensor.matmul(F[1][:, 0:HD], TT[:, c, :], Rr[:, :], start=True, stop=True
                                         ).then_inc(vn_sum.sem, 1)
                    elif what == "seq3":
                        c, = a
                        wait(pe, oq_made.after(turn, c))
                        wait(pe, vn_made.after(turn, c))
                        if c == 0:
                            wait(pe, kc_made.after(turn, 2))
                        nc.tensor.matmul(F[0][:, 0:HD], QK[:, c, :], vn[:, :], start=True, stop=True)
                        nc.tensor.matmul(F[0][:, HD:3 * HD], kc[:, c, :], vnd[:].rearrange("p h v -> p (h v)"),
                                         start=True, stop=True).then_inc(os_sum.sem, 1)
                    elif what == "otr":
                        g, = a
                        wait(pe, o_normed.after(turn))
                        wait(pe, bank_e[g % 2].free(turn, step))
                        for i, u in enumerate(group(g)):
                            m = nc.tensor.transpose(E[g % 2][:, P * i:P * i + P], on[:, u, :], ident[:, :])
                        m.then_inc(o_turned.sem, 1)
            turns(pe, body)

        @block.scalar
        def _(act):
            act.wait_ge(ready, 1)

            def body(turn):
                p = turn.p
                again = not (turn.fixed and p == 1)
                for step in turn.steps():
                    what, *a = step
                    if what == "split":
                        n, = a
                        act.wait_ge(w_in[n % RAW_RING], 16 * (SUBS // RAW_RING * p + n // RAW_RING + 1))
                        if not (turn.fixed and SUBS * p + n < SPLIT_RING):
                            act.wait_ge(sub_used, SUBS * p + n - SPLIT_RING + 1)
                        nc.scalar.activation(w_hi[:, n % SPLIT_RING], w_raw[:, n % RAW_RING], ACT.Copy
                                             ).then_inc(hi_made, 1)
                    elif what == "evac":
                        t, = a
                        act.wait_ge(sub_used, SUBS * p + 2 * t + 2)
                        wait(act, kept.after(turn, t, back=2))
                        b = main[2 * (t % 2):2 * (t % 2) + 2]
                        x = xp[:, t % 2]
                        nc.scalar.activation(x[:, HIST:HIST + HALF], b[0][:, 0:HALF], ACT.Copy)
                        nc.scalar.activation(x[:, HIST + HALF:HIST + PROMPT], b[1][:, 0:PROMPT - HALF], ACT.Copy)
                        nc.scalar.activation(x[:, HIST + SAMP0:HIST + SAMP0 + SAMPLE], b[1][:, PROMPT - HALF:HALF], ACT.Copy)
                        tile = (p, PAIRS + p, 2 * PAIRS + 2 * p, 2 * PAIRS + 2 * p + 1)[t]
                        nc.scalar.activation(x[:, SAMP0:SAMP0 + HIST], hist[:, :, bass.ds(tile, 1)].rearrange("p w t -> p (w t)"),
                                             ACT.Copy).then_inc(xp_made.sem, 1)
                    elif what == "conv":
                        t, = a
                        wait(act, taps.after(turn, t))
                        wait(act, silu.after(turn, t, back=1))
                        nc.scalar.activation(th[:], y[:], ACT.Tanh).then_inc(tanh_y.sem, 1)
                    elif what == "square":
                        t, = a
                        wait(act, silu.after(turn, t))
                        wait(act, sumsq.after(turn, t, back=1))
                        nc.scalar.activation(sq[:], cqk[:, t], ACT.Square).then_inc(square.sem, 1)
                    elif what == "root":
                        t, = a
                        wait(act, sumsq.after(turn, t))
                        wait(act, inverted.after(turn, t, back=1))
                        for e in range(2):
                            m = nc.scalar.activation(root[:, e * NPAD // 2:(e + 1) * NPAD // 2], E[e][:, 0:NPAD // 2],
                                                     ACT.Sqrt, bias=eps[:, 0:1])
                        m.then_inc(rooted.sem, 1)
                    elif what == "zevac":
                        t, = a
                        act.wait_ge(sub_used, SUBS * p + 2 * t + 2)
                        wait(act, z_made.after(turn, t, back=1))
                        b = main[2 * (t % 2):2 * (t % 2) + 2]
                        for h in range(2):
                            m = nc.scalar.activation(zt[:, h * HALF:(h + 1) * HALF], b[h][:, 0:HALF], ACT.Tanh, scale=0.5)
                        m.then_inc(z_tanh.sem, 1)
                    elif what == "tab":
                        if again:
                            wait(act, o_gated.after(turn, 2, ago=1))
                            wait(act, s_out.after(turn, ago=1))
                        wait(act, z_made.after(turn, 5, ago=1))
                        nc.scalar.activation(zs[:], znew[:], ACT.Copy).then_inc(z_moved.sem, 1)
                        act.dma_start(S[:, 1], state_in[:, bass.ds(2 * (p - 1), 2), :]).then_inc(s_in.sem, 16)
                    elif what == "fetch":
                        if turn.behind:
                            wait(act, kkq_took.after(turn, 2))
                        for src, dst, sig in ((scratch["G"], dec, g_in), (scratch["beta"], bdec, b_in)):
                            for h in range(2):
                                act.dma_start(dst[64 * h:64 * h + 64, :], src[bass.ds(2 * p + h, 1), :].broadcast_to([64, NPAD])
                                              ).then_inc(sig.sem, 16)
                    elif what == "states":
                        wait(act, s_made.after(turn, SAMP))
                        for i in range(2):
                            act.dma_start(states_out[i][:, bass.ds(2 * (p - 1), 2), :], S[:, i]).then_inc(s_out.sem, 16)
                    elif what == "put":
                        wait(act, o_gated.after(turn, 2))
                        act.dma_start(o_all[:, bass.ds(2 * (p - 1), 2), :], ot[:]).then_inc(o_out.sem, 16)
                    elif what == "decay":
                        wait(act, g_sum.after(turn))
                        nc.scalar.activation(dec[:], dec[:], ACT.Exp).then_inc(dec_made.sem, 1)
                    elif what == "inv1":
                        b, l = a
                        wait(act, y_made.after(turn, b, l))
                        wait(act, ty_sum.after(turn, b, l, back=1))
                        for h in range(2):
                            r = slice(64 * h, 64 * h + 64)
                            m = nc.scalar.activation(Y[r, :, 64 * h:64 * h + 64], Yc[r], ACT.Copy)
                        m.then_inc(y_spread.sem, 1)
                    elif what == "inv2":
                        b, l = a
                        wait(act, t_made.after(turn, b, l))
                        if l == 0 and not (turn.fixed and p == 1):
                            wait(act, vn_sum.after(turn, SAMP, ago=1))
                        for h in range(2):
                            r = slice(64 * h, 64 * h + 64)
                            m = nc.scalar.activation(TT[r, 5 * b:5 * b + 5, 64 * h:64 * h + 64], TTc[r, 5 * b:5 * b + 5], ACT.Copy)
                        m.then_inc(tt_spread.sem, 1)
                    elif what == "seq2":
                        c, = a
                        wait(act, vn_sum.after(turn, c))
                        wait(act, os_sum.after(turn, c, back=1))
                        nc.scalar.activation(vn[:], F[1][:, 0:HD], ACT.Copy)
                        for h in range(2):
                            r = slice(64 * h, 64 * h + 64)
                            m = nc.scalar.activation(vnd[r, h], F[1][r, 0:HD], ACT.Copy)
                        m.then_inc(vn_made.sem, 1)
                    elif what == "osq":
                        wait(act, s_made.after(turn, SAMP))
                        nc.scalar.activation(o_squares, on[:].rearrange("p u v -> p (u v)"), ACT.Square
                                             ).then_inc(o_squared.sem, 1)
                        wait(act, o_summed.after(turn))
                        nc.scalar.activation(osum[:, 1], osum[:, 0], ACT.Sqrt, bias=eps[:, 0:1], scale=1.0 / HD
                                             ).then_inc(o_rooted.sem, 1)
            o_squares = kc[:].rearrange("p u v -> p (u v)")
            state_in = io["state_delta"].rearrange("l b h k v -> k (l b h) v")
            states_out = [io[name].rearrange("l b h k v -> k (l b h) v") for name in ("delta_p", "delta_s")]
            o_all = scratch["o"].rearrange("k p t -> p k t")
            turns(act, body)
            act.wait_ge(s_out.sem, 32 * PAIRS)
            act.wait_ge(o_out.sem, 16 * PAIRS)

        @block.vector
        def _(dve):
            dve.wait_ge(ready, 1)
            nc.vector.memset(eps[:], EPS)

            def table(i, u0, n, width):
                return ptab[:, 10 * i + u0:10 * i + u0 + n, None].broadcast_to([P, n, width])

            def body(turn):
                p = turn.p
                again = not (turn.fixed and p == 1)
                for step in turn.steps():
                    what, *a = step
                    if what == "split":
                        n, = a
                        dve.wait_ge(hi_made, SUBS * p + n + 1)
                        nc.vector.tensor_tensor(w_lo[:, n % SPLIT_RING], w_raw[:, n % RAW_RING],
                                                w_hi[:, n % SPLIT_RING].bitcast(F32), ALU.subtract).then_inc(lo_made, 1)
                    elif what == "conv":
                        t, = a
                        wait(dve, xp_made.after(turn, t))
                        tile = (p, PAIRS + p, 2 * PAIRS + 2 * p, 2 * PAIRS + 2 * p + 1)[t]
                        wait(dve, silu.after(turn, t, back=1))
                        x = xp[:, t % 2]
                        for w in range(CONV_W):
                            weight = cw[:, w, bass.ds(tile, 1)]
                            if w == 0:
                                m = nc.vector.tensor_scalar(y[:], x[:, 0:NPAD], weight, None, ALU.mult)
                            else:
                                wait(dve, taps.after(turn, t, n=w))
                                m = nc.vector.scalar_tensor_tensor(out=y[:], in0=x[:, w:w + NPAD], scalar=weight,
                                                                   in1=y[:], op0=ALU.mult, op1=ALU.add)
                            m.then_inc(taps.sem, 1)
                        for s, c0 in ((0, PROMPT), (1, SAMP0 + SAMPLE)):
                            m = nc.vector.tensor_copy(cout[:, s, :, bass.ds(tile, 1)], x[:, c0:c0 + HIST, None])
                        m.then_inc(kept.sem, 1)
                    elif what == "silu":
                        t, = a
                        wait(dve, tanh_y.after(turn, t))
                        if t < 2:
                            if turn.behind:
                                wait(dve, kq_made.after(turn))
                            wait(dve, square.after(turn, t, ago=1))
                            out, i0, i1 = cqk[:, t], th[:], y[:]
                        else:
                            if turn.behind:
                                wait(dve, vnat_t.after(turn, 2))
                            out = cv[:, :, t - 2, :]
                            i0, i1 = (v[:].rearrange("p (u c) -> p u c", c=C) for v in (th, y))
                        nc.vector.scalar_tensor_tensor(out=out, in0=i0, scalar=1.0, in1=i1,
                                                       op0=ALU.add, op1=ALU.mult).then_inc(silu.sem, 1)
                    elif what == "root":
                        t, = a
                        wait(dve, rooted.after(turn, t))
                        if turn.behind:
                            wait(dve, kq_made.after(turn))
                        nc.vector.reciprocal(rqk[:, t], root[:]).then_inc(inverted.sem, 1)
                    elif what == "zevac":
                        t, = a
                        wait(dve, z_tanh.after(turn, t))
                        if turn.behind:
                            wait(dve, z_moved.after(turn))
                        b = main[2 * (t % 2):2 * (t % 2) + 2]
                        for h in range(2):
                            s = slice(h * HALF, (h + 1) * HALF)
                            m = nc.vector.scalar_tensor_tensor(out=znew[:, t - 4, s], in0=zt[:, s], scalar=1.0,
                                                               in1=b[h][:, 0:HALF], op0=ALU.add, op1=ALU.mult)
                        m.then_inc(z_made.sem, 1)
                    elif what == "tab":
                        if again:
                            wait(dve, o_normed.after(turn, ago=1))
                            wait(dve, s_out.after(turn, ago=1))
                        nc.vector.memset(S[:, 0], 0.0).then_inc(s_zero.sem, 1)
                        nc.vector.tensor_copy(ptab[:, None, :], tabs[:, bass.ds(p - 1, 1), :]).then_inc(tables.sem, 1)
                        wait(dve, tables.after(turn))
                    elif what == "decay":
                        wait(dve, g_in.after(turn, ago=1))
                        i = const["incl"][:, None, :].broadcast_to([P, UNITS, C])
                        st = const["strict"][:, None, :].broadcast_to([P, UNITS, C])
                        g3, b3, d3 = (v[:].rearrange("p (u c) -> p u c", c=C) for v in (dec, bdec, dec))
                        nc.vector.tensor_tensor(g3, g3, table(0, 0, UNITS, C), ALU.subtract).then_inc(g_sum.sem, 1)
                        wait(dve, g_sum.after(turn, n=1))
                        nc.vector.tensor_tensor(g3, g3, i, ALU.add).then_inc(g_sum.sem, 1)
                        wait(dve, b_in.after(turn, ago=1))
                        nc.vector.tensor_tensor(b3, b3, st, ALU.mult).then_inc(bdec_made.sem, 1)
                        wait(dve, bdec_made.after(turn, n=1))
                        wait(dve, dec_made.after(turn))
                        nc.vector.tensor_tensor(b3, b3, d3, ALU.mult).then_inc(bdec_made.sem, 1)
                    elif what == "kqn":
                        if again:
                            wait(dve, ks_sum.after(turn, SAMP, ago=1))
                        wait(dve, inverted.after(turn, 1, ago=1))
                        c3 = [cqk[:, t].rearrange("p (u c) -> p u c", c=C) for t in range(2)]
                        r3 = [rqk[:, t].rearrange("p (u c) -> p u c", c=C) for t in range(2)]
                        two = [v[:, :, None, :].broadcast_to([P, UNITS, 2, C]) for v in (c3[1], r3[1])]
                        nc.vector.tensor_tensor(kqk[:, :, 0:2, :], *two, ALU.mult).then_inc(kq_made.sem, 1)
                        nc.vector.tensor_tensor(kqk[:, :, 3, :], c3[1], r3[1], ALU.mult).then_inc(kq_made.sem, 1)
                        nc.vector.scalar_tensor_tensor(out=kqk[:, :, 2, :], in0=c3[0], scalar=HD ** -0.5, in1=r3[0],
                                                       op0=ALU.mult, op1=ALU.mult).then_inc(kq_made.sem, 1)
                    elif what == "kkq":
                        g, = a
                        us = group(g)
                        n = len(us)
                        wait(dve, kkq_sum.after(turn, g))
                        wait(dve, bdec_made.after(turn))
                        if g == 0 and again:
                            wait(dve, os_sum.after(turn, SAMP, ago=1))
                        e3 = E[g % 2].rearrange("p (u x) -> p u x", x=P)
                        for h in range(2):
                            r = slice(64 * h, 64 * h + 64)
                            d3, b3 = (v[r, C * us[0]:C * us[0] + C * n].rearrange("p (u c) -> p u c", c=C) for v in (dec, bdec))
                            nc.vector.tensor_tensor(MT[r, us[0]:us[0] + n, 64 * h:64 * h + 64], e3[r, 0:n, 0:C], b3, ALU.mult)
                            m = nc.vector.tensor_tensor(QK[r, us[0]:us[0] + n, 64 - 64 * h:128 - 64 * h], e3[r, 0:n, C:2 * C],
                                                        d3, ALU.mult)
                        m.then_inc(kkq_took.sem, 1)
                    elif what in ("knat", "vnat"):
                        g, = a
                        us = group(g)
                        n = len(us)
                        turned, made, dst, column, e = ((knat_t, kc_made, kc, 2, 1 - g % 2) if what == "knat" else
                                                        (vnat_t, bv_made, bv, 3, g % 2))
                        wait(dve, turned.after(turn, g))
                        nc.vector.tensor_tensor(dst[:, us[0]:us[0] + n], E[e].rearrange("p (u x) -> p u x", x=P)[:, 0:n],
                                                table(column, us[0], n, P), ALU.mult).then_inc(made.sem, 1)
                    elif what == "inv1":
                        b, l = a
                        wait(dve, mt_sum.after(turn, b, l))
                        wait(dve, y_spread.after(turn, b, l, back=1))
                        wait(dve, ty_sum.after(turn, b, l, back=1))
                        mask = const["level"][:, None, C * l:C * l + C].broadcast_to([P, 5, C])
                        nc.vector.tensor_tensor(Yc[:], E[0][:, 0:5 * C].rearrange("p (u c) -> p u c", c=C), mask, ALU.mult
                                                ).then_inc(y_made.sem, 1)
                    elif what == "inv2":
                        b, l = a
                        wait(dve, ty_sum.after(turn, b, l))
                        e = [E[i][:, 0:5 * C].rearrange("p (u c) -> p u c", c=C) for i in range(2)]
                        eye = eye64[:, None, :].broadcast_to([P, 5, C])
                        us = slice(5 * b, 5 * b + 5)
                        if l < LEVELS - 1:
                            wait(dve, y_made.after(turn, b, l))
                            if l:
                                wait(dve, t_made.after(turn, b, l - 1))
                            m = nc.vector.tensor_tensor(Tc[:, us], Tc[:, us] if l else eye, e[0] if l else Yc[:], ALU.subtract)
                            m.then_inc(t_made.sem, 1)
                        if l:
                            wait(dve, tt_spread.after(turn, b, l - 1))
                        elif again:
                            wait(dve, tt_spread.after(turn, b, LEVELS - 1, ago=1))
                        nc.vector.tensor_tensor(TTc[:, us], TTc[:, us] if l else eye, e[1], ALU.subtract
                                                ).then_inc(t_made.sem, 1 if l < LEVELS - 1 else 2)
                    elif what == "seq1":
                        c, = a
                        wait(dve, ks_sum.after(turn, c))
                        if c == 0:
                            wait(dve, bv_made.after(turn, 2))
                        wait(dve, vn_sum.after(turn, c, back=1))
                        for h in range(2):
                            r = slice(64 * h, 64 * h + 64)
                            m = nc.vector.scalar_tensor_tensor(out=Rr[r], in0=F[0][r, HD * h:HD * h + HD],
                                                               scalar=ptab[r, 10 + c:11 + c], in1=bv[r, c],
                                                               op0=ALU.mult, op1=ALU.add)
                        m.then_inc(r_made.sem, 1)
                        if c:
                            wait(dve, s_made.after(turn, c - 1))
                        for h in range(2):
                            r = slice(64 * h, 64 * h + 64)
                            m = nc.vector.tensor_scalar(oq[r], F[0][r, HD * (1 - h):HD * (2 - h)],
                                                        ptab[r, 40 + c:41 + c], None, ALU.mult)
                        m.then_inc(oq_made.sem, 1)
                    elif what == "seq3":
                        c, = a
                        wait(dve, os_sum.after(turn, c))
                        wait(dve, oq_made.after(turn, c))
                        if c == 0 and again:
                            wait(dve, o_turned.after(turn, 2, ago=1))
                        i = 1 if c == SAMP else 0
                        for h in range(2):
                            m = nc.vector.scalar_tensor_tensor(out=S[:, i, h], in0=S[:, i, h],
                                                               scalar=ptab[:, 50 + 10 * h + c:51 + 10 * h + c],
                                                               in1=F[0][:, HD * (1 + h):HD * (2 + h)],
                                                               op0=ALU.mult, op1=ALU.add)
                        nc.vector.tensor_tensor(on[:, c], oq[:], F[0][:, 0:HD], ALU.add).then_inc(s_made.sem, 1)
                    elif what == "osq":
                        wait(dve, o_squared.after(turn))
                        nc.vector.tensor_reduce(osum[:, 0], kc[:], AX.X, ALU.add).then_inc(o_summed.sem, 1)
                        wait(dve, o_rooted.after(turn))
                        nc.vector.reciprocal(osum[:, 2], osum[:, 1]).then_inc(o_normed.sem, 1)
                        wait(dve, o_normed.after(turn, n=1))
                        nc.vector.tensor_tensor(on[:], on[:], osum[:, 2, :, None].broadcast_to([P, UNITS, HD]), ALU.mult
                                                ).then_inc(o_normed.sem, 1)
                    elif what == "otr":
                        g, = a
                        us = group(g)
                        wait(dve, o_turned.after(turn, g))
                        if g == 0 and again:
                            wait(dve, o_out.after(turn, ago=1))
                        e3 = E[g % 2].rearrange("p (u x) -> p u x", x=P)
                        if g == 0:
                            wait(dve, z_moved.after(turn))
                        for h in range(2):
                            x0 = 64 - 64 * h
                            if g < 2:
                                parts = [(slice(4 * C * g, 4 * C * g + 4 * C), slice(0, 4), C)]
                            else:
                                parts = [(slice(TAIL * C, PROMPT), slice(0, 1), TAIL_N), (slice(PROMPT, NTOK), slice(1, 2), SAMPLE)]
                            for cols, u, n in parts:
                                m = nc.vector.scalar_tensor_tensor(
                                    out=ot[:, h, cols].rearrange("p (u c) -> p u c", c=n), in0=e3[:, u, x0:x0 + n],
                                    scalar=vec[:, 48:49], in1=zs[:, h, cols].rearrange("p (u c) -> p u c", c=n),
                                    op0=ALU.mult, op1=ALU.mult)
                        m.then_inc(o_gated.sem, 1)
            turns(dve, body)


def project_back(nc, top, io, keep, tag, kt, o_dram, w, residual, out=None):
    per = kt // KSUB
    raw_ring, split_ring, o_ring = 4, 2, 4
    with ExitStack() as ctx:
        def sb(name, shape, dt=F32):
            return ctx.enter_context(nc.sbuf_tensor(tag + name, shape, dt))

        def sem(name):
            return top.semaphore(tag + name)

        main = [ctx.enter_context(nc.psum_tensor(f"{tag}main{i}", [P, 512], F32)) for i in range(4)]
        E = [ctx.enter_context(nc.psum_tensor(f"{tag}E{i}", [P, 512], F32)) for i in range(2)]
        ident, ones = keep["const"]["ident"], keep["const"]["ones"]
        oh, ol = sb("oh", [P, kt, NTOK], F32R), sb("ol", [P, kt, NTOK], F32R)
        o_raw = sb("o_raw", [P, o_ring, NTOK])
        w_raw = sb("w_raw", [P, raw_ring, KSUB, P])
        w_hi = sb("w_hi", [P, split_ring, KSUB, P], F32R)
        w_lo = sb("w_lo", [P, split_ring, KSUB, P], F32R)
        res = sb("res", [P, 2, NTOK])
        h = sb("h", [P, 2, NTOK])
        sq = sb("sq", [P, NTOK])
        rows = sb("rows", [P, 4, P])
        rows_s = sb("rows_s", [SAMPLE, P])
        eps = sb("eps", [P, 1])

        w_in = [sem(f"w_in{i}") for i in range(raw_ring)]
        o_in = [sem(f"o_in{i}") for i in range(o_ring)]
        res_in = [sem(f"res_in{i}") for i in range(2)]
        h_out = [sem(f"h_out{i}") for i in range(2)]
        o_hi, o_lo, hi_made, lo_made, sub_used = (sem(x) for x in ("o_hi", "o_lo", "hi_made", "lo_made", "sub_used"))
        h_made, squared, summed, turned, copied = (sem(x) for x in ("h_made", "squared", "summed", "turned", "copied"))
        rooted, start, rows_out = sem("rooted"), sem("start"), sem("rows_out")
        block = ctx.enter_context(nc.Block())

        def tiles(engine, body):
            for m in (0, 1):
                body(m)
            with engine.Fori(2, KT - 2, 2) as i:
                body(i)
                body(i + 1, 1)
            for m in (KT - 2, KT - 1):
                body(m)

        def odd(m, second):
            return m % 2 if isinstance(m, int) else second

        def parts(m, second):
            known = isinstance(m, int)
            for j in range(2, per + 2):
                if not (known and per * m + j >= per * KT):
                    yield per * m + j, (per * odd(m, second) + j)

        @block.sync
        def _(sp):
            def part(g, at, column):
                if not (isinstance(g, int) and g < raw_ring):
                    sp.wait_ge(lo_made, g - raw_ring + 1)
                k0 = KSUB * (at % per)
                sp.dma_start(w_raw[:, at % raw_ring], w[:, k0:k0 + KSUB, bass.ds(column, P)]).then_inc(w_in[at % raw_ring], 16)

            def body(m, second=0):
                known, o = isinstance(m, int), odd(m, second)
                for j in range(per):
                    part(per * m + j, per * o + j, P * m)
                    if known and m == 0:
                        for k in range(KSUB * j, KSUB * (j + 1)):
                            if k >= o_ring:
                                sp.wait_ge(o_lo, k - o_ring + 1)
                            sp.dma_start(o_raw[:, k % o_ring], o_dram[k]).then_inc(o_in[k % o_ring], 16)
                if not (known and m < 2):
                    sp.wait_ge(h_made, m - 1)
                sp.dma_start(res[:, o], residual[bass.ds(m, 1)].rearrange("k p t -> p (k t)")).then_inc(res_in[o], 16)
            tiles(sp, body)

        @block.tensor
        def _(pe):
            pe.wait_ge(start, 1)

            def finish(m, second):
                o = odd(m, second)
                if out is None:
                    pe.wait_ge(squared, m + 1)
                    for e in range(2):
                        mm = nc.tensor.matmul(E[e][:, 0:HALF], ones[:, :], sq[:, e * HALF:(e + 1) * HALF],
                                              start=isinstance(m, int) and m == 0, stop=isinstance(m, int) and m == KT - 1,
                                              skip_group_check=True)
                    mm.then_inc(summed, 1)
                else:
                    pe.wait_ge(h_made, m + 1)
                    if not (isinstance(m, int) and m == 0):
                        pe.wait_ge(copied, m)
                    for c in range(4):
                        nc.tensor.transpose(E[0][:, P * c:P * c + P], h[:, o, N_META + P * c:N_META + P * c + P], ident[:, :])
                    nc.tensor.transpose(E[1][0:SAMPLE, 0:P], h[:, o, PROMPT:NTOK], ident[:, :]).then_inc(turned, 1)

            def body(m, second=0):
                known, o = isinstance(m, int), odd(m, second)
                for j in range(per):
                    pe.wait_ge(lo_made, per * m + j + 1)
                    if j == 0 and not (known and m < 2):
                        pe.wait_ge(h_made, m - 1)
                    for k in range(KSUB):
                        kk = KSUB * j + k
                        if known and m == 0:
                            pe.wait_ge(o_lo, kk + 1)
                        for wt, x in ((w_hi, oh), (w_hi, ol), (w_lo, oh)):
                            for e in range(2):
                                mm = nc.tensor.matmul(main[2 * o + e][:, 0:HALF], wt[:, (per * o + j) % split_ring, k, :],
                                                      x[:, kk, e * HALF:(e + 1) * HALF],
                                                      start=(kk == 0 and wt is w_hi and x is oh),
                                                      stop=(kk == kt - 1 and wt is w_lo))
                    mm.then_inc(sub_used, 1)
                    if j == 0 and not (known and m == 0):
                        finish(m - 1, 1 - o)
            tiles(pe, body)
            finish(KT - 1, 1)

        @block.scalar
        def _(act):
            def split(g, at):
                act.wait_ge(w_in[at % raw_ring], (g - at % raw_ring + raw_ring) * (16 // raw_ring))
                if not (isinstance(g, int) and g < split_ring):
                    act.wait_ge(sub_used, g - split_ring + 1)
                nc.scalar.activation(w_hi[:, at % split_ring], w_raw[:, at % raw_ring], ACT.Copy).then_inc(hi_made, 1)

            def body(m, second=0):
                known, o = isinstance(m, int), odd(m, second)
                if known and m == 0:
                    for g in range(per):
                        if g < 2:
                            split(g, g)
                        for k in range(KSUB * g, KSUB * (g + 1)):
                            act.wait_ge(o_in[k % o_ring], 16 * (k // o_ring + 1))
                            nc.scalar.activation(oh[:, k], o_raw[:, k % o_ring], ACT.Copy).then_inc(o_hi, 1)
                        if g >= 2:
                            split(g, g)
                    if per == 2:
                        split(2, 2)
                        split(3, 3)
                    else:
                        split(4, 4)
                        split(5, 5)
                else:
                    for g, at in parts(m, second):
                        split(g, at)
                act.wait_ge(h_made, m + 1)
                if out is None:
                    if not (known and m == 0):
                        act.wait_ge(summed, m)
                    nc.scalar.activation(sq[:], h[:, o], ACT.Square).then_inc(squared, 1)
                    act.dma_start(io["h1"][bass.ds(m, 1)].rearrange("k p t -> p (k t)"), h[:, o]).then_inc(h_out[o], 16)
                else:
                    act.wait_ge(turned, m + 1)
                    if not (known and m == 0):
                        act.wait_ge(rows_out, 32 * m)
                    nc.scalar.activation(rows[:].rearrange("p c d -> p (c d)"), E[0][:, 0:4 * P], ACT.Copy)
                    nc.scalar.activation(rows_s[:], E[1][0:SAMPLE, 0:P], ACT.Copy).then_inc(copied, 1)
                    act.wait_ge(copied, m + 1)
                    act.dma_start(out[0].rearrange("b (c p) d -> p (b c) d", p=P)[:, :, bass.ds(P * m, P)], rows[:]
                                  ).then_inc(rows_out, 16)
                    act.dma_start(out[1].rearrange("b p d -> p (b d)")[:, bass.ds(P * m, P)], rows_s[:]).then_inc(rows_out, 16)
            tiles(act, body)
            if out is None:
                act.wait_ge(summed, KT)
                for e in range(2):
                    a = nc.scalar.activation(sq[:, e * HALF:(e + 1) * HALF], E[e][:, 0:HALF], ACT.Sqrt,
                                             bias=eps[:, 0:1], scale=1.0 / D)
                a.then_inc(rooted, 1)
                for o in range(2):
                    act.wait_ge(h_out[o], 16 * KT // 2)
            else:
                act.wait_ge(rows_out, 32 * KT)

        @block.vector
        def _(dve):
            nc.vector.memset(eps[:], EPS).then_inc(start, 1)

            def split(g, at):
                dve.wait_ge(hi_made, g + 1)
                nc.vector.tensor_tensor(w_lo[:, at % split_ring], w_raw[:, at % raw_ring],
                                        w_hi[:, at % split_ring].bitcast(F32), ALU.subtract).then_inc(lo_made, 1)

            def body(m, second=0):
                known, o = isinstance(m, int), odd(m, second)
                if known and m == 0:
                    for g in range(per):
                        if g < 2:
                            split(g, g)
                        for k in range(KSUB * g, KSUB * (g + 1)):
                            dve.wait_ge(o_hi, k + 1)
                            nc.vector.tensor_tensor(ol[:, k], o_raw[:, k % o_ring], oh[:, k].bitcast(F32), ALU.subtract
                                                    ).then_inc(o_lo, 1)
                        if g >= 2:
                            split(g, g)
                    for g in range(per, per + 2):
                        split(g, g)
                else:
                    for g, at in parts(m, second):
                        split(g, at)
                dve.wait_ge(sub_used, per * m + per)
                if known and m < 2:
                    dve.wait_ge(res_in[o], 16)
                else:
                    dve.wait_ge(res_in[o], (m - o + 2) * 8)
                    if out is None:
                        dve.wait_ge(h_out[o], (m - o) * 8)
                        dve.wait_ge(squared, m - 1)
                    else:
                        dve.wait_ge(turned, m - 1)
                for e in range(2):
                    s = slice(e * HALF, (e + 1) * HALF)
                    v = nc.vector.tensor_tensor(h[:, o, s], res[:, o, s], main[2 * o + e][:, 0:HALF], ALU.add)
                v.then_inc(h_made, 1)
            tiles(dve, body)
            if out is None:
                dve.wait_ge(rooted, 1)
                nc.vector.reciprocal(keep["r"][:], sq[:])


SUBS_B = 8
BLOCKS = 6
QN = [P, P, P, P, PROMPT - 4 * P, SAMPLE]
Q0 = [0, P, 2 * P, 3 * P, 4 * P, PROMPT]
KN = [P, 2 * P, 3 * P, 4 * P, PROMPT, PAST + SAMPLE]


def key_blocks(i):
    n = -(-KN[i] // P)
    return n, KN[i] - P * (n - 1)


def head_order():
    at = {k: [] for k in range(SUBS_B * KSUB + 1)}
    for n in range(SUBS_B + 2):
        at[max(0, KSUB * (n - 1) - 4)].append(("scale", n))
        at[max(0, KSUB * (n - 1))].append(("split", n))
    for t in range(4):
        end = (2 * t + 2) * KSUB
        at[end].append(("evac", t))
        if t in (0, 2):
            at[end + 3] += [("sumsq", t), ("root", t)]
    at[0] += [("tab",)]
    at[2].append(("kout",))
    at[3].append(("vout",))
    at[5].append(("kcache",))
    for i in range(BLOCKS):
        at[7 + 8 * i].append(("score", i))
        at[7 + 8 * i + 6].append(("prob", i))
        at[min(7 + 8 * i + 9, 64)].append(("turn", i))
        at[min(7 + 8 * i + 12, 64)].append(("value", i))
    at[64].append(("put",))
    at[30].append(("fetchk",))
    at[64].append(("fetch",))
    steps = []
    for k in range(SUBS_B * KSUB + 1):
        steps += at[k]
        if k < SUBS_B * KSUB:
            steps.append(("kstep", k // KSUB, k % KSUB))
    return Order(steps, {"scale", "split", "kstep", "evac", "sumsq", "root", "fetch", "fetchk"}, SUBS_B)


def forget_gates(nc, top, io, keep, scratch):
    with ExitStack() as ctx:
        def sb(name, shape, dt=F32):
            return ctx.enter_context(nc.sbuf_tensor("g_" + name, shape, dt))

        def sem(name):
            return top.semaphore("g_" + name)

        bank = [ctx.enter_context(nc.psum_tensor(f"g_bank{i}", [P, 512], F32)) for i in range(8)]
        ident, ones, vec = keep["const"]["ident"], keep["const"]["ones"], keep["vec"]
        xh, xl, r = keep["xh_b"], keep["xl_b"], keep["r"]
        hin = sb("hin", [P, 4, NTOK])
        xn = sb("xn", [P, 2, NTOK])
        wf = sb("wf", [P, KT, FH])
        fb = sb("fb", [FH, 1])
        cl_rows = sb("cl_rows", [P, PAST // P, FH])
        lf = sb("lf", [FH, 4, NTOK])
        cl = sb("cl", [FH, PAST + SAMPLE])
        fp, fs = sb("fp", [FH, PROMPT]), sb("fs", [FH, PAST + SAMPLE])
        lf_rows = sb("lf_rows", [P, BLOCKS, FH])
        fcol = keep["fcol"]
        cs = keep["const"]
        h_in = [sem(f"h_in{i}") for i in range(4)]
        small, normed, high, low, used, wf_made = (sem(x) for x in ("small", "normed", "high", "low", "used", "wf_made"))
        step_a, step_v, step_p, stored, cleared = (sem(x) for x in ("step_a", "step_v", "step_p", "stored", "cleared"))
        block = ctx.enter_context(nc.Block())

        @block.sync
        def _(sp):
            sp.dma_start(wf[:], io["kv_w"].rearrange("(k p) n -> p k n", p=P)[:, :, 2 * D:2 * D + FH]).then_inc(small, 16)
            sp.dma_start(fb[:], io["kv_f_bias"].rearrange("(h o) -> h o", o=1)).then_inc(small, 16)
            sp.dma_start(cl_rows[:], io["cache_logf"].rearrange("b (c p) h -> p (b c) h", p=P)).then_inc(small, 16)
            for k in range(KT):
                if k >= 4:
                    sp.wait_ge(normed, k - 3)
                sp.dma_start(hin[:, k % 4], io["h1"][k]).then_inc(h_in[k % 4], 16)
            sp.wait_ge(step_v, 5)
            sp.dma_start(scratch["FP"], fp[:]).then_inc(stored, 16)
            sp.dma_start(scratch["FS"], fs[:]).then_inc(stored, 16)
            sp.wait_ge(step_v, 6)
            sp.dma_start(io["logf_p"][:, 0:4 * P].rearrange("b (c p) h -> p (b c) h", p=P), lf_rows[:, 0:4]).then_inc(stored, 16)
            sp.dma_start(io["logf_p"].rearrange("b t h -> (b t) h")[4 * P:PROMPT], lf_rows[0:QN[4], 4]).then_inc(stored, 16)
            sp.dma_start(io["logf_s"].rearrange("b t h -> (b t) h"), lf_rows[0:SAMPLE, 5]).then_inc(stored, 16)
            sp.wait_ge(stored, 80)

        @block.tensor
        def _(pe):
            pe.wait_ge(small, 48)
            for c in range(PAST // P):
                m = nc.tensor.transpose(bank[2 + c // 4][0:FH, P * (c % 4):P * (c % 4) + P], cl_rows[:, c, :], ident[:, :])
            m.then_inc(step_p, 1)
            pe.wait_ge(wf_made, 1)
            for k in range(KT):
                pe.wait_ge(normed, k + 1)
                for e in range(2):
                    m = nc.tensor.matmul(bank[e][0:FH, 0:HALF], wf[:, k, :], xn[:, k % 2, e * HALF:(e + 1) * HALF],
                                         start=(k == 0), stop=(k == KT - 1))
                m.then_inc(used, 1)
            pe.wait_ge(step_v, 5)
            for i in range(BLOCKS):
                m = nc.tensor.transpose(bank[4][0:QN[i], FH * i:FH * i + FH], lf[:, 3, Q0[i]:Q0[i] + QN[i]], ident[0:FH, 0:FH])
                src = fp[:, Q0[i]:Q0[i] + QN[i]] if i < 5 else fs[:, PAST:PAST + SAMPLE]
                m = nc.tensor.transpose(bank[5][0:QN[i], FH * i:FH * i + FH], src, ident[0:FH, 0:FH])
            m.then_inc(step_p, 1)

        @block.scalar
        def _(act):
            for k in range(KT):
                act.wait_ge(normed, k + 1)
                nc.scalar.activation(xh[:, k], xn[:, k % 2], ACT.Copy).then_inc(high, 1)
            act.wait_ge(used, KT)
            for e in range(2):
                s = slice(e * HALF, (e + 1) * HALF)
                nc.scalar.activation(lf[:, 0, s], bank[e][0:FH, 0:HALF], ACT.Identity, bias=fb[:, 0:1])
                a = nc.scalar.activation(lf[:, 1, s], bank[e][0:FH, 0:HALF], ACT.Abs, bias=fb[:, 0:1])
            a.then_inc(step_a, 1)
            act.wait_ge(step_a, 1)
            nc.scalar.activation(lf[:, 2], lf[:, 1], ACT.Exp, scale=-1.0).then_inc(step_a, 1)
            act.wait_ge(step_a, 2)
            nc.scalar.activation(lf[:, 1], lf[:, 2], ACT.Ln, bias=1.0).then_inc(step_a, 1)

        @block.vector
        def _(dve):
            nc.vector.memset(fcol[:], 0.0).then_inc(cleared, 1)
            dve.wait_ge(small, 48)
            nc.vector.tensor_tensor(wf[:], wf[:], vec[:, 16:32, None].broadcast_to([P, KT, FH]), ALU.mult).then_inc(wf_made, 1)
            for k in range(KT):
                if k >= 2:
                    dve.wait_ge(used, k - 1)
                    dve.wait_ge(low, k - 1)
                dve.wait_ge(h_in[k % 4], 16 * (k // 4 + 1))
                nc.vector.tensor_tensor(xn[:, k % 2], hin[:, k % 4], r[:], ALU.mult).then_inc(normed, 1)
                dve.wait_ge(high, k + 1)
                nc.vector.tensor_tensor(xl[:, k], xn[:, k % 2], xh[:, k].bitcast(F32), ALU.subtract).then_inc(low, 1)
            dve.wait_ge(step_p, 1)
            for b in range(2):
                v = nc.vector.tensor_copy(cl[:, 512 * b:512 * b + 512], bank[2 + b][0:FH, :])
            v.then_inc(step_v, 1)
            dve.wait_ge(step_a, 3)
            nc.vector.scalar_tensor_tensor(out=lf[:, 3], in0=lf[:, 0], scalar=0.0, in1=lf[:, 1], op0=ALU.min,
                                           op1=ALU.subtract).then_inc(step_v, 1)
            dve.wait_ge(step_v, 2)
            nc.vector.tensor_copy(cl[:, PAST:], lf[:, 3, PROMPT:NTOK]).then_inc(step_v, 1)
            nc.vector.tensor_tensor_scan(fp[:], ones[0:FH, 0:1].broadcast_to([FH, PROMPT]), lf[:, 3, 0:PROMPT], 0.0,
                                         ALU.mult, ALU.add).then_inc(step_v, 1)
            dve.wait_ge(step_v, 3)
            nc.vector.tensor_tensor_scan(fs[:], ones[0:FH, 0:1].broadcast_to([FH, PAST + SAMPLE]), cl[:], 0.0,
                                         ALU.mult, ALU.add).then_inc(step_v, 1)
            dve.wait_ge(step_p, 2)
            dve.wait_ge(cleared, 1)
            for i in range(BLOCKS):
                nc.vector.tensor_copy(fcol[0:QN[i], :, i], bank[5][0:QN[i], FH * i:FH * i + FH])
                v = nc.vector.tensor_copy(lf_rows[0:QN[i], i], bank[4][0:QN[i], FH * i:FH * i + FH])
            v.then_inc(step_v, 1)
            nc.vector.tensor_scalar(vec[:, 50:51], vec[:, 50:51], HD ** -0.5, None, ALU.mult)


def attention_layer(nc, top, io, keep, scratch):
    order = head_order()
    raw_ring, split_ring = 4, 2
    with ExitStack() as ctx:
        def sb(name, shape, dt=F32):
            return ctx.enter_context(nc.sbuf_tensor("b_" + name, shape, dt))

        def sem(name):
            return top.semaphore("b_" + name)

        def signal(name, kind, per=1):
            return Signal(sem(name), kind, per)

        main = [ctx.enter_context(nc.psum_tensor(f"b_main{i}", [P, 512], F32)) for i in range(4)]
        E = [ctx.enter_context(nc.psum_tensor(f"b_E{i}", [P, 512], F32)) for i in range(2)]
        F = [ctx.enter_context(nc.psum_tensor(f"b_F{i}", [P, 512], F32)) for i in range(2)]
        const, vec, xh, xl = keep["const"], keep["vec"], keep["xh_b"], keep["xl_b"]
        ident, ones, causal = const["ident"], const["ones"], const["causal"]
        w_raw = sb("w_raw", [P, raw_ring, KSUB, P])
        w_hi = sb("w_hi", [P, split_ring, KSUB, P], F32R)
        w_lo = sb("w_lo", [P, split_ring, KSUB, P], F32R)
        raw = sb("raw", [P, 3, NTOK])
        sq, root, rr = sb("sq", [P, NTOK]), sb("root", [P, NTOK]), sb("rr", [P, 2, NTOK])
        kT, qT = sb("kT", [P, NTOK]), sb("qT", [P, NTOK])
        zt, znew, zs = sb("zt", [P, NTOK]), sb("znew", [P, NTOK]), sb("zs", [P, NTOK])
        kn, vn = sb("kn", [P, 4, P]), sb("vn", [P, 4, P])
        kn2, vn2 = sb("kn2", [SAMPLE, 2, P]), sb("vn2", [SAMPLE, 2, P])
        kc, vc = sb("kc", [P, PAST // P, P]), sb("vc", [P, PAST // P, P])
        kcT = sb("kcT", [P, PAST])
        fbp, fbs = sb("fbp", [P, PROMPT]), sb("fbs", [SAMPLE, PAST + SAMPLE])
        fq = sb("fq", [P, BLOCKS])
        pr = sb("pr", [P, 2, PAST + SAMPLE])
        stat = sb("stat", [P, 2, 4])
        pt = sb("pt", [P, 2, 512])
        fo = sb("fo", [P, NTOK])
        eps = sb("eps", [P, 1])

        w_in = [sem(f"w_in{i}") for i in range(raw_ring)]
        scaled, hi_made, lo_made, sub_used, start = (sem(x) for x in ("scaled", "hi_made", "lo_made", "sub_used", "start"))
        kept = signal("kept", "evac")
        gate = signal("gate", "evac")
        sumsq = signal("sumsq", "sumsq")
        rooted, inverted = signal("rooted", "root"), signal("inverted", "root")
        moved = signal("moved", "tab")
        kq_made = signal("kq_made", "tab", 3)
        k_turned, k_took, k_out = signal("k_turned", "kout"), signal("k_took", "kout"), signal("k_out", "kout", 48)
        v_turned, v_took, v_out = signal("v_turned", "vout"), signal("v_took", "vout"), signal("v_out", "vout", 48)
        kc_in, vc_in = signal("kc_in", "fetchk", 16), signal("vc_in", "fetch", 16)
        fb_in = signal("fb_in", "fetch", 32)
        kc_turned, kc_took = signal("kc_turned", "kcache"), signal("kc_took", "kcache")
        scored, biased, masked, maxed, expd = (signal("scored", "score"), signal("biased", "score"), signal("masked", "score"),
                                               signal("maxed", "score", 2), signal("expd", "score"))
        inv_sum, prob = signal("inv_sum", "prob"), signal("prob", "prob")
        p_turned, pt_made = signal("p_turned", "turn"), signal("pt_made", "turn")
        summed, gated = signal("summed", "value"), signal("gated", "value")
        fo_out = signal("fo_out", "put", 16)

        bank_e = [
            Bank({"kout": (lambda: True, k_took), "kcache": (lambda: True, kc_took), "sumsq": (lambda t: True, rooted),
                  "turn": (lambda i: True, pt_made)}),
            Bank({"kout": (lambda: True, k_took), "kcache": (lambda: True, kc_took), "sumsq": (lambda t: True, rooted),
                  "value": (lambda i: True, gated), "score": (lambda i: i == 5, biased)}),
        ]
        bank_f = [
            Bank({"vout": (lambda: True, v_took), "score": (lambda i: i % 2 == 0 or i >= 4, biased)}),
            Bank({"vout": (lambda: True, v_took), "score": (lambda i: i % 2 == 1 or i >= 4, biased)}),
        ]

        def score_banks(i):
            if i < 4:
                return [(bank_f[i % 2], F[i % 2], 0, KN[i])]
            if i == 4:
                return [(bank_f[0], F[0], 0, 512), (bank_f[1], F[1], 512, KN[4] - 512)]
            return [(bank_f[0], F[0], 0, 512), (bank_f[1], F[1], 512, 512), (bank_e[1], E[1], PAST, SAMPLE)]

        def turns(engine, body):
            body(Turn(order, 0, behind=False))
            body(Turn(order, 1))
            with engine.Fori(2, FH - 1) as p:
                body(Turn(order, p))
            body(Turn(order, FH - 1, split=False))
            body(Turn(order, FH, front=False))

        block = ctx.enter_context(nc.Block())

        @block.sync
        def _(sp):
            kv = io["kv_w"].rearrange("(k p) n -> p k n", p=P)
            wb = io["b_w_in"].rearrange("l (k p) n -> p (l k) n", p=P)

            def body(turn):
                if not turn.front:
                    return
                p = turn.p
                sources = [(kv, P * p), (kv, D + P * p), (wb, P * p), (wb, D + P * p)]
                for n in range(SUBS_B):
                    if not (turn.fixed and SUBS_B * p + n < raw_ring):
                        sp.wait_ge(lo_made, SUBS_B * p + n - raw_ring + 1)
                    w, column = sources[n // 2]
                    k0 = KSUB * (n % 2)
                    sp.dma_start(w_raw[:, n % raw_ring], w[:, k0:k0 + KSUB, bass.ds(column, P)]
                                 ).then_inc(w_in[n % raw_ring], 16)
            turns(sp, body)

        @block.tensor
        def _(pe):
            pe.wait_ge(start, 1)

            def body(turn):
                p = turn.p
                for step in turn.steps():
                    what, *a = step
                    if what == "kstep":
                        n, k = a
                        t = n // 2
                        if k == 0:
                            pe.wait_ge(lo_made, SUBS_B * p + n + 1)
                            if n % 2 == 0:
                                wait(pe, gate.after(turn, t, back=2))
                        for hi, x in ((w_hi, xh), (w_hi, xl), (w_lo, xh)):
                            for e in range(2):
                                m = nc.tensor.matmul(main[2 * (t % 2) + e][:, 0:HALF], hi[:, n % split_ring, k, :],
                                                     x[:, KSUB * (n % 2) + k, e * HALF:(e + 1) * HALF],
                                                     start=(n % 2 == 0 and k == 0 and hi is w_hi and x is xh),
                                                     stop=(n % 2 == 1 and k == KSUB - 1 and hi is w_lo))
                        if k == KSUB - 1:
                            m.then_inc(sub_used, 1)
                    elif what == "sumsq":
                        t, = a
                        wait(pe, kept.after(turn, t))
                        for e in range(2):
                            wait(pe, bank_e[e].free(turn, step))
                            m = nc.tensor.matmul(E[e][:, 0:HALF], ones[:, :], sq[:, e * HALF:(e + 1) * HALF], start=True, stop=True)
                        m.then_inc(sumsq.sem, 1)
                    elif what in ("kout", "vout"):
                        src, b, guards, sig = ((kT[:], E, bank_e, k_turned) if what == "kout" else (raw[:, 1], F, bank_f, v_turned))
                        wait(pe, kq_made.after(turn))
                        for g in guards:
                            wait(pe, g.free(turn, step))
                        for c in range(4):
                            nc.tensor.transpose(b[0][:, P * c:P * c + P], src[:, P * c:P * c + P], ident[:, :])
                        for j in range(2):
                            i = 4 + j
                            m = nc.tensor.transpose(b[1][0:QN[i], P * j:P * j + P], src[:, Q0[i]:Q0[i] + QN[i]], ident[:, :])
                        m.then_inc(sig.sem, 1)
                    elif what == "kcache":
                        wait(pe, kc_in.after(turn, ago=1))
                        for g in bank_e:
                            wait(pe, g.free(turn, step))
                        for c in range(8):
                            m = nc.tensor.transpose(E[c // 4][:, P * (c % 4):P * (c % 4) + P], kc[:, c, :], ident[:, :])
                        m.then_inc(kc_turned.sem, 1)
                    elif what == "score":
                        i, = a
                        if i == 5:
                            wait(pe, kc_took.after(turn))
                        for guard, b, k0, n in score_banks(i):
                            wait(pe, guard.free(turn, step))
                            keys = kT[:, k0:k0 + n] if i < 5 else (kcT[:, k0:k0 + n] if k0 < PAST else kT[:, PROMPT:NTOK])
                            m = nc.tensor.matmul(b[0:QN[i], 0:n], qT[:, Q0[i]:Q0[i] + QN[i]], keys, start=True, stop=True)
                        m.then_inc(scored.sem, 1)
                    elif what == "turn":
                        i, = a
                        wait(pe, prob.after(turn, i))
                        wait(pe, bank_e[0].free(turn, step))
                        nb, tail = key_blocks(i)
                        for j in range(nb):
                            n = tail if j == nb - 1 else P
                            out, src = E[0][0:n, QN[i] * j:QN[i] * j + QN[i]], pr[0:QN[i], i % 2, P * j:P * j + n]
                            if i < 4:
                                m = nc.tensor.transpose(out, src, ident[:, :])
                            else:
                                m = nc.tensor.matmul(out, src, ident[0:QN[i], 0:QN[i]], start=True, stop=True)
                        m.then_inc(p_turned.sem, 1)
                    elif what == "value":
                        i, = a
                        wait(pe, pt_made.after(turn, i))
                        wait(pe, v_took.after(turn))
                        if i == 5:
                            wait(pe, vc_in.after(turn, ago=1))
                        wait(pe, bank_e[1].free(turn, step))
                        nb, tail = key_blocks(i)
                        for j in range(nb):
                            n = tail if j == nb - 1 else P
                            if i == 5 and j < 8:
                                v = vc[:, j, :]
                            elif i < 4 or j < 4 and i == 4:
                                v = vn[:, j, :]
                            else:
                                v = vn2[0:n, i - 4, :]
                            m = nc.tensor.matmul(E[1][:, 0:QN[i]], v, pt[0:n, i % 2, QN[i] * j:QN[i] * j + QN[i]],
                                                 start=(j == 0), stop=(j == nb - 1))
                        m.then_inc(summed.sem, 1)
            turns(pe, body)

        @block.scalar
        def _(act):
            act.wait_ge(start, 1)
            kp, ks = (io[n].rearrange("b t h d -> (b t) h d") for n in ("k_p", "k_s"))
            vp, vs = (io[n].rearrange("b t h d -> (b t) h d") for n in ("v_p", "v_s"))
            cache_k, cache_v = (io[n].rearrange("b (c p) h d -> p (b c) h d", p=P) for n in ("cache_k", "cache_v"))

            def body(turn):
                p = turn.p
                again = not (turn.fixed and p == 1)
                for step in turn.steps():
                    what, *a = step
                    if what == "split":
                        n, = a
                        act.wait_ge(scaled, SUBS_B * p + n + 1)
                        if not (turn.fixed and SUBS_B * p + n < split_ring):
                            act.wait_ge(sub_used, SUBS_B * p + n - split_ring + 1)
                        nc.scalar.activation(w_hi[:, n % split_ring], w_raw[:, n % raw_ring], ACT.Copy).then_inc(hi_made, 1)
                    elif what == "evac":
                        t, = a
                        act.wait_ge(sub_used, SUBS_B * p + 2 * t + 2)
                        b = main[2 * (t % 2):2 * (t % 2) + 2]
                        if t < 3:
                            if turn.behind:
                                wait(act, kq_made.after(turn))
                                wait(act, v_turned.after(turn))
                            if t != 1:
                                wait(act, sumsq.after(turn, t, back=1))
                            for e in range(2):
                                s = slice(e * HALF, (e + 1) * HALF)
                                if t != 1:
                                    nc.scalar.activation(sq[:, s], b[e][:, 0:HALF], ACT.Square)
                                m = nc.scalar.activation(raw[:, t, s], b[e][:, 0:HALF], ACT.Copy)
                        else:
                            wait(act, gate.after(turn, 3, ago=1))
                            for e in range(2):
                                m = nc.scalar.activation(zt[:, e * HALF:(e + 1) * HALF], b[e][:, 0:HALF], ACT.Tanh, scale=0.5)
                        m.then_inc(kept.sem, 1)
                    elif what == "root":
                        t, = a
                        wait(act, sumsq.after(turn, t))
                        wait(act, inverted.after(turn, t, back=1))
                        for e in range(2):
                            m = nc.scalar.activation(root[:, e * HALF:(e + 1) * HALF], E[e][:, 0:HALF], ACT.Sqrt,
                                                     bias=eps[:, 0:1], scale=1.0 / HD)
                        m.then_inc(rooted.sem, 1)
                    elif what == "tab":
                        if again:
                            wait(act, gated.after(turn, 5, ago=1))
                        wait(act, gate.after(turn, 3, ago=1))
                        nc.scalar.activation(zs[:], znew[:], ACT.Copy).then_inc(moved.sem, 1)
                    elif what in ("kout", "vout"):
                        turned, took, out, b, rows, rows2, dst, dst2 = (
                            (k_turned, k_took, k_out, E, kn, kn2, kp, ks) if what == "kout" else
                            (v_turned, v_took, v_out, F, vn, vn2, vp, vs))
                        wait(act, turned.after(turn))
                        if again:
                            wait(act, out.after(turn, ago=1))
                            wait(act, summed.after(turn, 5, ago=1))
                        nc.scalar.activation(rows[:].rearrange("p c d -> p (c d)"), b[0][:, 0:4 * P], ACT.Copy)
                        for j in range(2):
                            m = nc.scalar.activation(rows2[0:QN[4 + j], j], b[1][0:QN[4 + j], P * j:P * j + P], ACT.Copy)
                        m.then_inc(took.sem, 1)
                        wait(act, took.after(turn))
                        h = bass.ds(p - 1, 1)
                        act.dma_start(dst[0:4 * P, h, :].rearrange("(c p) h d -> p c (h d)", p=P), rows[:]).then_inc(out.sem, 16)
                        act.dma_start(dst[4 * P:PROMPT, h, :].rearrange("t h d -> t (h d)"), rows2[0:QN[4], 0]).then_inc(out.sem, 16)
                        act.dma_start(dst2[:, h, :].rearrange("t h d -> t (h d)"), rows2[0:SAMPLE, 1]).then_inc(out.sem, 16)
                    elif what == "kcache":
                        wait(act, kc_turned.after(turn))
                        if again:
                            wait(act, scored.after(turn, 5, ago=1))
                        for e in range(2):
                            m = nc.scalar.activation(kcT[:, 512 * e:512 * e + 512], E[e][:, :], ACT.Copy)
                        m.then_inc(kc_took.sem, 1)
                    elif what == "fetchk":
                        if turn.behind:
                            wait(act, kc_turned.after(turn))
                        act.dma_start(kc[:], cache_k[:, :, bass.ds(p, 1), :].rearrange("p c h d -> p c (h d)")).then_inc(kc_in.sem, 16)
                    elif what == "fetch":
                        if turn.behind:
                            wait(act, summed.after(turn, 5))
                            wait(act, biased.after(turn, 5))
                        act.dma_start(vc[:], cache_v[:, :, bass.ds(p, 1), :].rearrange("p c h d -> p c (h d)")).then_inc(vc_in.sem, 16)
                        act.dma_start(fbp[:], scratch["FP"][bass.ds(p, 1), :].broadcast_to([P, PROMPT])).then_inc(fb_in.sem, 16)
                        act.dma_start(fbs[:], scratch["FS"][bass.ds(p, 1), :].broadcast_to([SAMPLE, PAST + SAMPLE])
                                      ).then_inc(fb_in.sem, 16)
                    elif what == "score":
                        i, = a
                        q = slice(0, QN[i])
                        wait(act, maxed.after(turn, i))
                        nc.scalar.activation(pr[q, i % 2, 0:KN[i]], pr[q, i % 2, 0:KN[i]], ACT.Exp, bias=stat[q, i % 2, 1:2],
                                             accum_out=stat[q, i % 2, 2:3]).then_inc(expd.sem, 1)
                    elif what == "turn":
                        i, = a
                        wait(act, p_turned.after(turn, i))
                        wait(act, summed.after(turn, i, back=2))
                        nb, tail = key_blocks(i)
                        full = nb if tail == P else nb - 1
                        m = nc.scalar.activation(pt[:, i % 2, 0:QN[i] * full], E[0][:, 0:QN[i] * full], ACT.Copy)
                        if tail < P:
                            c = slice(QN[i] * full, QN[i] * nb)
                            m = nc.scalar.activation(pt[0:tail, i % 2, c], E[0][0:tail, c], ACT.Copy)
                        m.then_inc(pt_made.sem, 1)
                    elif what == "put":
                        wait(act, gated.after(turn, 5))
                        act.dma_start(scratch["fo"][bass.ds(p - 1, 1)].rearrange("k p t -> p (k t)"), fo[:]).then_inc(fo_out.sem, 16)
            turns(act, body)
            act.wait_ge(k_out.sem, 48 * FH)
            act.wait_ge(v_out.sem, 48 * FH)
            act.wait_ge(fo_out.sem, 16 * FH)

        @block.vector
        def _(dve):
            nc.vector.memset(eps[:], EPS).then_inc(start, 1)

            def body(turn):
                p = turn.p
                again = not (turn.fixed and p == 1)
                for step in turn.steps():
                    what, *a = step
                    if what == "scale":
                        n, = a
                        dve.wait_ge(w_in[n % raw_ring], 16 * (SUBS_B // raw_ring * p + n // raw_ring + 1))
                        g0 = (16 if n % SUBS_B < 4 else 32) + KSUB * (n % 2)
                        nc.vector.tensor_tensor(w_raw[:, n % raw_ring], w_raw[:, n % raw_ring],
                                                vec[:, g0:g0 + KSUB, None].broadcast_to([P, KSUB, P]), ALU.mult).then_inc(scaled, 1)
                    elif what == "split":
                        n, = a
                        dve.wait_ge(hi_made, SUBS_B * p + n + 1)
                        nc.vector.tensor_tensor(w_lo[:, n % split_ring], w_raw[:, n % raw_ring],
                                                w_hi[:, n % split_ring].bitcast(F32), ALU.subtract).then_inc(lo_made, 1)
                    elif what == "evac":
                        t, = a
                        wait(dve, kept.after(turn, t))
                        if t < 3:
                            nc.vector.memset(dummy[:], 0.0).then_inc(gate.sem, 1)
                            continue
                        if turn.behind:
                            wait(dve, moved.after(turn))
                        b = main[2 * (t % 2):2 * (t % 2) + 2]
                        for e in range(2):
                            s = slice(e * HALF, (e + 1) * HALF)
                            m = nc.vector.scalar_tensor_tensor(out=znew[:, s], in0=zt[:, s], scalar=1.0, in1=b[e][:, 0:HALF],
                                                               op0=ALU.add, op1=ALU.mult)
                        m.then_inc(gate.sem, 1)
                    elif what == "root":
                        t, = a
                        wait(dve, rooted.after(turn, t))
                        if turn.behind:
                            wait(dve, kq_made.after(turn))
                        nc.vector.reciprocal(rr[:, t // 2], root[:]).then_inc(inverted.sem, 1)
                    elif what == "tab":
                        wait(dve, inverted.after(turn, 2, ago=1))
                        if again:
                            wait(dve, scored.after(turn, 5, ago=1))
                        for out, t, g in ((kT, 0, 49), (qT, 2, 50)):
                            nc.vector.scalar_tensor_tensor(out=out[:], in0=raw[:, t], scalar=vec[:, g:g + 1], in1=rr[:, t // 2],
                                                           op0=ALU.mult, op1=ALU.mult).then_inc(kq_made.sem, 1)
                        if again:
                            wait(dve, biased.after(turn, 5, ago=1))
                        nc.vector.tensor_copy(fq[:, None, :], keep["fcol"][:, bass.ds(p - 1, 1), :]).then_inc(kq_made.sem, 1)
                        wait(dve, kq_made.after(turn))
                    elif what == "score":
                        i, = a
                        q, slot = slice(0, QN[i]), i % 2
                        wait(dve, scored.after(turn, i))
                        if i == 0:
                            wait(dve, fb_in.after(turn, ago=1))
                        wait(dve, p_turned.after(turn, i, back=2))
                        fb = fbp if i < 5 else fbs
                        for _, b, k0, n in score_banks(i):
                            m = nc.vector.scalar_tensor_tensor(out=pr[q, slot, k0:k0 + n], in0=b[q, 0:n], scalar=fq[q, i:i + 1],
                                                               in1=fb[q, k0:k0 + n], op0=ALU.add, op1=ALU.subtract)
                        m.then_inc(biased.sem, 1)
                        wait(dve, biased.after(turn, i))
                        diag = pr[q, slot, KN[i] - QN[i]:KN[i]]
                        nc.vector.tensor_tensor(diag, diag, causal[q, q], ALU.add).then_inc(masked.sem, 1)
                        wait(dve, masked.after(turn, i))
                        nc.vector.tensor_reduce(stat[q, slot, 0:1], pr[q, slot, 0:KN[i]], AX.X, ALU.max).then_inc(maxed.sem, 1)
                        wait(dve, maxed.after(turn, i, n=1))
                        nc.vector.tensor_scalar(stat[q, slot, 1:2], stat[q, slot, 0:1], -1.0, None, ALU.mult).then_inc(maxed.sem, 1)
                    elif what == "prob":
                        i, = a
                        q, slot = slice(0, QN[i]), i % 2
                        wait(dve, expd.after(turn, i))
                        nc.vector.reciprocal(stat[q, slot, 3:4], stat[q, slot, 2:3]).then_inc(inv_sum.sem, 1)
                        wait(dve, inv_sum.after(turn, i))
                        nc.vector.tensor_scalar(pr[q, slot, 0:KN[i]], pr[q, slot, 0:KN[i]], stat[q, slot, 3:4], None, ALU.mult
                                                ).then_inc(prob.sem, 1)
                    elif what == "value":
                        i, = a
                        wait(dve, summed.after(turn, i))
                        if i == 0:
                            wait(dve, moved.after(turn))
                            if again:
                                wait(dve, fo_out.after(turn, ago=1))
                        c = slice(Q0[i], Q0[i] + QN[i])
                        nc.vector.scalar_tensor_tensor(out=fo[:, c], in0=E[1][:, 0:QN[i]], scalar=0.5, in1=zs[:, c],
                                                       op0=ALU.mult, op1=ALU.mult).then_inc(gated.sem, 1)
            dummy = sb("dummy", [P, 1])
            turns(dve, body)


def conv_states(nc, top, io, keep):
    with ExitStack() as ctx:
        banks = [ctx.enter_context(nc.psum_tensor(f"c_bank{i}", [P, 512], F32)) for i in range(2)]
        rows = ctx.enter_context(nc.sbuf_tensor("c_rows", [P, 4, P], F32))
        turned, copied, stored = (top.semaphore("c_" + n) for n in ("turned", "copied", "stored"))
        cout = keep["cout"][:].rearrange("p s w t -> p (s w t)")
        n = HIST * CONV_TILES // 2
        block = ctx.enter_context(nc.Block())

        @block.tensor
        def _(pe):
            for i in range(4):
                m = nc.tensor.transpose(banks[0][0:n, P * i:P * i + P], cout[:, n * i:n * i + n], keep["const"]["ident"][:, :])
            m.then_inc(turned, 1)

        @block.vector
        def _(dve):
            dve.wait_ge(turned, 1)
            nc.vector.tensor_copy(rows[0:n].rearrange("p c d -> p (c d)"), banks[0][0:n, :]).then_inc(copied, 1)

        @block.sync
        def _(sp):
            sp.wait_ge(copied, 1)
            for s, name in enumerate(("conv_p", "conv_s")):
                dst = io[name].rearrange("l b w (t p) -> (l b w t) p", p=P)
                for i in range(2):
                    sp.dma_start(dst[n * i:n * i + n, :], rows[0:n, 2 * s + i]).then_inc(stored, 16)
            sp.wait_ge(stored, 64)



INPUTS = ["x_prompt", "x_sample", "cache_k", "cache_v", "cache_logf", "state_delta", "state_conv", "meta_tokens",
          "a_norm_g", "a_w_in", "a_conv_w", "a_a_log", "a_dt_bias", "a_out_norm_g", "a_w_out", "kv_norm_g", "kv_w",
          "kv_f_bias", "kv_k_norm_g", "b_norm_g", "b_w_in", "b_q_norm_g", "b_w_out"]
OUTPUTS = [("y_prompt", (1, SEQ, D)), ("y_sample", (1, SAMPLE, D)), ("delta_p", (1, 1, VH, HD, HD)),
           ("conv_p", (1, 1, HIST, CONV_DIM)), ("k_p", (1, PROMPT, FH, HD)), ("v_p", (1, PROMPT, FH, HD)),
           ("logf_p", (1, PROMPT, FH)), ("delta_s", (1, 1, VH, HD, HD)), ("conv_s", (1, 1, HIST, CONV_DIM)),
           ("k_s", (1, SAMPLE, FH, HD)), ("v_s", (1, SAMPLE, FH, HD)), ("logf_s", (1, SAMPLE, FH))]


def trunk(nc, io):
    with ExitStack() as top:
        def sb(name, shape, dt=F32):
            return top.enter_context(nc.sbuf_tensor(name, shape, dt))

        def dram(name, shape):
            return nc.dram_tensor(name, shape, F32, kind="Internal").ap()

        const_all = sb("const_all", [P, NCONST])
        keep = {"const_all": const_all, "const": {n: const_all[:, lo:hi] for n, (lo, hi) in CONST.items()},
                "vec": sb("vec", [P, 51]), "hist": sb("hist", [P, HIST, CONV_TILES]),
                "cw": sb("cw", [P, CONV_W, CONV_TILES]), "cout": sb("cout", [P, 2, HIST, CONV_TILES]),
                "fcol": sb("fcol", [P, FH, BLOCKS])}
        scratch = {"h0": dram("h0", (KT, P, NTOK)), "G": dram("G", (VH, NPAD)), "beta": dram("beta", (VH, NPAD)),
                   "o": dram("o", (VH, P, NTOK)), "FP": dram("FP", (FH, PROMPT)), "FS": dram("FS", (FH, PAST + SAMPLE)),
                   "fo": dram("fo", (FH, P, NTOK))}
        io["h1"] = dram("h1", (KT, P, NTOK))
        sems = Semaphores(nc)
        with ExitStack() as part:
            keep["tabs"] = part.enter_context(nc.sbuf_tensor("tabs", [P, PAIRS, 70], F32))
            for n in ("xh", "xl"):
                keep[n] = part.enter_context(nc.sbuf_tensor(n, [P, KT, NTOK], F32R))
            norm_and_gates(nc, sems, io, keep, scratch)
            sems.retire()
            delta_layer(nc, sems, io, keep, scratch)
        sems.retire()
        conv_states(nc, sems, io, keep)
        sems.retire()
        with ExitStack() as part:
            keep["r"] = part.enter_context(nc.sbuf_tensor("r", [P, NTOK], F32))
            project_back(nc, sems, io, keep, "a_", VH, scratch["o"], io["a_w_out"].rearrange("l (k p) n -> p (l k) n", p=P),
                         scratch["h0"])
            sems.retire()
            for n in ("xh_b", "xl_b"):
                keep[n] = part.enter_context(nc.sbuf_tensor(n, [P, KT, NTOK], F32R))
            forget_gates(nc, sems, io, keep, scratch)
            sems.retire()
            attention_layer(nc, sems, io, keep, scratch)
        sems.retire()
        project_back(nc, sems, io, keep, "y_", FH, scratch["fo"], io["b_w_out"].rearrange("l (k p) n -> p (l k) n", p=P),
                     io["h1"], (io["y_prompt"], io["y_sample"]))


def kernel(**inputs):
    import numpy as np
    import concourse.bacc as bacc
    from concourse.bass_utils import run_bass_kernel_spmd as run

    nc = bacc.Bacc("TRN2", target_bir_lowering=False, num_devices=1, dynamic_dma_scratch_size=4096)
    arrays = {"in_" + n: np.ascontiguousarray(inputs[n]) for n in INPUTS}
    arrays["in_consts"] = constants()
    io = {n[3:]: nc.dram_tensor(n, a.shape, F32, kind="ExternalInput").ap() for n, a in arrays.items()}
    for n, shape in OUTPUTS:
        io[n] = nc.dram_tensor("out_" + n, shape, F32, kind="ExternalOutput").ap()
    trunk(nc, io)
    r = run(nc, [arrays], core_ids=[0])
    return tuple(r.results[0]["out_" + n] for n, _ in OUTPUTS)
```

```python
from contextlib import ExitStack

import concourse.bass as bass
from concourse import mybir

ALU = mybir.AluOpType
ACT = mybir.ActivationFunctionType
AX = mybir.AxisListType
F32 = mybir.dt.float32
F32R = mybir.dt.float32r

P = 128
D = 2048
KT = D // P
N_META = 16
SEQ = 512
PROMPT = N_META + SEQ
SAMPLE = 32
NTOK = PROMPT + SAMPLE
HALF = NTOK // 2
PAST = 1024
EPS = 1e-6

HD = 128
PAIRS = 16
VH = 2 * PAIRS
CONV_W = 4
CONV_TILES = 4 * PAIRS
CONV_DIM = CONV_TILES * P
V_W = VH * HD
OFF_K, OFF_V, OFF_Z, OFF_B = D, 2 * D, CONV_DIM, CONV_DIM + V_W

C = 64
UNITS = 10
NPAD = UNITS * C
TAIL, SAMP = 8, 9
TAIL_N = PROMPT - TAIL * C
SAMP0 = SAMP * C
LEVELS = 6
HIST = CONV_W - 1

FH = 16
KSUB = 8
SUBS = 12
RAW_RING, SPLIT_RING = 3, 2
SKEW = 1
BUSY_A, BUSY_B = 6, 3

NEG = -1e30

_at = 0
CONST = {}
for _name, _n in (("ident", P), ("ones", P), ("eye64", C), ("level", LEVELS * C), ("below", C), ("above", C), ("incl", C), ("strict", C),
                  ("causal", P), ("scan", NPAD)):
    CONST[_name] = (_at, _at + _n)
    _at += _n
NCONST = _at


def constants():
    import numpy as np
    c = np.zeros((P, NCONST), np.float32)

    def put(name, a):
        lo, hi = CONST[name]
        c[:, lo:hi] = a
    put("ident", np.eye(P))
    put("ones", 1.0)
    row = np.arange(P)[:, None]
    j = row % C
    i = np.arange(C)[None, :]
    put("eye64", j == i)
    put("level", np.concatenate([((j >> l) % 2 == 1) & ((i >> l) == (j >> l) - 1) for l in range(LEVELS)], 1))
    put("below", -1.0 * ((j % 2 == 1) & (i == j - 1)))
    put("above", -1.0 * ((i % 2 == 1) & (j == i - 1)))
    put("incl", np.where(j <= i, 0.0, NEG))
    put("strict", j < i)
    put("causal", np.where(np.arange(P)[None, :] <= row, 0.0, NEG))
    put("scan", np.broadcast_to((np.arange(NPAD) % C != 0)[None, :], (P, NPAD)))
    return c


class Order:

    def __init__(self, steps, ahead, subs):
        self.steps = steps
        self.subs = subs
        self.ahead = ahead
        self.index, self.count = {}, {}
        for s in steps:
            self.index[s] = self.count.get(s[0], 0)
            self.count[s[0]] = self.index[s] + 1


class Turn:

    def __init__(self, order, p, front=True, behind=True, split=True, before=None):
        self.order, self.p, self.front, self.behind, self.split = order, p, front, behind, split
        self.before = before or order
        self.fixed = isinstance(p, int)

    def has(self, kind):
        return self.front if kind in self.order.ahead else self.behind

    def steps(self):
        def runs(s):
            if s[0] in ("scale", "split") and s[1] < 2:
                return self.fixed and self.p == 0
            if s[0] in ("scale", "split") and s[1] >= self.order.subs:
                return self.front and self.split
            return self.has(s[0])
        return [s for s in self.order.steps if runs(s)]

    def turns_before(self, kind):
        return self.p if kind in self.order.ahead else self.p - 1


class Signal:

    def __init__(self, sem, kind, per=1):
        self.sem, self.kind, self.per = sem, kind, per

    def after(self, turn, *args, n=None, ago=0, back=0):
        i = turn.order.index[(self.kind, *args)] - back
        each = turn.order.count[self.kind] * self.per
        value = (turn.turns_before(self.kind) - ago) * each + i * self.per + (self.per if n is None else n)
        return None if turn.fixed and value <= 0 else (self.sem, value)


class Bank:

    def __init__(self, taken):
        self.taken = taken

    def uses(self, s):
        return s[0] in self.taken and self.taken[s[0]][0](*s[1:])

    def free(self, turn, step):
        now = turn.steps()
        for s in reversed(now[:now.index(step)]):
            if self.uses(s):
                return self.taken[s[0]][1].after(turn, *s[1:])
        if turn.fixed and turn.p == 0:
            return None
        before = [s for s in turn.before.steps if s[0] in turn.order.ahead or not (turn.fixed and turn.p == 1)]
        for s in reversed(before):
            if self.uses(s):
                return self.taken[s[0]][1].after(turn, *s[1:], ago=1)
        return None


class Semaphores:

    def __init__(self, nc):
        self.nc, self.held = nc, []

    def semaphore(self, name):
        self.held.append(self.nc.alloc_semaphore(name=name))
        return self.held[-1]

    def retire(self):
        self.nc.all_engine_barrier()
        self.nc.clear_and_free_semaphores(self.held)
        self.nc.all_engine_barrier()
        self.held = []


def wait(engine, point):
    if point is not None:
        engine.wait_ge(*point)


PAIR_PLACES = {
    "tab": [0.01],
    "kqn": [1.01],
    "decay": [3.01],
    "split": [4.01, 11.01, 13.01, 19.01, 27.01, 36.02, 42.01, 50.01, 57.02, 64.03, 76.01, 82.02, 91.01, 96.05],
    "kkq": [10.01, 10.02, 12.01],
    "evac": [14.01, 32.01, 47.01, 76.02],
    "inv0": [14.02, 19.02],
    "knat": [16.01, 53.01, 54.02],
    "inv1": [17.01, 25.01, 26.01, 33.01, 40.01, 41.01, 47.02, 48.01, 60.02, 67.01],
    "vnat": [18.01, 18.02, 32.02],
    "tap": [20.01, 21.01, 23.01, 25.02, 33.02, 34.02, 36.01, 40.02, 53.02, 56.01, 59.01, 65.01, 78.04, 78.05,
        80.01, 82.01],
    "inv2": [23.02, 28.01, 30.02, 38.01, 43.01, 45.01, 50.02, 52.01, 66.03, 70.02],
    "conv": [28.02, 43.02, 66.02, 84.02],
    "silu": [30.01, 51.01, 70.03, 89.01],
    "square": [31.01, 58.01],
    "seq1": [33.03, 57.01, 60.04, 64.02, 67.02, 71.01, 76.03, 81.01, 86.01, 91.02],
    "sumsq": [34.01, 62.02],
    "root": [37.01, 64.01],
    "recip": [37.02, 48.02, 68.01, 73.01],
    "fetch": [39.01],
    "seq2": [54.01, 59.02, 62.01, 66.01, 69.01, 73.02, 78.03, 83.01, 88.01, 93.03],
    "square_o": [54.03, 60.03, 74.02, 77.01, 78.01, 87.01, 87.02, 87.03, 93.01, 94.02],
    "seq3": [55.01, 60.01, 62.03, 66.04, 70.01, 74.01, 79.01, 84.01, 89.02, 94.01],
    "osq": [78.02, 93.02, 96.01],
    "zevac": [91.03, 96.06],
    "otr": [94.03, 96.03, 96.04],
    "states": [96.02],
    "put": [96.07],
}
LAST_PAIR_PLACES = {
    "tab": [0.01],
    "kqn": [0.02],
    "decay": [1.01],
    "kkq": [3.01, 4.01, 5.01],
    "inv0": [5.02, 7.01],
    "inv1": [6.01, 8.01, 12.01, 13.01, 17.02, 19.02, 26.01, 27.01, 48.01, 65.02],
    "inv2": [7.02, 12.02, 12.03, 19.01, 20.01, 21.01, 34.01, 35.01, 54.01, 70.02],
    "vnat": [7.03, 8.02, 37.01],
    "knat": [17.01, 41.02, 42.01],
    "seq1": [41.01, 44.01, 50.01, 57.01, 67.01, 71.02, 74.02, 83.01, 86.01, 89.01],
    "seq2": [41.03, 45.01, 51.01, 64.01, 68.01, 73.01, 77.02, 84.01, 87.01, 92.01],
    "square_o": [42.02, 57.02, 71.01, 73.02, 76.01, 77.01, 86.02, 87.02, 88.03, 93.01],
    "seq3": [43.01, 45.02, 53.01, 65.01, 70.01, 74.01, 77.03, 85.01, 88.01, 92.02],
    "osq": [85.02, 88.02, 93.02],
    "otr": [92.03, 94.01, 96.01],
    "put": [93.03],
    "states": [96.02],
}


def place(places, arguments, ksteps, ahead, subs):
    steps = [((n, 1.0), ("kstep", *divmod(n, KSUB))) for n in range(ksteps)]
    for kind, at in places.items():
        assert len(at) == len(arguments[kind])
        steps += [((int(x), x - int(x)), (kind, *a)) for x, a in zip(at, arguments[kind])]
    return Order([s for _, s in sorted(steps, key=lambda s: s[0])], ahead | {"kstep"}, subs)


def pair_order(places):
    inverse = [(b, l) for n in range(LEVELS + SKEW) for b, l in ((0, n), (1, n - SKEW)) if 1 <= l < LEVELS]
    units, groups, once = [(c,) for c in range(UNITS)], [(g,) for g in range(3)], [()]
    tiles, qk = [(t,) for t in range(4)], [(t,) for t in range(2)]
    arguments = {
        "split": [(n,) for n in range(SUBS + 2)], "evac": tiles, "tap": [(t, w) for t in range(4) for w in range(CONV_W)],
        "conv": tiles, "silu": tiles, "square": qk, "sumsq": qk, "root": qk, "recip": [(t, e) for t in range(2) for e in range(2)],
        "zevac": [(4,), (5,)], "fetch": once,
        "tab": once, "decay": once, "kqn": once, "kkq": groups, "knat": groups, "vnat": groups, "inv0": [(b,) for b in range(2)], "inv1": inverse,
        "inv2": inverse, "seq1": units, "seq2": units, "seq3": units, "square_o": units, "states": once, "osq": groups,
        "otr": groups, "put": once}
    return place(places, arguments, SUBS * KSUB, set(list(arguments)[:list(arguments).index("tab")]), SUBS)


def batch(b, l=0):
    return list(range(5 * b, 5 * b + 5 if (b, l) != (1, LEVELS - 1) else TAIL))


def group(g):
    return list(range(4 * g, min(4 * g + 4, UNITS)))


def norm_and_gates(nc, top, io, keep, scratch):
    with ExitStack() as ctx:
        def sb(name, shape, dt=F32):
            return ctx.enter_context(nc.sbuf_tensor(name, shape, dt))

        def sem(name):
            return top.semaphore(name)

        banks = [ctx.enter_context(nc.psum_tensor(f"p1_bank{i}", [P, 512], F32)) for i in range(8)]
        const, xh, xl = keep["const"], keep["xh"], keep["xl"]
        ident, ones = const["ident"], const["ones"]
        hT = sb("hT", [P, KT, NTOK])
        rows = sb("rows", [P, 2, D])
        vec_rows = sb("vec_rows", [51, P])
        cw_rows = sb("cw_rows", [P, 2, P])
        hist_rows = sb("hist_rows", [96, 2, P])
        wab = sb("wab", [P, KT, 2 * VH])
        gate_in = sb("gate_in", [64, 2])
        sq = sb("sq", [P, 2, NTOK])
        xn = sb("xn", [P, 2, NTOK])
        rt = sb("rt", [P, NTOK])
        rb = sb("rb", [P, NTOK])
        eps = sb("eps", [P, 1])
        gat = sb("gat", [64, 4, NTOK])
        decay_rate = sb("decay_rate", [64, 1])
        GT = sb("GT", [64, NPAD])
        BT = sb("BT", [32, NPAD])
        twice = sb("twice", [64, UNITS, 2, C])
        glast_in = sb("glast_in", [64, UNITS, VH])
        Gs = sb("Gs", [P, 4, PAIRS, UNITS])
        tabs = keep["tabs"]

        row_in = [sem(f"row_in{i}") for i in range(2)]
        small_in = sem("small_in")
        wab_in = sem("wab_in")
        turned = sem("turned")
        took_a = sem("took_a")
        took_v = sem("took_v")
        took_small = sem("took_small")
        squared = sem("squared")
        summed = sem("summed")
        rooted = sem("rooted")
        inverted = sem("inverted")
        normed = sem("normed")
        high = sem("high")
        low = sem("low")
        ab_step = sem("ab_step")
        gate_a = sem("gate_a")
        gate_v = sem("gate_v")
        gate_p = sem("gate_p")
        stored = sem("p1_stored")
        block = ctx.enter_context(nc.Block())

        x_p = io["x_prompt"].rearrange("b t d -> (b t) d")
        x_s = io["x_sample"].rearrange("b t d -> (b t) d")
        tiles = [(P, [(io["meta_tokens"], 0, N_META, 0), (x_p, 0, P - N_META, N_META)])]
        tiles += [(P, [(x_p, P * i - N_META, P, 0)]) for i in range(1, 4)]
        tiles += [(N_META + SAMPLE, [(x_p, SEQ - N_META, N_META, 0), (x_s, 0, SAMPLE, N_META)])]

        @block.sync
        def _(sp):
            sp.dma_start(keep["const_all"][:], io["consts"]).then_inc(small_in, 16)
            for n, name in enumerate(("a_norm_g", "kv_norm_g", "b_norm_g")):
                src = io[name] if name == "kv_norm_g" else io[name].rearrange("l d -> (l d)")
                sp.dma_start(vec_rows[16 * n:16 * n + 16, :], src.rearrange("(k p) -> k p", p=P)).then_inc(small_in, 16)
            for n, name in enumerate(("a_out_norm_g", "kv_k_norm_g", "b_q_norm_g")):
                src = io[name].rearrange("(l d) -> l d", l=1) if name == "kv_k_norm_g" else io[name]
                sp.dma_start(vec_rows[48 + n:49 + n, :], src).then_inc(small_in, 16)
            cw = io["a_conv_w"].rearrange("l w (t p) -> (l w t) p", p=P)
            for n in range(2):
                sp.dma_start(cw_rows[:, n, :], cw[P * n:P * n + P, :]).then_inc(small_in, 16)
            hist = io["state_conv"].rearrange("l b w (t p) -> (l b w t) p", p=P)
            for n in range(2):
                sp.dma_start(hist_rows[:, n, :], hist[96 * n:96 * n + 96, :]).then_inc(small_in, 16)
            sp.dma_start(gate_in[32:64, 0:1], io["a_a_log"].rearrange("l h -> h l")).then_inc(small_in, 16)
            sp.dma_start(gate_in[32:64, 1:2], io["a_dt_bias"].rearrange("l h -> h l")).then_inc(small_in, 16)
            for i, (_, parts) in enumerate(tiles):
                if i >= 2:
                    sp.wait_ge(turned, 2 + 4 * (i - 1))
                for n, (src, r0, nr, at) in enumerate(parts):
                    d = sp.dma_start(rows[at:at + nr, i % 2, :], src[r0:r0 + nr, :])
                    d.then_inc(row_in[i % 2], 16)
                if i == 0:
                    sp.dma_start(wab[:], io["a_w_in"].rearrange("l (k p) n -> p (l k) n", p=P)[:, :, OFF_B:OFF_B + 2 * VH]
                                 ).then_inc(wab_in, 16)
            sp.wait_ge(took_a, 10)
            sp.wait_ge(took_v, 10)
            sp.dma_start(scratch["h0"].rearrange("k p t -> p k t"), hT[:]).then_inc(stored, 16)
            sp.wait_ge(gate_v, 9)
            sp.dma_start(scratch["G"], GT[32:64, :]).then_inc(stored, 16)
            sp.dma_start(scratch["beta"], BT[:]).then_inc(stored, 16)
            sp.wait_ge(stored, 48)

        SMALL = 13 * 16

        @block.tensor
        def _(pe):
            pe.wait_ge(small_in, SMALL)
            nc.tensor.transpose(banks[6][:, 0:51], vec_rows[:, :], ident[0:51, 0:51])
            for n in range(2):
                nc.tensor.transpose(banks[6][:, 64 + 96 * n:160 + 96 * n], hist_rows[:, n, :], ident[0:96, 0:96])
            for n in range(2):
                m = nc.tensor.transpose(banks[7][:, P * n:P * n + P], cw_rows[:, n, :], ident[:, :])
            m.then_inc(turned, 2)
            per_slot = [0, 0]
            for i, (nr, parts) in enumerate(tiles):
                per_slot[i % 2] += 16 * len(parts)
                pe.wait_ge(row_in[i % 2], per_slot[i % 2])
                for q in range(4):
                    b = (4 * i + q) % 4
                    if 4 * i + q >= 4:
                        pe.wait_ge(took_a if b % 2 == 0 else took_v, 2 * (i - 1) + q // 2 + 1)
                    for k in range(4):
                        m = nc.tensor.transpose(banks[b][:, P * k:P * k + nr],
                                                rows[0:nr, i % 2, P * (4 * q + k):P * (4 * q + k) + P],
                                                ident[0:nr, 0:nr])
                    m.then_inc(turned, 1)
            for k in range(KT):
                pe.wait_ge(squared, k + 1)
                for h in range(2):
                    m = nc.tensor.matmul(banks[4 + h][:, 0:HALF], ones[:, :], sq[:, k % 2, h * HALF:(h + 1) * HALF],
                                         start=(k == 0), stop=(k == KT - 1))
                m.then_inc(summed, 1)
            pe.wait_ge(took_a, 10)
            pe.wait_ge(took_v, 10)
            pe.wait_ge(wab_in, 16)
            for k in range(KT):
                pe.wait_ge(normed, k + 1)
                for h in range(2):
                    m = nc.tensor.matmul(banks[h][0:64, 0:HALF], wab[:, k, :], xn[:, k % 2, h * HALF:(h + 1) * HALF],
                                         start=(k == 0), stop=(k == KT - 1))
                m.then_inc(ab_step, 1)
            pe.wait_ge(gate_v, 10)
            pe.wait_ge(took_small, 1)
            for u in range(UNITS):
                for r, b in ((slice(32, 64), 2), (slice(0, 32), 3)):
                    m = nc.tensor.transpose(banks[b][:, 32 * u:32 * u + 32], twice[r, u].rearrange("h c t -> h (c t)"),
                                            ident[r, r])
            m.then_inc(gate_p, 1)
            nc.tensor.matmul(banks[6][:, 0:32 * UNITS], ones[32:64, :], glast_in[32:64].rearrange("h u g -> h (u g)"),
                             start=True, stop=True).then_inc(gate_p, 1)

        @block.scalar
        def _(act):
            act.wait_ge(turned, 2)
            nc.scalar.activation(keep["vec"][:], banks[6][:, 0:51], ACT.Copy)
            nc.scalar.activation(keep["hist"][:].rearrange("p w t -> p (w t)"), banks[6][:, 64:256], ACT.Copy)
            nc.scalar.activation(keep["cw"][:].rearrange("p w t -> p (w t)"), banks[7][:, 0:256], ACT.Copy,
                                 scale=0.5).then_inc(took_small, 1)
            col = 0
            for i, (nr, _) in enumerate(tiles):
                for q in (0, 2):
                    act.wait_ge(turned, 2 + 4 * i + q + 1)
                    nc.scalar.activation(hT[:, 4 * q:4 * q + 4, col:col + nr],
                                         banks[q].rearrange("p (k t) -> p k t", k=4)[:, :, 0:nr],
                                         ACT.Copy).then_inc(took_a, 1)
                col += nr
            act.wait_ge(took_v, 10)
            act.wait_ge(took_a, 10)
            for k in range(KT):
                if k >= 2:
                    act.wait_ge(summed, k - 1)
                nc.scalar.activation(sq[:, k % 2, :], hT[:, k, :], ACT.Square).then_inc(squared, 1)
            act.wait_ge(summed, KT)
            act.wait_ge(gate_v, 1)
            for h in range(2):
                m = nc.scalar.activation(rt[:, h * HALF:(h + 1) * HALF], banks[4 + h][:, 0:HALF], ACT.Sqrt,
                                         bias=eps[:, 0:1], scale=1.0 / D)
            m.then_inc(rooted, 1)
            for k in range(KT):
                act.wait_ge(normed, k + 1)
                nc.scalar.activation(xh[:, k, :], xn[:, k % 2, :], ACT.Copy).then_inc(high, 1)
            act.wait_ge(ab_step, KT)
            for h in range(2):
                s = slice(h * HALF, (h + 1) * HALF)
                nc.scalar.activation(gat[0:32, 0, s], banks[h][0:32, 0:HALF], ACT.Exp, scale=-1.0)
                nc.scalar.activation(gat[32:64, 0, s], banks[h][32:64, 0:HALF], ACT.Identity, bias=gate_in[32:64, 1:2])
                m = nc.scalar.activation(gat[32:64, 1, s], banks[h][32:64, 0:HALF], ACT.Abs, bias=gate_in[32:64, 1:2])
            m.then_inc(gate_a, 1)
            act.wait_ge(gate_a, 1)
            nc.scalar.activation(gat[32:64, 2, :], gat[32:64, 1, :], ACT.Exp, scale=-1.0).then_inc(gate_a, 1)
            nc.scalar.activation(decay_rate[32:64, :], gate_in[32:64, 0:1], ACT.Exp).then_inc(gate_a, 1)
            act.wait_ge(gate_a, 2)
            nc.scalar.activation(gat[32:64, 3, :], gat[32:64, 2, :], ACT.Ln, bias=1.0).then_inc(gate_a, 1)
            act.wait_ge(gate_v, 12)
            nc.scalar.activation(Gs[:, 1], tabs[:, :, 0:10], ACT.Exp)
            nc.scalar.activation(tabs[:, :, 40:50], Gs[:, 0], ACT.Exp)
            nc.scalar.activation(tabs[:, :, 20:30], Gs[:, 2], ACT.Exp).then_inc(gate_a, 1)
            act.wait_ge(gate_p, 2)
            glast = banks[6][:, 0:32 * UNITS].rearrange("p (u q h) -> p h q u", q=PAIRS, h=2)
            for h in range(2):
                m = nc.scalar.activation(tabs[:, :, 50 + 10 * h:60 + 10 * h], glast[:, h], ACT.Exp)
            m.then_inc(gate_a, 1)

        @block.vector
        def _(dve):
            def low_part(k):
                dve.wait_ge(high, k + 1)
                nc.vector.tensor_tensor(xl[:, k, :], xn[:, k % 2, :], xh[:, k, :].bitcast(F32),
                                        ALU.subtract).then_inc(low, 1)

            nc.vector.memset(eps[:], EPS).then_inc(gate_v, 1)
            col = 0
            for i, (nr, _) in enumerate(tiles):
                for q in (1, 3):
                    dve.wait_ge(turned, 2 + 4 * i + q + 1)
                    nc.vector.tensor_copy(hT[:, 4 * q:4 * q + 4, col:col + nr],
                                          banks[q].rearrange("p (k t) -> p k t", k=4)[:, :, 0:nr]).then_inc(took_v, 1)
                col += nr
            nc.vector.memset(GT[:], 0.0)
            nc.vector.memset(BT[:], 0.0).then_inc(gate_v, 1)
            dve.wait_ge(rooted, 1)
            nc.vector.reciprocal(rb[:], rt[:]).then_inc(inverted, 1)
            dve.wait_ge(took_small, 1)
            dve.wait_ge(inverted, 1)
            dve.wait_ge(took_a, 10)
            for k in range(KT):
                if k >= 2:
                    dve.wait_ge(high, k - 1)
                    dve.wait_ge(low, k - 1)
                    dve.wait_ge(ab_step, k - 1)
                nc.vector.scalar_tensor_tensor(out=xn[:, k % 2, :], in0=hT[:, k, :], scalar=keep["vec"][:, k:k + 1],
                                               in1=rb[:], op0=ALU.mult, op1=ALU.mult).then_inc(normed, 1)
                if k:
                    low_part(k - 1)
            low_part(KT - 1)
            dve.wait_ge(gate_a, 1)
            b = gat[0:32]
            nc.vector.tensor_scalar(b[:, 1, :], b[:, 0, :], 1.0, None, ALU.add).then_inc(gate_v, 1)
            dve.wait_ge(gate_v, 3)
            for dst, src in ((slice(0, PROMPT), slice(0, PROMPT)), (slice(SAMP0, SAMP0 + SAMPLE), slice(PROMPT, NTOK))):
                m = nc.vector.reciprocal(BT[:, dst], b[:, 1, src])
            m.then_inc(gate_v, 1)
            a = gat[32:64]
            dve.wait_ge(gate_a, 4)
            nc.vector.scalar_tensor_tensor(out=a[:, 1, :], in0=a[:, 0, :], scalar=0.0, in1=a[:, 3, :],
                                           op0=ALU.max, op1=ALU.add).then_inc(gate_v, 1)
            dve.wait_ge(gate_v, 5)
            nc.vector.tensor_scalar(a[:, 2, :], a[:, 1, :], decay_rate[32:64, 0:1], -1.0,
                                    ALU.mult, ALU.mult).then_inc(gate_v, 1)
            dve.wait_ge(gate_v, 6)
            nc.vector.tensor_copy(GT[32:64, 0:PROMPT], a[:, 2, 0:PROMPT])
            nc.vector.tensor_copy(GT[32:64, SAMP0:SAMP0 + SAMPLE], a[:, 2, PROMPT:NTOK]).then_inc(gate_v, 1)
            dve.wait_ge(gate_v, 7)
            nc.vector.tensor_tensor_scan(GT[32:64, :], const["scan"][32:64, :], GT[32:64, :], 0.0,
                                         ALU.mult, ALU.add).then_inc(gate_v, 2)
            dve.wait_ge(gate_v, 9)
            for r, x in ((slice(32, 64), GT), (slice(0, 32), BT)):
                nc.vector.tensor_copy(twice[r], x[r].rearrange("h (u c) -> h u c", c=C)[:, :, None, :].broadcast_to([32, UNITS, 2, C]))
            last = GT[32:64].rearrange("h (u c) -> h u c", c=C)[:, :, C - 1:C].broadcast_to([32, UNITS, VH])
            nc.vector.tensor_tensor(glast_in[32:64], last, ident[32:64, None, 32:64].broadcast_to([32, UNITS, VH]),
                                    ALU.mult).then_inc(gate_v, 1)
            dve.wait_ge(gate_p, 2)
            G = banks[2][:, 0:32 * UNITS].rearrange("p (u q h) -> p h q u", q=PAIRS, h=2)
            Bt = banks[3][:, 0:32 * UNITS].rearrange("p (u q h) -> p h q u", q=PAIRS, h=2)
            gl = banks[6][:, 0:32 * UNITS].rearrange("p (u q h) -> p h q u", q=PAIRS, h=2)
            for h in range(2):
                r = slice(64 * h, 64 * h + 64)
                nc.vector.tensor_copy(tabs[r, :, 0:10], G[r, h])
                nc.vector.tensor_copy(Gs[r, 0], G[r, 1 - h])
                nc.vector.tensor_copy(Gs[r, 3], gl[r, h])
                m = nc.vector.tensor_copy(tabs[r, :, 30:40], Bt[r, h])
            m.then_inc(gate_v, 1)
            dve.wait_ge(gate_v, 11)
            nc.vector.tensor_tensor(Gs[:, 2], Gs[:, 3], tabs[:, :, 0:10], ALU.subtract).then_inc(gate_v, 1)
            dve.wait_ge(gate_a, 5)
            nc.vector.scalar_tensor_tensor(out=tabs[:, :, 10:20], in0=Gs[:, 1], scalar=-1.0, in1=tabs[:, :, 30:40],
                                           op0=ALU.mult, op1=ALU.mult).then_inc(gate_v, 1)
            dve.wait_ge(gate_v, 13)
            nc.vector.tensor_scalar(keep["vec"][:, 48:49], keep["vec"][:, 48:49], 0.5, None, ALU.mult)



def delta_layer(nc, top, io, keep, scratch):
    order, last_order = pair_order(PAIR_PLACES), pair_order({**PAIR_PLACES, **LAST_PAIR_PLACES})
    with ExitStack() as ctx:
        def sb(name, shape, dt=F32):
            return ctx.enter_context(nc.sbuf_tensor(name, shape, dt))

        def sem(name):
            return top.semaphore(name)

        def signal(name, kind, per=1):
            return Signal(sem(name), kind, per)

        main = [ctx.enter_context(nc.psum_tensor(f"main{i}", [P, 512], F32)) for i in range(4)]
        E = [ctx.enter_context(nc.psum_tensor(f"E{i}", [P, 512], F32)) for i in range(2)]
        F = [ctx.enter_context(nc.psum_tensor(f"F{i}", [P, 512], F32)) for i in range(2)]
        const, xh, xl, tabs = keep["const"], keep["xh"], keep["xl"], keep["tabs"]
        ident, ones, eye64 = const["ident"], const["ones"], const["eye64"]
        vec, cw, hist = keep["vec"], keep["cw"], keep["hist"]

        w_raw = sb("w_raw", [P, RAW_RING, KSUB, P])
        w_hi = sb("w_hi", [P, SPLIT_RING, KSUB, P], F32R)
        w_lo = sb("w_lo", [P, SPLIT_RING, KSUB, P], F32R)
        xp = sb("xp", [P, 2, NPAD + 8])
        y = sb("y", [P, NPAD])
        th = sb("th", [P, NPAD])
        cqk = sb("cqk", [P, 2, NPAD])
        cv = sb("cv", [P, UNITS, 2, C])
        sq = sb("sq2", [P, NPAD])
        root = sq
        rqk = sb("rqk", [P, 2, NPAD])
        zt = th[:, 0:NTOK]
        znew = sb("znew", [P, 2, NTOK])
        zs = sb("zs", [P, 2, NTOK])
        kqk = sb("kqk", [P, UNITS, 4, C])
        kc = sb("kc", [P, UNITS, P])
        bv = sb("bv", [P, UNITS, P])
        dec = sb("dec", [P, NPAD])
        bdec = sb("bdec", [P, NPAD])
        MT = sb("MT", [P, UNITS, P])
        QK = sb("QK", [P, UNITS, P])
        Tc = sb("Tc", [P, UNITS, C])
        TTc = sb("TTc", [P, UNITS, C])
        TT = sb("TT", [P, UNITS, P])
        Yc = sb("Yc", [P, 2, 5, C])
        Y = sb("Y", [P, 2, 5, P])
        S = sb("S", [P, 2, 2, HD])
        Rr = sb("Rr", [P, HD])
        oq = sb("oq", [P, HD])
        vn = sb("vn", [P, HD])
        vnd = sb("vnd", [P, 2, HD])
        on = sb("on", [P, UNITS, HD])
        osum = sb("osum", [P, 3, UNITS])
        o_squares = sb("o_squares", [P, HD])
        ot = sb("ot", [P, 2, NTOK])
        ptab = sb("ptab", [P, 70])
        cout = keep["cout"]
        eps = sb("eps2", [P, 1])

        w_in = [sem(f"w_in{i}") for i in range(RAW_RING)]
        hi_made, lo_made, sub_used = sem("hi_made"), sem("lo_made"), sem("sub_used")
        ready = sem("p2_ready")
        xp_made = signal("xp_made", "evac")
        taps = signal("taps", "tap")
        kept = signal("kept", "conv")
        tanh_y = signal("tanh_y", "conv")
        silu = signal("silu", "silu")
        z_tanh = signal("z_tanh", "zevac")
        z_made = signal("z_made", "zevac")
        square = signal("square", "square")
        sumsq = signal("sumsq", "sumsq")
        rooted = signal("rooted2", "root")
        inverted = signal("inverted2", "recip")
        tables = signal("tables", "tab")
        g_in, b_in = signal("g_in", "fetch", 32), signal("b_in", "fetch", 32)
        s_in = signal("s_in", "tab", 16)
        s_zero = signal("s_zero", "tab")
        z_moved = signal("z_moved", "tab")
        g_sum = signal("g_sum", "decay", 2)
        dec_made = signal("dec_made", "decay")
        bdec_made = signal("bdec_made", "decay", 2)
        kq_made = signal("kq_made", "kqn", 3)
        kkq_sum, kkq_took = signal("kkq_sum", "kkq"), signal("kkq_took", "kkq")
        knat_t, kc_made = signal("knat_t", "knat"), signal("kc_made", "knat")
        vnat_t, bv_made = signal("vnat_t", "vnat"), signal("bv_made", "vnat")
        mt_sum, y_made, y_spread = signal("mt_sum", "inv1"), signal("y_made", "inv1"), signal("y_spread", "inv1")
        ty_sum, t_made, tt_spread = signal("ty_sum", "inv2"), signal("t_made", "inv2", 2), signal("tt_spread", "inv2")
        m_sum, t0_made, tt0_spread = signal("m_sum", "inv0"), signal("t0_made", "inv0", 4), signal("tt0_spread", "inv0")
        ks_sum, r_made, oq_made = signal("ks_sum", "seq1"), signal("r_made", "seq1"), signal("oq_made", "seq1")
        vn_sum, vn_made = signal("vn_sum", "seq2"), signal("vn_made", "seq2")
        os_sum, s_made = signal("os_sum", "seq3"), signal("s_made", "seq3")
        o_summed = signal("o_summed", "square_o")
        o_rooted, o_normed = signal("o_rooted", "osq"), signal("o_normed", "osq", 2)
        o_turned, o_gated = signal("o_turned", "otr"), signal("o_gated", "otr")
        o_out = signal("o_out", "put", 16)
        s_out = signal("s_out", "states", 32)

        bank_e = [
            Bank({"kkq": (lambda g: g % 2 == 0, kkq_took), "knat": (lambda g: g % 2 == 1, kc_made),
                  "vnat": (lambda g: g % 2 == 0, bv_made), "inv0": (lambda b: True, t0_made),
                  "inv1": (lambda b, l: True, y_made), "inv2": (lambda b, l: l < LEVELS - 1, t_made), "otr": (lambda g: g % 2 == 0, o_gated),
                  "sumsq": (lambda t: True, rooted)}),
            Bank({"kkq": (lambda g: g % 2 == 1, kkq_took), "knat": (lambda g: g % 2 == 0, kc_made),
                  "vnat": (lambda g: g % 2 == 1, bv_made), "inv2": (lambda b, l: True, t_made),
                  "otr": (lambda g: g % 2 == 1, o_gated), "sumsq": (lambda t: True, rooted)}),
        ]


        def turns(engine, body):
            body(Turn(order, 0, behind=False))
            body(Turn(order, 1))
            with engine.Fori(2, PAIRS - 1) as p:
                body(Turn(order, p))
            body(Turn(order, PAIRS - 1, split=False))
            body(Turn(last_order, PAIRS, front=False, before=order))

        block = ctx.enter_context(nc.Block())

        @block.sync
        def _(sp):
            w = io["a_w_in"].rearrange("l (k p) n -> p (l k) n", p=P)

            def body(turn):
                if not turn.front:
                    return
                p = turn.p
                column = [P * p, OFF_K + P * p, OFF_V + 2 * P * p, OFF_V + 2 * P * p + P,
                          OFF_Z + 2 * P * p, OFF_Z + 2 * P * p + P]
                for n in range(SUBS):
                    if not (turn.fixed and SUBS * p + n < RAW_RING):
                        sp.wait_ge(lo_made, SUBS * p + n - RAW_RING + 1)
                    k0 = KSUB * (n % 2)
                    sp.dma_start(w_raw[:, n % RAW_RING], w[:, k0:k0 + KSUB, bass.ds(column[n // 2], P)]
                                 ).then_inc(w_in[n % RAW_RING], 16)
            turns(sp, body)

        @block.gpsimd
        def _(pool):
            nc.gpsimd.memset(MT[:], 0.0)
            nc.gpsimd.memset(QK[:], 0.0)
            nc.gpsimd.memset(TT[:], 0.0)
            nc.gpsimd.memset(Y[:], 0.0)
            nc.gpsimd.memset(vnd[:], 0.0)
            nc.gpsimd.memset(xp[:], 0.0).then_inc(ready, 1)

        @block.tensor
        def _(pe):
            pe.wait_ge(ready, 1)

            def keep_busy(n):
                for _ in range(n):
                    nc.tensor.matmul(main[0][:, 0:HALF], w_hi[:, 0, 0, :], xh[:, 0, 0:HALF], start=True, stop=True)

            def body(turn):
                p = turn.p
                if not turn.front:
                    wait(pe, z_made.after(turn, 5, ago=1))
                for step in turn.steps():
                    what, *a = step
                    if not turn.front and what in ("kkq", "inv0", "inv1", "inv2", "seq1", "seq2", "seq3", "otr"):
                        keep_busy(BUSY_A)
                    if what == "kstep":
                        n, k = a
                        t = n // 2
                        if k == 0:
                            pe.wait_ge(lo_made, SUBS * p + n + 1)
                            if n % 2 == 0 and not (turn.fixed and p == 0 and t < 2):
                                wait(pe, z_made.after(turn, 4 + t, ago=1) if t < 2 else xp_made.after(turn, t - 2))
                        for hi, x in ((w_hi, xh), (w_hi, xl), (w_lo, xh)):
                            for h in range(2):
                                m = nc.tensor.matmul(main[2 * (t % 2) + h][:, 0:HALF], hi[:, n % SPLIT_RING, k, :],
                                                     x[:, KSUB * (n % 2) + k, h * HALF:(h + 1) * HALF],
                                                     start=(n % 2 == 0 and k == 0 and hi is w_hi and x is xh),
                                                     stop=(n % 2 == 1 and k == KSUB - 1 and hi is w_lo))
                        if k == KSUB - 1:
                            m.then_inc(sub_used, 1)
                    elif what == "sumsq":
                        t, = a
                        wait(pe, square.after(turn, t))
                        for e in range(2):
                            wait(pe, bank_e[e].free(turn, step))
                        for e in range(2):
                            m = nc.tensor.matmul(E[e][:, 0:NPAD // 2], ones[:, :], sq[:, e * NPAD // 2:(e + 1) * NPAD // 2],
                                                 start=True, stop=True)
                        m.then_inc(sumsq.sem, 1)
                    elif what == "kkq":
                        g, = a
                        wait(pe, kq_made.after(turn))
                        wait(pe, bank_e[g % 2].free(turn, step))
                        for i, u in enumerate(group(g)):
                            m = nc.tensor.matmul(E[g % 2][:, P * i:P * i + P], kqk[:, u, 0:2, :].rearrange("p s c -> p (s c)"),
                                                 kqk[:, u, 1:3, :], start=True, stop=True)
                        m.then_inc(kkq_sum.sem, 1)
                    elif what == "knat":
                        g, = a
                        wait(pe, kq_made.after(turn))
                        wait(pe, bank_e[1 - g % 2].free(turn, step))
                        for i, u in enumerate(group(g)):
                            m = nc.tensor.transpose(E[1 - g % 2][:, P * i:P * i + P], kqk[:, u, 0:2, :].rearrange("p s c -> p (s c)"), ident[:, :])
                        m.then_inc(knat_t.sem, 1)
                    elif what == "vnat":
                        g, = a
                        wait(pe, kq_made.after(turn))
                        wait(pe, bank_e[g % 2].free(turn, step))
                        for i, u in enumerate(group(g)):
                            m = nc.tensor.transpose(E[g % 2][:, P * i:P * i + P], cv[:, u].rearrange("p s c -> p (s c)"), ident[:, :])
                        m.then_inc(vnat_t.sem, 1)
                    elif what == "inv0":
                        b, = a
                        wait(pe, bank_e[0].free(turn, step))
                        wait(pe, kkq_took.after(turn, 2))
                        for i in range(5):
                            m = nc.tensor.matmul(E[0][:, C * i:C * i + C], MT[:, 5 * b + i, :], eye64[:, :], start=True, stop=True)
                        m.then_inc(m_sum.sem, 1)
                    elif what == "inv1":
                        b, l = a
                        wait(pe, bank_e[0].free(turn, step))
                        wait(pe, t_made.after(turn, b, l - 1) if l > 1 else t0_made.after(turn, b))
                        for i, u in enumerate(batch(b, l)):
                            m = nc.tensor.matmul(E[0][:, C * i:C * i + C], MT[:, u, :],
                                                 Tc[:, u, :], start=True, stop=True)
                        m.then_inc(mt_sum.sem, 1)
                    elif what == "inv2":
                        b, l = a
                        wait(pe, bank_e[1].free(turn, step))
                        wait(pe, y_spread.after(turn, b, l))
                        wait(pe, tt_spread.after(turn, b, l - 1) if l > 1 else tt0_spread.after(turn, b))
                        if l < LEVELS - 1:
                            wait(pe, bank_e[0].free(turn, step))
                        for i, u in enumerate(batch(b, l)):
                            if l < LEVELS - 1:
                                nc.tensor.matmul(E[0][:, C * i:C * i + C], TT[:, u, :], Yc[:, b, i, :],
                                                 start=True, stop=True)
                            m = nc.tensor.matmul(E[1][:, C * i:C * i + C], Y[:, b, i, :],
                                                 TTc[:, u, :], start=True, stop=True)
                        m.then_inc(ty_sum.sem, 1)
                    elif what == "seq1":
                        c, = a
                        if c == 0 or c == SAMP:
                            wait(pe, s_zero.after(turn))
                            wait(pe, s_in.after(turn))
                        if c > 0:
                            wait(pe, s_made.after(turn, c - 1))
                        elif not (turn.fixed and p == 1):
                            wait(pe, s_made.after(turn, SAMP, ago=1))
                        s = S[:, 1 if c == SAMP else 0]
                        nc.tensor.matmul(F[0][:, 0:HD], kqk[:, c, 1:3, :].rearrange("p s c -> p (s c)"), s[:, 0, :], start=True, stop=True)
                        nc.tensor.matmul(F[0][:, HD:2 * HD], kqk[:, c, 2:4, :].rearrange("p s c -> p (s c)"), s[:, 1, :], start=True, stop=True
                                         ).then_inc(ks_sum.sem, 1)
                    elif what == "seq2":
                        c, = a
                        wait(pe, r_made.after(turn, c))
                        wait(pe, tt_spread.after(turn, c // 5, LEVELS - 1))
                        nc.tensor.matmul(F[1][:, 0:HD], TT[:, c, :], Rr[:, :], start=True, stop=True
                                         ).then_inc(vn_sum.sem, 1)
                    elif what == "seq3":
                        c, = a
                        wait(pe, oq_made.after(turn, c))
                        wait(pe, vn_made.after(turn, c))
                        if c == 0:
                            wait(pe, kc_made.after(turn, 2))
                        nc.tensor.matmul(F[0][:, 0:HD], QK[:, c, :], vn[:, :], start=True, stop=True)
                        nc.tensor.matmul(F[0][:, HD:3 * HD], kc[:, c, :], vnd[:].rearrange("p h v -> p (h v)"),
                                         start=True, stop=True).then_inc(os_sum.sem, 1)
                    elif what == "otr":
                        g, = a
                        wait(pe, o_normed.after(turn, g))
                        wait(pe, bank_e[g % 2].free(turn, step))
                        for i, u in enumerate(group(g)):
                            m = nc.tensor.transpose(E[g % 2][:, P * i:P * i + P], on[:, u, :], ident[:, :])
                        m.then_inc(o_turned.sem, 1)
            turns(pe, body)

        @block.scalar
        def _(act):
            act.wait_ge(ready, 1)

            def body(turn):
                p = turn.p
                again = not (turn.fixed and p == 1)
                for step in turn.steps():
                    what, *a = step
                    if what == "split":
                        n, = a
                        act.wait_ge(w_in[n % RAW_RING], 16 * (SUBS // RAW_RING * p + n // RAW_RING + 1))
                        if not (turn.fixed and SUBS * p + n < SPLIT_RING):
                            act.wait_ge(sub_used, SUBS * p + n - SPLIT_RING + 1)
                        nc.scalar.activation(w_hi[:, n % SPLIT_RING], w_raw[:, n % RAW_RING], ACT.Copy
                                             ).then_inc(hi_made, 1)
                    elif what == "evac":
                        t, = a
                        act.wait_ge(sub_used, SUBS * p + 2 * t + 2)
                        wait(act, kept.after(turn, t, back=2))
                        b = main[2 * (t % 2):2 * (t % 2) + 2]
                        x = xp[:, t % 2]
                        nc.scalar.activation(x[:, HIST:HIST + HALF], b[0][:, 0:HALF], ACT.Copy)
                        nc.scalar.activation(x[:, HIST + HALF:HIST + PROMPT], b[1][:, 0:PROMPT - HALF], ACT.Copy)
                        nc.scalar.activation(x[:, HIST + SAMP0:HIST + SAMP0 + SAMPLE], b[1][:, PROMPT - HALF:HALF], ACT.Copy)
                        tile = (p, PAIRS + p, 2 * PAIRS + 2 * p, 2 * PAIRS + 2 * p + 1)[t]
                        nc.scalar.activation(x[:, SAMP0:SAMP0 + HIST], hist[:, :, bass.ds(tile, 1)].rearrange("p w t -> p (w t)"),
                                             ACT.Copy).then_inc(xp_made.sem, 1)
                    elif what == "conv":
                        t, = a
                        wait(act, taps.after(turn, t, CONV_W - 1))
                        wait(act, silu.after(turn, t - 1) if t else z_made.after(turn, 5, ago=1))
                        nc.scalar.activation(th[:], y[:], ACT.Tanh).then_inc(tanh_y.sem, 1)
                    elif what == "square":
                        t, = a
                        wait(act, silu.after(turn, t))
                        wait(act, inverted.after(turn, 0, 1) if t else inverted.after(turn, 1, 1, ago=1))
                        nc.scalar.activation(sq[:], cqk[:, t], ACT.Square).then_inc(square.sem, 1)
                    elif what == "root":
                        t, = a
                        wait(act, sumsq.after(turn, t))
                        for e in range(2):
                            m = nc.scalar.activation(root[:, e * NPAD // 2:(e + 1) * NPAD // 2], E[e][:, 0:NPAD // 2],
                                                     ACT.Sqrt, bias=eps[:, 0:1])
                        m.then_inc(rooted.sem, 1)
                    elif what == "zevac":
                        t, = a
                        act.wait_ge(sub_used, SUBS * p + 2 * t + 2)
                        wait(act, z_made.after(turn, 4) if t == 5 else silu.after(turn, 3))
                        b = main[2 * (t % 2):2 * (t % 2) + 2]
                        for h in range(2):
                            m = nc.scalar.activation(zt[:, h * HALF:(h + 1) * HALF], b[h][:, 0:HALF], ACT.Tanh, scale=0.5)
                        m.then_inc(z_tanh.sem, 1)
                    elif what == "tab":
                        if again:
                            wait(act, o_gated.after(turn, 2, ago=1))
                            wait(act, s_out.after(turn, ago=1))
                        wait(act, z_made.after(turn, 5, ago=1))
                        nc.scalar.activation(zs[:], znew[:], ACT.Copy).then_inc(z_moved.sem, 1)
                        act.dma_start(S[:, 1], state_in[:, bass.ds(2 * (p - 1), 2), :]).then_inc(s_in.sem, 16)
                    elif what == "fetch":
                        if turn.behind:
                            wait(act, kkq_took.after(turn, 2))
                        for src, dst, sig in ((scratch["G"], dec, g_in), (scratch["beta"], bdec, b_in)):
                            for h in range(2):
                                act.dma_start(dst[64 * h:64 * h + 64, :], src[bass.ds(2 * p + h, 1), :].broadcast_to([64, NPAD])
                                              ).then_inc(sig.sem, 16)
                    elif what == "states":
                        wait(act, s_made.after(turn, SAMP))
                        for i in range(2):
                            act.dma_start(states_out[i][:, bass.ds(2 * (p - 1), 2), :], S[:, i]).then_inc(s_out.sem, 16)
                    elif what == "put":
                        wait(act, o_gated.after(turn, 2))
                        act.dma_start(o_all[:, bass.ds(2 * (p - 1), 2), :], ot[:]).then_inc(o_out.sem, 16)
                    elif what == "decay":
                        wait(act, g_sum.after(turn))
                        nc.scalar.activation(dec[:], dec[:], ACT.Exp).then_inc(dec_made.sem, 1)
                    elif what == "inv1":
                        b, l = a
                        wait(act, y_made.after(turn, b, l))
                        wait(act, ty_sum.after(turn, b, l - 1) if l > 1 else ty_sum.after(turn, b, LEVELS - 1, ago=1))
                        n = len(batch(b, l))
                        for h in range(2):
                            r = slice(64 * h, 64 * h + 64)
                            m = nc.scalar.activation(Y[r, b, 0:n, 64 * h:64 * h + 64], Yc[r, b, 0:n], ACT.Copy)
                        m.then_inc(y_spread.sem, 1)
                    elif what in ("inv0", "inv2"):
                        us = slice(batch(*a)[0], batch(*a)[-1] + 1)
                        made, spread = (t0_made, tt0_spread) if what == "inv0" else (t_made, tt_spread)
                        wait(act, made.after(turn, *a))
                        if what == "inv0" and again:
                            wait(act, vn_sum.after(turn, SAMP, ago=1))
                        for h in range(2):
                            r = slice(64 * h, 64 * h + 64)
                            m = nc.scalar.activation(TT[r, us, 64 * h:64 * h + 64], TTc[r, us], ACT.Copy)
                        m.then_inc(spread.sem, 1)
                    elif what == "seq2":
                        c, = a
                        wait(act, vn_sum.after(turn, c))
                        wait(act, os_sum.after(turn, c, back=1))
                        nc.scalar.activation(vn[:], F[1][:, 0:HD], ACT.Copy)
                        for h in range(2):
                            r = slice(64 * h, 64 * h + 64)
                            m = nc.scalar.activation(vnd[r, h], F[1][r, 0:HD], ACT.Copy)
                        m.then_inc(vn_made.sem, 1)
                    elif what == "square_o":
                        c, = a
                        wait(act, s_made.after(turn, c))
                        wait(act, o_summed.after(turn, c, back=1))
                        nc.scalar.activation(o_squares[:], on[:, c], ACT.Square, accum_out=osum[:, 0, c:c + 1]
                                             ).then_inc(o_summed.sem, 1)
                    elif what == "osq":
                        g, = a
                        us = slice(group(g)[0], group(g)[-1] + 1)
                        wait(act, o_summed.after(turn, group(g)[-1]))
                        wait(act, o_normed.after(turn, g, ago=1))
                        nc.scalar.activation(osum[:, 1, us], osum[:, 0, us], ACT.Sqrt, bias=eps[:, 0:1], scale=1.0 / HD
                                             ).then_inc(o_rooted.sem, 1)
            state_in = io["state_delta"].rearrange("l b h k v -> k (l b h) v")
            states_out = [io[name].rearrange("l b h k v -> k (l b h) v") for name in ("delta_p", "delta_s")]
            o_all = scratch["o"].rearrange("k p t -> p k t")
            turns(act, body)
            act.wait_ge(s_out.sem, 32 * PAIRS)
            act.wait_ge(o_out.sem, 16 * PAIRS)

        @block.vector
        def _(dve):
            dve.wait_ge(ready, 1)
            nc.vector.memset(eps[:], EPS)

            def table(i, u0, n, width):
                return ptab[:, 10 * i + u0:10 * i + u0 + n, None].broadcast_to([P, n, width])

            def body(turn):
                p = turn.p
                again = not (turn.fixed and p == 1)
                for step in turn.steps():
                    what, *a = step
                    if what == "split":
                        n, = a
                        dve.wait_ge(hi_made, SUBS * p + n + 1)
                        nc.vector.tensor_tensor(w_lo[:, n % SPLIT_RING], w_raw[:, n % RAW_RING],
                                                w_hi[:, n % SPLIT_RING].bitcast(F32), ALU.subtract).then_inc(lo_made, 1)
                    elif what == "tap":
                        t, w = a
                        tile = (p, PAIRS + p, 2 * PAIRS + 2 * p, 2 * PAIRS + 2 * p + 1)[t]
                        weight = cw[:, w, bass.ds(tile, 1)]
                        x = xp[:, t % 2, w:w + NPAD]
                        if w == 0:
                            wait(dve, xp_made.after(turn, t))
                            wait(dve, silu.after(turn, t - 1) if t else silu.after(turn, 3, ago=1))
                            m = nc.vector.tensor_scalar(y[:], x, weight, None, ALU.mult)
                        else:
                            wait(dve, taps.after(turn, t, w - 1))
                            m = nc.vector.scalar_tensor_tensor(out=y[:], in0=x, scalar=weight, in1=y[:],
                                                               op0=ALU.mult, op1=ALU.add)
                        m.then_inc(taps.sem, 1)
                    elif what == "conv":
                        t, = a
                        tile = (p, PAIRS + p, 2 * PAIRS + 2 * p, 2 * PAIRS + 2 * p + 1)[t]
                        wait(dve, taps.after(turn, t, CONV_W - 1))
                        x = xp[:, t % 2]
                        for s, c0 in ((0, PROMPT), (1, SAMP0 + SAMPLE)):
                            m = nc.vector.tensor_copy(cout[:, s, :, bass.ds(tile, 1)], x[:, c0:c0 + HIST, None])
                        m.then_inc(kept.sem, 1)
                    elif what == "silu":
                        t, = a
                        wait(dve, tanh_y.after(turn, t))
                        if t < 2:
                            if turn.behind:
                                wait(dve, kq_made.after(turn))
                            wait(dve, square.after(turn, t, ago=1))
                            out, i0, i1 = cqk[:, t], th[:], y[:]
                        else:
                            if turn.behind:
                                wait(dve, vnat_t.after(turn, 2))
                            out = cv[:, :, t - 2, :]
                            i0, i1 = (v[:].rearrange("p (u c) -> p u c", c=C) for v in (th, y))
                        nc.vector.scalar_tensor_tensor(out=out, in0=i0, scalar=1.0, in1=i1,
                                                       op0=ALU.add, op1=ALU.mult).then_inc(silu.sem, 1)
                    elif what == "recip":
                        t, e = a
                        wait(dve, rooted.after(turn, t))
                        if turn.behind:
                            wait(dve, kq_made.after(turn))
                        s = slice(e * NPAD // 2, (e + 1) * NPAD // 2)
                        nc.vector.reciprocal(rqk[:, t, s], root[:, s]).then_inc(inverted.sem, 1)
                    elif what == "zevac":
                        t, = a
                        wait(dve, z_tanh.after(turn, t))
                        if turn.behind:
                            wait(dve, z_moved.after(turn))
                        b = main[2 * (t % 2):2 * (t % 2) + 2]
                        for h in range(2):
                            s = slice(h * HALF, (h + 1) * HALF)
                            m = nc.vector.scalar_tensor_tensor(out=znew[:, t - 4, s], in0=zt[:, s], scalar=1.0,
                                                               in1=b[h][:, 0:HALF], op0=ALU.add, op1=ALU.mult)
                        m.then_inc(z_made.sem, 1)
                    elif what == "tab":
                        if again:
                            wait(dve, o_normed.after(turn, 2, ago=1))
                            wait(dve, s_out.after(turn, ago=1))
                        nc.vector.memset(S[:, 0], 0.0).then_inc(s_zero.sem, 1)
                        nc.vector.tensor_copy(ptab[:, None, :], tabs[:, bass.ds(p - 1, 1), :]).then_inc(tables.sem, 1)
                        wait(dve, tables.after(turn))
                    elif what == "decay":
                        wait(dve, g_in.after(turn, ago=1))
                        i = const["incl"][:, None, :].broadcast_to([P, UNITS, C])
                        st = const["strict"][:, None, :].broadcast_to([P, UNITS, C])
                        g3, b3, d3 = (v[:].rearrange("p (u c) -> p u c", c=C) for v in (dec, bdec, dec))
                        nc.vector.tensor_tensor(g3, g3, table(0, 0, UNITS, C), ALU.subtract).then_inc(g_sum.sem, 1)
                        wait(dve, g_sum.after(turn, n=1))
                        nc.vector.tensor_tensor(g3, g3, i, ALU.add).then_inc(g_sum.sem, 1)
                        wait(dve, b_in.after(turn, ago=1))
                        nc.vector.tensor_tensor(b3, b3, st, ALU.mult).then_inc(bdec_made.sem, 1)
                        wait(dve, bdec_made.after(turn, n=1))
                        wait(dve, dec_made.after(turn))
                        nc.vector.tensor_tensor(b3, b3, d3, ALU.mult).then_inc(bdec_made.sem, 1)
                    elif what == "kqn":
                        if again:
                            wait(dve, ks_sum.after(turn, SAMP, ago=1))
                        wait(dve, inverted.after(turn, 1, 1, ago=1))
                        c3 = [cqk[:, t].rearrange("p (u c) -> p u c", c=C) for t in range(2)]
                        r3 = [rqk[:, t].rearrange("p (u c) -> p u c", c=C) for t in range(2)]
                        two = [v[:, :, None, :].broadcast_to([P, UNITS, 2, C]) for v in (c3[1], r3[1])]
                        nc.vector.tensor_tensor(kqk[:, :, 0:2, :], *two, ALU.mult).then_inc(kq_made.sem, 1)
                        nc.vector.tensor_tensor(kqk[:, :, 3, :], c3[1], r3[1], ALU.mult).then_inc(kq_made.sem, 1)
                        nc.vector.scalar_tensor_tensor(out=kqk[:, :, 2, :], in0=c3[0], scalar=HD ** -0.5, in1=r3[0],
                                                       op0=ALU.mult, op1=ALU.mult).then_inc(kq_made.sem, 1)
                    elif what == "kkq":
                        g, = a
                        us = group(g)
                        n = len(us)
                        wait(dve, kkq_sum.after(turn, g))
                        wait(dve, bdec_made.after(turn))
                        if g == 0 and again:
                            wait(dve, os_sum.after(turn, SAMP, ago=1))
                        e3 = E[g % 2].rearrange("p (u x) -> p u x", x=P)
                        for h in range(2):
                            r = slice(64 * h, 64 * h + 64)
                            d3, b3 = (v[r, C * us[0]:C * us[0] + C * n].rearrange("p (u c) -> p u c", c=C) for v in (dec, bdec))
                            nc.vector.tensor_tensor(MT[r, us[0]:us[0] + n, 64 * h:64 * h + 64], e3[r, 0:n, 0:C], b3, ALU.mult)
                            m = nc.vector.tensor_tensor(QK[r, us[0]:us[0] + n, 64 - 64 * h:128 - 64 * h], e3[r, 0:n, C:2 * C],
                                                        d3, ALU.mult)
                        m.then_inc(kkq_took.sem, 1)
                    elif what in ("knat", "vnat"):
                        g, = a
                        us = group(g)
                        n = len(us)
                        turned, made, dst, column, e = ((knat_t, kc_made, kc, 2, 1 - g % 2) if what == "knat" else
                                                        (vnat_t, bv_made, bv, 3, g % 2))
                        wait(dve, turned.after(turn, g))
                        nc.vector.tensor_tensor(dst[:, us[0]:us[0] + n], E[e].rearrange("p (u x) -> p u x", x=P)[:, 0:n],
                                                table(column, us[0], n, P), ALU.mult).then_inc(made.sem, 1)
                    elif what == "inv0":
                        b, = a
                        us = slice(5 * b, 5 * b + 5)
                        eye, below = (v[:, None, :].broadcast_to([P, 5, C]) for v in (eye64, const["below"]))
                        wait(dve, m_sum.after(turn, b))
                        wait(dve, mt_sum.after(turn, b, LEVELS - 1, ago=1))
                        wait(dve, ty_sum.after(turn, b, LEVELS - 1, ago=1))
                        wait(dve, tt_spread.after(turn, b, LEVELS - 1, ago=1))
                        nc.vector.tensor_tensor(Tc[:, us], E[0][:, 0:5 * C].rearrange("p (u c) -> p u c", c=C), below, ALU.mult
                                                ).then_inc(t0_made.sem, 1)
                        for h in range(2):
                            r = slice(64 * h, 64 * h + 64)
                            above = const["above"][r, None, :].broadcast_to([64, 5, C])
                            m = nc.vector.tensor_tensor(TTc[r, us], MT[r, us, 64 * h:64 * h + 64], above, ALU.mult)
                        m.then_inc(t0_made.sem, 1)
                        wait(dve, t0_made.after(turn, b, n=1))
                        nc.vector.tensor_tensor(Tc[:, us], Tc[:, us], eye, ALU.add).then_inc(t0_made.sem, 1)
                        wait(dve, t0_made.after(turn, b, n=2))
                        nc.vector.tensor_tensor(TTc[:, us], TTc[:, us], eye, ALU.add).then_inc(t0_made.sem, 1)
                    elif what == "inv1":
                        b, l = a
                        wait(dve, mt_sum.after(turn, b, l))
                        last = (b, l - 1) if l > 1 else (b, LEVELS - 1)
                        wait(dve, y_spread.after(turn, *last, ago=0 if l > 1 else 1))
                        wait(dve, ty_sum.after(turn, *last, ago=0 if l > 1 else 1))
                        n = len(batch(b, l))
                        mask = const["level"][:, None, C * l:C * l + C].broadcast_to([P, n, C])
                        nc.vector.tensor_tensor(Yc[:, b, 0:n], E[0][:, 0:n * C].rearrange("p (u c) -> p u c", c=C), mask, ALU.mult
                                                ).then_inc(y_made.sem, 1)
                    elif what == "inv2":
                        b, l = a
                        wait(dve, ty_sum.after(turn, b, l))
                        n = len(batch(b, l))
                        e = [E[i][:, 0:n * C].rearrange("p (u c) -> p u c", c=C) for i in range(2)]
                        wait(dve, t_made.after(turn, b, l - 1) if l > 1 else t0_made.after(turn, b))
                        us = slice(5 * b, 5 * b + n)
                        if l < LEVELS - 1:
                            nc.vector.tensor_tensor(Tc[:, us], Tc[:, us], e[0], ALU.subtract).then_inc(t_made.sem, 1)
                        wait(dve, tt_spread.after(turn, b, l - 1) if l > 1 else tt0_spread.after(turn, b))
                        nc.vector.tensor_tensor(TTc[:, us], TTc[:, us], e[1], ALU.subtract
                                                ).then_inc(t_made.sem, 1 if l < LEVELS - 1 else 2)
                    elif what == "seq1":
                        c, = a
                        wait(dve, ks_sum.after(turn, c))
                        if c == 0:
                            wait(dve, bv_made.after(turn, 2))
                        wait(dve, vn_sum.after(turn, c, back=1))
                        for h in range(2):
                            r = slice(64 * h, 64 * h + 64)
                            m = nc.vector.scalar_tensor_tensor(out=Rr[r], in0=F[0][r, HD * h:HD * h + HD],
                                                               scalar=ptab[r, 10 + c:11 + c], in1=bv[r, c],
                                                               op0=ALU.mult, op1=ALU.add)
                        m.then_inc(r_made.sem, 1)
                        if c:
                            wait(dve, s_made.after(turn, c - 1))
                        for h in range(2):
                            r = slice(64 * h, 64 * h + 64)
                            m = nc.vector.tensor_scalar(oq[r], F[0][r, HD * (1 - h):HD * (2 - h)],
                                                        ptab[r, 40 + c:41 + c], None, ALU.mult)
                        m.then_inc(oq_made.sem, 1)
                    elif what == "seq3":
                        c, = a
                        wait(dve, os_sum.after(turn, c))
                        wait(dve, oq_made.after(turn, c))
                        if c == 0 and again:
                            wait(dve, o_turned.after(turn, 2, ago=1))
                        i = 1 if c == SAMP else 0
                        for h in range(2):
                            m = nc.vector.scalar_tensor_tensor(out=S[:, i, h], in0=S[:, i, h],
                                                               scalar=ptab[:, 50 + 10 * h + c:51 + 10 * h + c],
                                                               in1=F[0][:, HD * (1 + h):HD * (2 + h)],
                                                               op0=ALU.mult, op1=ALU.add)
                        nc.vector.tensor_tensor(on[:, c], oq[:], F[0][:, 0:HD], ALU.add).then_inc(s_made.sem, 1)
                    elif what == "osq":
                        g, = a
                        n = len(group(g))
                        us = slice(group(g)[0], group(g)[0] + n)
                        wait(dve, o_rooted.after(turn, g))
                        nc.vector.reciprocal(osum[:, 2, us], osum[:, 1, us]).then_inc(o_normed.sem, 1)
                        wait(dve, o_normed.after(turn, g, n=1))
                        nc.vector.tensor_tensor(on[:, us], on[:, us], osum[:, 2, us, None].broadcast_to([P, n, HD]), ALU.mult
                                                ).then_inc(o_normed.sem, 1)
                    elif what == "otr":
                        g, = a
                        us = group(g)
                        wait(dve, o_turned.after(turn, g))
                        if g == 0 and again:
                            wait(dve, o_out.after(turn, ago=1))
                        e3 = E[g % 2].rearrange("p (u x) -> p u x", x=P)
                        if g == 0:
                            wait(dve, z_moved.after(turn))
                        for h in range(2):
                            x0 = 64 - 64 * h
                            if g < 2:
                                parts = [(slice(4 * C * g, 4 * C * g + 4 * C), slice(0, 4), C)]
                            else:
                                parts = [(slice(TAIL * C, PROMPT), slice(0, 1), TAIL_N), (slice(PROMPT, NTOK), slice(1, 2), SAMPLE)]
                            for cols, u, n in parts:
                                m = nc.vector.scalar_tensor_tensor(
                                    out=ot[:, h, cols].rearrange("p (u c) -> p u c", c=n), in0=e3[:, u, x0:x0 + n],
                                    scalar=vec[:, 48:49], in1=zs[:, h, cols].rearrange("p (u c) -> p u c", c=n),
                                    op0=ALU.mult, op1=ALU.mult)
                        m.then_inc(o_gated.sem, 1)
            turns(dve, body)


def project_back(nc, top, io, keep, tag, kt, o_dram, w, residual, out=None):
    per = kt // KSUB
    raw_ring, split_ring, o_ring = 4, 2, 4
    with ExitStack() as ctx:
        def sb(name, shape, dt=F32):
            return ctx.enter_context(nc.sbuf_tensor(tag + name, shape, dt))

        def sem(name):
            return top.semaphore(tag + name)

        main = [ctx.enter_context(nc.psum_tensor(f"{tag}main{i}", [P, 512], F32)) for i in range(4)]
        E = [ctx.enter_context(nc.psum_tensor(f"{tag}E{i}", [P, 512], F32)) for i in range(2)]
        ident, ones = keep["const"]["ident"], keep["const"]["ones"]
        oh, ol = sb("oh", [P, kt, NTOK], F32R), sb("ol", [P, kt, NTOK], F32R)
        o_raw = sb("o_raw", [P, o_ring, NTOK])
        w_raw = sb("w_raw", [P, raw_ring, KSUB, P])
        w_hi = sb("w_hi", [P, split_ring, KSUB, P], F32R)
        w_lo = sb("w_lo", [P, split_ring, KSUB, P], F32R)
        res = sb("res", [P, 2, NTOK])
        h = sb("h", [P, 2, NTOK])
        sq = sb("sq", [P, NTOK])
        rows = sb("rows", [P, 4, P])
        rows_s = sb("rows_s", [SAMPLE, P])
        eps = sb("eps", [P, 1])

        w_in = [sem(f"w_in{i}") for i in range(raw_ring)]
        o_in = [sem(f"o_in{i}") for i in range(o_ring)]
        res_in = [sem(f"res_in{i}") for i in range(2)]
        h_out = [sem(f"h_out{i}") for i in range(2)]
        o_hi, o_lo, hi_made, lo_made, sub_used = (sem(x) for x in ("o_hi", "o_lo", "hi_made", "lo_made", "sub_used"))
        h_made, squared, summed, turned, copied = (sem(x) for x in ("h_made", "squared", "summed", "turned", "copied"))
        rooted, start, rows_out = sem("rooted"), sem("start"), sem("rows_out")
        block = ctx.enter_context(nc.Block())

        def tiles(engine, body):
            for m in (0, 1):
                body(m)
            with engine.Fori(2, KT - 2, 2) as i:
                body(i)
                body(i + 1, 1)
            for m in (KT - 2, KT - 1):
                body(m)

        def odd(m, second):
            return m % 2 if isinstance(m, int) else second

        def parts(m, second):
            known = isinstance(m, int)
            for j in range(2, per + 2):
                if not (known and per * m + j >= per * KT):
                    yield per * m + j, (per * odd(m, second) + j)

        @block.sync
        def _(sp):
            def part(g, at, column):
                if not (isinstance(g, int) and g < raw_ring):
                    sp.wait_ge(lo_made, g - raw_ring + 1)
                k0 = KSUB * (at % per)
                sp.dma_start(w_raw[:, at % raw_ring], w[:, k0:k0 + KSUB, bass.ds(column, P)]).then_inc(w_in[at % raw_ring], 16)

            def body(m, second=0):
                known, o = isinstance(m, int), odd(m, second)
                for j in range(per):
                    part(per * m + j, per * o + j, P * m)
                    if known and m == 0:
                        for k in range(KSUB * j, KSUB * (j + 1)):
                            if k >= o_ring:
                                sp.wait_ge(o_lo, k - o_ring + 1)
                            sp.dma_start(o_raw[:, k % o_ring], o_dram[k]).then_inc(o_in[k % o_ring], 16)
                if not (known and m < 2):
                    sp.wait_ge(h_made, m - 1)
                sp.dma_start(res[:, o], residual[bass.ds(m, 1)].rearrange("k p t -> p (k t)")).then_inc(res_in[o], 16)
            tiles(sp, body)

        @block.tensor
        def _(pe):
            pe.wait_ge(start, 1)

            def finish(m, second):
                o = odd(m, second)
                if out is None:
                    pe.wait_ge(squared, m + 1)
                    for e in range(2):
                        mm = nc.tensor.matmul(E[e][:, 0:HALF], ones[:, :], sq[:, e * HALF:(e + 1) * HALF],
                                              start=isinstance(m, int) and m == 0, stop=isinstance(m, int) and m == KT - 1,
                                              skip_group_check=True)
                    mm.then_inc(summed, 1)
                else:
                    pe.wait_ge(h_made, m + 1)
                    if not (isinstance(m, int) and m == 0):
                        pe.wait_ge(copied, m)
                    for c in range(4):
                        nc.tensor.transpose(E[0][:, P * c:P * c + P], h[:, o, N_META + P * c:N_META + P * c + P], ident[:, :])
                    nc.tensor.transpose(E[1][0:SAMPLE, 0:P], h[:, o, PROMPT:NTOK], ident[:, :]).then_inc(turned, 1)

            def body(m, second=0):
                known, o = isinstance(m, int), odd(m, second)
                for j in range(per):
                    pe.wait_ge(lo_made, per * m + j + 1)
                    if j == 0 and not (known and m < 2):
                        pe.wait_ge(h_made, m - 1)
                    for k in range(KSUB):
                        kk = KSUB * j + k
                        if known and m == 0:
                            pe.wait_ge(o_lo, kk + 1)
                        for wt, x in ((w_hi, oh), (w_hi, ol), (w_lo, oh)):
                            for e in range(2):
                                mm = nc.tensor.matmul(main[2 * o + e][:, 0:HALF], wt[:, (per * o + j) % split_ring, k, :],
                                                      x[:, kk, e * HALF:(e + 1) * HALF],
                                                      start=(kk == 0 and wt is w_hi and x is oh),
                                                      stop=(kk == kt - 1 and wt is w_lo))
                    mm.then_inc(sub_used, 1)
                    if j == 0 and not (known and m == 0):
                        finish(m - 1, 1 - o)
            tiles(pe, body)
            finish(KT - 1, 1)

        @block.scalar
        def _(act):
            def split(g, at):
                act.wait_ge(w_in[at % raw_ring], (g - at % raw_ring + raw_ring) * (16 // raw_ring))
                if not (isinstance(g, int) and g < split_ring):
                    act.wait_ge(sub_used, g - split_ring + 1)
                nc.scalar.activation(w_hi[:, at % split_ring], w_raw[:, at % raw_ring], ACT.Copy).then_inc(hi_made, 1)

            def body(m, second=0):
                known, o = isinstance(m, int), odd(m, second)
                if known and m == 0:
                    for g in range(per):
                        split(g, g)
                        for k in range(KSUB * g, KSUB * (g + 1)):
                            act.wait_ge(o_in[k % o_ring], 16 * (k // o_ring + 1))
                            nc.scalar.activation(oh[:, k], o_raw[:, k % o_ring], ACT.Copy).then_inc(o_hi, 1)
                    if per == 2:
                        split(2, 2)
                        split(3, 3)
                    else:
                        split(4, 4)
                        split(5, 5)
                else:
                    for g, at in parts(m, second):
                        split(g, at)
                act.wait_ge(h_made, m + 1)
                if out is None:
                    if not (known and m == 0):
                        act.wait_ge(summed, m)
                    nc.scalar.activation(sq[:], h[:, o], ACT.Square).then_inc(squared, 1)
                    act.dma_start(io["h1"][bass.ds(m, 1)].rearrange("k p t -> p (k t)"), h[:, o]).then_inc(h_out[o], 16)
                else:
                    act.wait_ge(turned, m + 1)
                    if not (known and m == 0):
                        act.wait_ge(rows_out, 32 * m)
                    nc.scalar.activation(rows[:].rearrange("p c d -> p (c d)"), E[0][:, 0:4 * P], ACT.Copy)
                    nc.scalar.activation(rows_s[:], E[1][0:SAMPLE, 0:P], ACT.Copy).then_inc(copied, 1)
                    act.wait_ge(copied, m + 1)
                    act.dma_start(out[0].rearrange("b (c p) d -> p (b c) d", p=P)[:, :, bass.ds(P * m, P)], rows[:]
                                  ).then_inc(rows_out, 16)
                    act.dma_start(out[1].rearrange("b p d -> p (b d)")[:, bass.ds(P * m, P)], rows_s[:]).then_inc(rows_out, 16)
            tiles(act, body)
            if out is None:
                act.wait_ge(summed, KT)
                for e in range(2):
                    a = nc.scalar.activation(sq[:, e * HALF:(e + 1) * HALF], E[e][:, 0:HALF], ACT.Sqrt,
                                             bias=eps[:, 0:1], scale=1.0 / D)
                a.then_inc(rooted, 1)
                for o in range(2):
                    act.wait_ge(h_out[o], 16 * KT // 2)
            else:
                act.wait_ge(rows_out, 32 * KT)

        @block.vector
        def _(dve):
            nc.vector.memset(eps[:], EPS).then_inc(start, 1)

            def split(g, at):
                dve.wait_ge(hi_made, g + 1)
                nc.vector.tensor_tensor(w_lo[:, at % split_ring], w_raw[:, at % raw_ring],
                                        w_hi[:, at % split_ring].bitcast(F32), ALU.subtract).then_inc(lo_made, 1)

            def body(m, second=0):
                known, o = isinstance(m, int), odd(m, second)
                if known and m == 0:
                    for g in range(per):
                        split(g, g)
                        for k in range(KSUB * g, KSUB * (g + 1)):
                            dve.wait_ge(o_hi, k + 1)
                            nc.vector.tensor_tensor(ol[:, k], o_raw[:, k % o_ring], oh[:, k].bitcast(F32), ALU.subtract
                                                    ).then_inc(o_lo, 1)
                    for g in range(per, per + 2):
                        split(g, g)
                else:
                    for g, at in parts(m, second):
                        split(g, at)
                dve.wait_ge(sub_used, per * m + per)
                if known and m < 2:
                    dve.wait_ge(res_in[o], 16)
                else:
                    dve.wait_ge(res_in[o], (m - o + 2) * 8)
                    if out is None:
                        dve.wait_ge(h_out[o], (m - o) * 8)
                        dve.wait_ge(squared, m - 1)
                    else:
                        dve.wait_ge(turned, m - 1)
                for e in range(2):
                    s = slice(e * HALF, (e + 1) * HALF)
                    v = nc.vector.tensor_tensor(h[:, o, s], res[:, o, s], main[2 * o + e][:, 0:HALF], ALU.add)
                v.then_inc(h_made, 1)
            tiles(dve, body)
            if out is None:
                dve.wait_ge(rooted, 1)
                nc.vector.reciprocal(keep["r"][:], sq[:])


SUBS_B = 8
BLOCKS = 6
QN = [P, P, P, P, PROMPT - 4 * P, SAMPLE]
Q0 = [0, P, 2 * P, 3 * P, 4 * P, PROMPT]
KN = [P, 2 * P, 3 * P, 4 * P, PROMPT, PAST + SAMPLE]


def key_blocks(i):
    n = -(-KN[i] // P)
    return n, KN[i] - P * (n - 1)


HEAD_PLACES = {
    "scale": [0.01, 7.01, 8.02, 14.01, 16.02, 17.02, 29.01, 31.01, 41.01, 46.02],
    "tab": [2.01],
    "split": [2.02, 8.01, 10.01, 17.01, 29.02, 32.01, 46.03, 51.01, 53.03, 63.01],
    "kcache": [5.01],
    "score": [11.01, 13.01, 21.01, 23.01, 32.03, 35.01],
    "vout": [15.01],
    "prob": [15.02, 16.01, 21.02, 26.01, 34.02, 44.02],
    "turn": [19.01, 22.01, 25.01, 31.02, 37.01, 57.01],
    "evac": [23.02, 46.01, 47.02, 62.02],
    "value": [23.03, 27.01, 30.01, 34.01, 58.01, 61.01],
    "fetchk": [32.02],
    "sumsq": [44.01, 51.02],
    "root": [47.01, 53.02],
    "recip": [50.01, 53.01, 61.02, 62.01],
    "fetch": [59.01],
    "kout": [64.01],
    "gate": [64.02],
    "put": [64.03],
}
LAST_HEAD_PLACES = {
    "tab": [0.01],
    "kcache": [0.02],
    "score": [0.03, 6.01, 12.01, 29.01, 41.01, 50.01],
    "kout": [2.01],
    "prob": [3.01, 19.01, 21.01, 35.01, 57.01, 58.01],
    "turn": [17.01, 28.01, 38.01, 43.02, 61.01, 62.01],
    "vout": [25.01],
    "value": [34.01, 43.01, 51.01, 58.02, 62.02, 62.03],
    "put": [64.01],
}


def head_order(places):
    blocks, once = [(i,) for i in range(BLOCKS)], [()]
    arguments = {
        "scale": [(n,) for n in range(SUBS_B + 2)], "split": [(n,) for n in range(SUBS_B + 2)],
        "evac": [(t,) for t in range(4)], "gate": once, "sumsq": [(0,), (2,)], "root": [(0,), (2,)],
        "recip": [(t, e) for t in (0, 2) for e in range(2)], "fetchk": once, "fetch": once,
        "tab": once, "kout": once, "vout": once, "kcache": once, "score": blocks, "prob": blocks, "turn": blocks,
        "value": blocks, "put": once}
    return place(places, arguments, SUBS_B * KSUB, set(list(arguments)[:list(arguments).index("tab")]), SUBS_B)


def forget_gates(nc, top, io, keep, scratch):
    with ExitStack() as ctx:
        def sb(name, shape, dt=F32):
            return ctx.enter_context(nc.sbuf_tensor("g_" + name, shape, dt))

        def sem(name):
            return top.semaphore("g_" + name)

        bank = [ctx.enter_context(nc.psum_tensor(f"g_bank{i}", [P, 512], F32)) for i in range(8)]
        ident, ones, vec = keep["const"]["ident"], keep["const"]["ones"], keep["vec"]
        xh, xl, r = keep["xh_b"], keep["xl_b"], keep["r"]
        hin = sb("hin", [P, 4, NTOK])
        xn = sb("xn", [P, 2, NTOK])
        wf = sb("wf", [P, KT, FH])
        fb = sb("fb", [FH, 1])
        cl_rows = sb("cl_rows", [P, PAST // P, FH])
        lf = sb("lf", [FH, 4, NTOK])
        cl = sb("cl", [FH, PAST + SAMPLE])
        fp, fs = sb("fp", [FH, PROMPT]), sb("fs", [FH, PAST + SAMPLE])
        lf_rows = sb("lf_rows", [P, BLOCKS, FH])
        fcol = keep["fcol"]
        crow = sb("crow", [P, 4, P])
        cout = keep["cout"][:].rearrange("p s w t -> p (s w t)")
        per_rows = HIST * CONV_TILES // 2
        h_in = [sem(f"h_in{i}") for i in range(4)]
        small, normed, high, low, used, wf_made = (sem(x) for x in ("small", "normed", "high", "low", "used", "wf_made"))
        step_a, step_v, step_p, stored, cleared = (sem(x) for x in ("step_a", "step_v", "step_p", "stored", "cleared"))
        conv_turned, conv_copied = sem("conv_turned"), sem("conv_copied")
        block = ctx.enter_context(nc.Block())

        @block.sync
        def _(sp):
            sp.dma_start(wf[:], io["kv_w"].rearrange("(k p) n -> p k n", p=P)[:, :, 2 * D:2 * D + FH]).then_inc(small, 16)
            sp.dma_start(fb[:], io["kv_f_bias"].rearrange("(h o) -> h o", o=1)).then_inc(small, 16)
            sp.dma_start(cl_rows[:], io["cache_logf"].rearrange("b (c p) h -> p (b c) h", p=P)).then_inc(small, 16)
            for k in range(KT):
                if k >= 4:
                    sp.wait_ge(normed, k - 3)
                sp.dma_start(hin[:, k % 4], io["h1"][k]).then_inc(h_in[k % 4], 16)
            sp.wait_ge(conv_copied, 1)
            for s, name in enumerate(("conv_p", "conv_s")):
                dst = io[name].rearrange("l b w (t p) -> (l b w t) p", p=P)
                for i in range(2):
                    sp.dma_start(dst[per_rows * i:per_rows * i + per_rows, :], crow[0:per_rows, 2 * s + i]).then_inc(stored, 16)
            sp.wait_ge(step_v, 5)
            sp.dma_start(scratch["FP"], fp[:]).then_inc(stored, 16)
            sp.dma_start(scratch["FS"], fs[:]).then_inc(stored, 16)
            sp.wait_ge(step_v, 6)
            sp.dma_start(io["logf_p"][:, 0:4 * P].rearrange("b (c p) h -> p (b c) h", p=P), lf_rows[:, 0:4]).then_inc(stored, 16)
            sp.dma_start(io["logf_p"].rearrange("b t h -> (b t) h")[4 * P:PROMPT], lf_rows[0:QN[4], 4]).then_inc(stored, 16)
            sp.dma_start(io["logf_s"].rearrange("b t h -> (b t) h"), lf_rows[0:SAMPLE, 5]).then_inc(stored, 16)
            sp.wait_ge(stored, 9 * 16)

        @block.tensor
        def _(pe):
            pe.wait_ge(small, 48)
            for c in range(PAST // P):
                m = nc.tensor.transpose(bank[2 + c // 4][0:FH, P * (c % 4):P * (c % 4) + P], cl_rows[:, c, :], ident[:, :])
            m.then_inc(step_p, 1)
            for i in range(4):
                m = nc.tensor.transpose(bank[6][0:per_rows, P * i:P * i + P], cout[:, per_rows * i:per_rows * i + per_rows], ident[:, :])
            m.then_inc(conv_turned, 1)
            pe.wait_ge(wf_made, 1)
            for k in range(KT):
                pe.wait_ge(normed, k + 1)
                for e in range(2):
                    m = nc.tensor.matmul(bank[e][0:FH, 0:HALF], wf[:, k, :], xn[:, k % 2, e * HALF:(e + 1) * HALF],
                                         start=(k == 0), stop=(k == KT - 1))
                m.then_inc(used, 1)
            pe.wait_ge(step_v, 5)
            for i in range(BLOCKS):
                m = nc.tensor.transpose(bank[4][0:QN[i], FH * i:FH * i + FH], lf[:, 3, Q0[i]:Q0[i] + QN[i]], ident[0:FH, 0:FH])
                src = fp[:, Q0[i]:Q0[i] + QN[i]] if i < 5 else fs[:, PAST:PAST + SAMPLE]
                m = nc.tensor.transpose(bank[5][0:QN[i], FH * i:FH * i + FH], src, ident[0:FH, 0:FH])
            m.then_inc(step_p, 1)

        @block.scalar
        def _(act):
            for k in range(KT):
                act.wait_ge(normed, k + 1)
                nc.scalar.activation(xh[:, k], xn[:, k % 2], ACT.Copy).then_inc(high, 1)
            act.wait_ge(used, KT)
            for e in range(2):
                s = slice(e * HALF, (e + 1) * HALF)
                nc.scalar.activation(lf[:, 0, s], bank[e][0:FH, 0:HALF], ACT.Identity, bias=fb[:, 0:1])
                a = nc.scalar.activation(lf[:, 1, s], bank[e][0:FH, 0:HALF], ACT.Abs, bias=fb[:, 0:1])
            a.then_inc(step_a, 1)
            act.wait_ge(step_a, 1)
            nc.scalar.activation(lf[:, 2], lf[:, 1], ACT.Exp, scale=-1.0).then_inc(step_a, 1)
            act.wait_ge(step_a, 2)
            nc.scalar.activation(lf[:, 1], lf[:, 2], ACT.Ln, bias=1.0).then_inc(step_a, 1)

        @block.vector
        def _(dve):
            def low_part(k):
                dve.wait_ge(high, k + 1)
                nc.vector.tensor_tensor(xl[:, k], xn[:, k % 2], xh[:, k].bitcast(F32), ALU.subtract).then_inc(low, 1)

            nc.vector.memset(fcol[:], 0.0).then_inc(cleared, 1)
            dve.wait_ge(small, 48)
            nc.vector.tensor_tensor(wf[:], wf[:], vec[:, 16:32, None].broadcast_to([P, KT, FH]), ALU.mult).then_inc(wf_made, 1)
            for k in range(KT):
                if k >= 2:
                    dve.wait_ge(used, k - 1)
                    dve.wait_ge(low, k - 1)
                dve.wait_ge(h_in[k % 4], 16 * (k // 4 + 1))
                nc.vector.tensor_tensor(xn[:, k % 2], hin[:, k % 4], r[:], ALU.mult).then_inc(normed, 1)
                if k:
                    low_part(k - 1)
            low_part(KT - 1)
            dve.wait_ge(conv_turned, 1)
            nc.vector.tensor_copy(crow[0:per_rows].rearrange("p c d -> p (c d)"), bank[6][0:per_rows, :]).then_inc(conv_copied, 1)
            dve.wait_ge(step_p, 1)
            for b in range(2):
                v = nc.vector.tensor_copy(cl[:, 512 * b:512 * b + 512], bank[2 + b][0:FH, :])
            v.then_inc(step_v, 1)
            dve.wait_ge(step_a, 3)
            nc.vector.scalar_tensor_tensor(out=lf[:, 3], in0=lf[:, 0], scalar=0.0, in1=lf[:, 1], op0=ALU.min,
                                           op1=ALU.subtract).then_inc(step_v, 1)
            dve.wait_ge(step_v, 2)
            nc.vector.tensor_copy(cl[:, PAST:], lf[:, 3, PROMPT:NTOK]).then_inc(step_v, 1)
            nc.vector.tensor_tensor_scan(fp[:], ones[0:FH, 0:1].broadcast_to([FH, PROMPT]), lf[:, 3, 0:PROMPT], 0.0,
                                         ALU.mult, ALU.add).then_inc(step_v, 1)
            dve.wait_ge(step_v, 3)
            nc.vector.tensor_tensor_scan(fs[:], ones[0:FH, 0:1].broadcast_to([FH, PAST + SAMPLE]), cl[:], 0.0,
                                         ALU.mult, ALU.add).then_inc(step_v, 1)
            dve.wait_ge(step_p, 2)
            dve.wait_ge(cleared, 1)
            for i in range(BLOCKS):
                nc.vector.tensor_copy(fcol[0:QN[i], :, i], bank[5][0:QN[i], FH * i:FH * i + FH])
                v = nc.vector.tensor_copy(lf_rows[0:QN[i], i], bank[4][0:QN[i], FH * i:FH * i + FH])
            v.then_inc(step_v, 1)
            nc.vector.tensor_scalar(vec[:, 50:51], vec[:, 50:51], HD ** -0.5, None, ALU.mult)


def attention_layer(nc, top, io, keep, scratch):
    order, last_order = head_order(HEAD_PLACES), head_order({**HEAD_PLACES, **LAST_HEAD_PLACES})
    raw_ring, split_ring = 4, 2
    with ExitStack() as ctx:
        def sb(name, shape, dt=F32):
            return ctx.enter_context(nc.sbuf_tensor("b_" + name, shape, dt))

        def sem(name):
            return top.semaphore("b_" + name)

        def signal(name, kind, per=1):
            return Signal(sem(name), kind, per)

        main = [ctx.enter_context(nc.psum_tensor(f"b_main{i}", [P, 512], F32)) for i in range(4)]
        E = [ctx.enter_context(nc.psum_tensor(f"b_E{i}", [P, 512], F32)) for i in range(2)]
        F = [ctx.enter_context(nc.psum_tensor(f"b_F{i}", [P, 512], F32)) for i in range(2)]
        const, vec, xh, xl = keep["const"], keep["vec"], keep["xh_b"], keep["xl_b"]
        ident, ones, causal = const["ident"], const["ones"], const["causal"]
        w_raw = sb("w_raw", [P, raw_ring, KSUB, P])
        w_hi = sb("w_hi", [P, split_ring, KSUB, P], F32R)
        w_lo = sb("w_lo", [P, split_ring, KSUB, P], F32R)
        raw = sb("raw", [P, 3, NTOK])
        sq, root, rr = sb("sq", [P, NTOK]), sb("root", [P, NTOK]), sb("rr", [P, 2, NTOK])
        kT, qT = sb("kT", [P, NTOK]), sb("qT", [P, NTOK])
        zt, znew, zs = sb("zt", [P, NTOK]), sb("znew", [P, NTOK]), sb("zs", [P, NTOK])
        kn, vn = sb("kn", [P, 4, P]), sb("vn", [P, 4, P])
        kn2, vn2 = sb("kn2", [SAMPLE, 2, P]), sb("vn2", [SAMPLE, 2, P])
        kc, vc = sb("kc", [P, PAST // P, P]), sb("vc", [P, PAST // P, P])
        kcT = sb("kcT", [P, PAST])
        fbp, fbs = sb("fbp", [P, PROMPT]), sb("fbs", [SAMPLE, PAST + SAMPLE])
        fq = sb("fq", [P, BLOCKS])
        pr = sb("pr", [P, 2, PAST + SAMPLE])
        stat = sb("stat", [P, 2, 4])
        pt = sb("pt", [P, 2, 512])
        fo = sb("fo", [P, NTOK])
        eps = sb("eps", [P, 1])

        w_in = [sem(f"w_in{i}") for i in range(raw_ring)]
        scaled, hi_made, lo_made, sub_used, start = (sem(x) for x in ("scaled", "hi_made", "lo_made", "sub_used", "start"))
        kept = signal("kept", "evac")
        gate = signal("gate", "gate")
        sumsq = signal("sumsq", "sumsq")
        rooted, inverted = signal("rooted", "root"), signal("inverted", "recip")
        moved = signal("moved", "tab")
        kq_made = signal("kq_made", "tab", 3)
        k_turned, k_took, k_out = signal("k_turned", "kout"), signal("k_took", "kout"), signal("k_out", "kout", 48)
        v_turned, v_took, v_out = signal("v_turned", "vout"), signal("v_took", "vout"), signal("v_out", "vout", 48)
        kc_in, vc_in = signal("kc_in", "fetchk", 16), signal("vc_in", "fetch", 16)
        fb_in = signal("fb_in", "fetch", 32)
        kc_turned, kc_took = signal("kc_turned", "kcache"), signal("kc_took", "kcache")
        scored, biased, masked, maxed, expd = (signal("scored", "score"), signal("biased", "score"), signal("masked", "score"),
                                               signal("maxed", "score", 2), signal("expd", "score"))
        inv_sum, prob = signal("inv_sum", "prob"), signal("prob", "prob")
        p_turned, pt_made = signal("p_turned", "turn"), signal("pt_made", "turn")
        summed, gated = signal("summed", "value"), signal("gated", "value")
        fo_out = signal("fo_out", "put", 16)

        bank_e = [
            Bank({"kout": (lambda: True, k_took), "kcache": (lambda: True, kc_took), "sumsq": (lambda t: True, rooted),
                  "turn": (lambda i: True, pt_made)}),
            Bank({"kout": (lambda: True, k_took), "kcache": (lambda: True, kc_took), "sumsq": (lambda t: True, rooted),
                  "value": (lambda i: True, gated), "score": (lambda i: i == 5, biased)}),
        ]
        bank_f = [
            Bank({"vout": (lambda: True, v_took), "score": (lambda i: i % 2 == 0 or i >= 4, biased)}),
            Bank({"vout": (lambda: True, v_took), "score": (lambda i: i % 2 == 1 or i >= 4, biased)}),
        ]

        def score_banks(i):
            if i < 4:
                return [(bank_f[i % 2], F[i % 2], 0, KN[i])]
            if i == 4:
                return [(bank_f[0], F[0], 0, 512), (bank_f[1], F[1], 512, KN[4] - 512)]
            return [(bank_f[0], F[0], 0, 512), (bank_f[1], F[1], 512, 512), (bank_e[1], E[1], PAST, SAMPLE)]

        def turns(engine, body):
            body(Turn(order, 0, behind=False))
            body(Turn(order, 1))
            with engine.Fori(2, FH - 1) as p:
                body(Turn(order, p))
            body(Turn(order, FH - 1, split=False))
            body(Turn(last_order, FH, front=False, before=order))

        block = ctx.enter_context(nc.Block())

        @block.sync
        def _(sp):
            kv = io["kv_w"].rearrange("(k p) n -> p k n", p=P)
            wb = io["b_w_in"].rearrange("l (k p) n -> p (l k) n", p=P)

            def body(turn):
                if not turn.front:
                    return
                p = turn.p
                sources = [(kv, P * p), (kv, D + P * p), (wb, P * p), (wb, D + P * p)]
                for n in range(SUBS_B):
                    if not (turn.fixed and SUBS_B * p + n < raw_ring):
                        sp.wait_ge(lo_made, SUBS_B * p + n - raw_ring + 1)
                    w, column = sources[n // 2]
                    k0 = KSUB * (n % 2)
                    sp.dma_start(w_raw[:, n % raw_ring], w[:, k0:k0 + KSUB, bass.ds(column, P)]
                                 ).then_inc(w_in[n % raw_ring], 16)
            turns(sp, body)

        @block.tensor
        def _(pe):
            pe.wait_ge(start, 1)

            def keep_busy(n):
                for _ in range(n):
                    nc.tensor.matmul(main[0][:, 0:HALF], w_hi[:, 0, 0, :], xh[:, 0, 0:HALF], start=True, stop=True)

            def body(turn):
                p = turn.p
                if not turn.front:
                    wait(pe, kept.after(turn, 2, ago=1))
                for step in turn.steps():
                    what, *a = step
                    if not turn.front and what in ("kout", "vout", "score", "turn", "value"):
                        keep_busy(BUSY_B)
                    if what == "kstep":
                        n, k = a
                        t = n // 2
                        if k == 0:
                            pe.wait_ge(lo_made, SUBS_B * p + n + 1)
                            if n % 2 == 0:
                                wait(pe, (kept.after(turn, 2, ago=1), gate.after(turn, ago=1), kept.after(turn, 0),
                                          kept.after(turn, 1))[t])
                        for hi, x in ((w_hi, xh), (w_hi, xl), (w_lo, xh)):
                            for e in range(2):
                                m = nc.tensor.matmul(main[2 * (t % 2) + e][:, 0:HALF], hi[:, n % split_ring, k, :],
                                                     x[:, KSUB * (n % 2) + k, e * HALF:(e + 1) * HALF],
                                                     start=(n % 2 == 0 and k == 0 and hi is w_hi and x is xh),
                                                     stop=(n % 2 == 1 and k == KSUB - 1 and hi is w_lo))
                        if k == KSUB - 1:
                            m.then_inc(sub_used, 1)
                    elif what == "sumsq":
                        t, = a
                        wait(pe, kept.after(turn, t))
                        for e in range(2):
                            wait(pe, bank_e[e].free(turn, step))
                            m = nc.tensor.matmul(E[e][:, 0:HALF], ones[:, :], sq[:, e * HALF:(e + 1) * HALF], start=True, stop=True)
                        m.then_inc(sumsq.sem, 1)
                    elif what in ("kout", "vout"):
                        src, b, guards, sig = ((kT[:], E, bank_e, k_turned) if what == "kout" else (raw[:, 1], F, bank_f, v_turned))
                        wait(pe, kq_made.after(turn))
                        for g in guards:
                            wait(pe, g.free(turn, step))
                        for c in range(4):
                            nc.tensor.transpose(b[0][:, P * c:P * c + P], src[:, P * c:P * c + P], ident[:, :])
                        for j in range(2):
                            i = 4 + j
                            m = nc.tensor.transpose(b[1][0:QN[i], P * j:P * j + P], src[:, Q0[i]:Q0[i] + QN[i]], ident[:, :])
                        m.then_inc(sig.sem, 1)
                    elif what == "kcache":
                        wait(pe, kc_in.after(turn, ago=1))
                        for g in bank_e:
                            wait(pe, g.free(turn, step))
                        for c in range(8):
                            m = nc.tensor.transpose(E[c // 4][:, P * (c % 4):P * (c % 4) + P], kc[:, c, :], ident[:, :])
                        m.then_inc(kc_turned.sem, 1)
                    elif what == "score":
                        i, = a
                        wait(pe, kq_made.after(turn))
                        if i == 5:
                            wait(pe, kc_took.after(turn))
                        for guard, b, k0, n in score_banks(i):
                            wait(pe, guard.free(turn, step))
                            keys = kT[:, k0:k0 + n] if i < 5 else (kcT[:, k0:k0 + n] if k0 < PAST else kT[:, PROMPT:NTOK])
                            m = nc.tensor.matmul(b[0:QN[i], 0:n], qT[:, Q0[i]:Q0[i] + QN[i]], keys, start=True, stop=True)
                        m.then_inc(scored.sem, 1)
                    elif what == "turn":
                        i, = a
                        wait(pe, prob.after(turn, i))
                        wait(pe, bank_e[0].free(turn, step))
                        nb, tail = key_blocks(i)
                        for j in range(nb):
                            n = tail if j == nb - 1 else P
                            out, src = E[0][0:n, QN[i] * j:QN[i] * j + QN[i]], pr[0:QN[i], i % 2, P * j:P * j + n]
                            if i < 4:
                                m = nc.tensor.transpose(out, src, ident[:, :])
                            else:
                                m = nc.tensor.matmul(out, src, ident[0:QN[i], 0:QN[i]], start=True, stop=True)
                        m.then_inc(p_turned.sem, 1)
                    elif what == "value":
                        i, = a
                        wait(pe, pt_made.after(turn, i))
                        wait(pe, v_took.after(turn))
                        if i == 5:
                            wait(pe, vc_in.after(turn, ago=1))
                        wait(pe, bank_e[1].free(turn, step))
                        nb, tail = key_blocks(i)
                        for j in range(nb):
                            n = tail if j == nb - 1 else P
                            if i == 5 and j < 8:
                                v = vc[:, j, :]
                            elif i < 4 or j < 4 and i == 4:
                                v = vn[:, j, :]
                            else:
                                v = vn2[0:n, i - 4, :]
                            m = nc.tensor.matmul(E[1][:, 0:QN[i]], v, pt[0:n, i % 2, QN[i] * j:QN[i] * j + QN[i]],
                                                 start=(j == 0), stop=(j == nb - 1))
                        m.then_inc(summed.sem, 1)
            turns(pe, body)

        @block.scalar
        def _(act):
            act.wait_ge(start, 1)
            kp, ks = (io[n].rearrange("b t h d -> (b t) h d") for n in ("k_p", "k_s"))
            vp, vs = (io[n].rearrange("b t h d -> (b t) h d") for n in ("v_p", "v_s"))
            cache_k, cache_v = (io[n].rearrange("b (c p) h d -> p (b c) h d", p=P) for n in ("cache_k", "cache_v"))

            def body(turn):
                p = turn.p
                again = not (turn.fixed and p == 1)
                for step in turn.steps():
                    what, *a = step
                    if what == "split":
                        n, = a
                        act.wait_ge(scaled, SUBS_B * p + n + 1)
                        if not (turn.fixed and SUBS_B * p + n < split_ring):
                            act.wait_ge(sub_used, SUBS_B * p + n - split_ring + 1)
                        nc.scalar.activation(w_hi[:, n % split_ring], w_raw[:, n % raw_ring], ACT.Copy).then_inc(hi_made, 1)
                    elif what == "evac":
                        t, = a
                        act.wait_ge(sub_used, SUBS_B * p + 2 * t + 2)
                        b = main[2 * (t % 2):2 * (t % 2) + 2]
                        if t < 3:
                            if turn.behind:
                                wait(act, kq_made.after(turn))
                                wait(act, v_turned.after(turn))
                            if t != 1:
                                wait(act, sumsq.after(turn, t, back=1))
                            for e in range(2):
                                s = slice(e * HALF, (e + 1) * HALF)
                                if t != 1:
                                    nc.scalar.activation(sq[:, s], b[e][:, 0:HALF], ACT.Square)
                                m = nc.scalar.activation(raw[:, t, s], b[e][:, 0:HALF], ACT.Copy)
                        else:
                            wait(act, gate.after(turn, ago=1))
                            for e in range(2):
                                m = nc.scalar.activation(zt[:, e * HALF:(e + 1) * HALF], b[e][:, 0:HALF], ACT.Tanh, scale=0.5)
                        m.then_inc(kept.sem, 1)
                    elif what == "root":
                        t, = a
                        wait(act, sumsq.after(turn, t))
                        wait(act, inverted.after(turn, 0, 1) if t else inverted.after(turn, 2, 1, ago=1))
                        for e in range(2):
                            m = nc.scalar.activation(root[:, e * HALF:(e + 1) * HALF], E[e][:, 0:HALF], ACT.Sqrt,
                                                     bias=eps[:, 0:1], scale=1.0 / HD)
                        m.then_inc(rooted.sem, 1)
                    elif what == "tab":
                        if again:
                            wait(act, gated.after(turn, 5, ago=1))
                        wait(act, gate.after(turn, ago=1))
                        nc.scalar.activation(zs[:], znew[:], ACT.Copy).then_inc(moved.sem, 1)
                    elif what in ("kout", "vout"):
                        turned, took, out, b, rows, rows2, dst, dst2 = (
                            (k_turned, k_took, k_out, E, kn, kn2, kp, ks) if what == "kout" else
                            (v_turned, v_took, v_out, F, vn, vn2, vp, vs))
                        wait(act, turned.after(turn))
                        if again:
                            wait(act, out.after(turn, ago=1))
                            wait(act, summed.after(turn, 5, ago=1))
                        nc.scalar.activation(rows[:].rearrange("p c d -> p (c d)"), b[0][:, 0:4 * P], ACT.Copy)
                        for j in range(2):
                            m = nc.scalar.activation(rows2[0:QN[4 + j], j], b[1][0:QN[4 + j], P * j:P * j + P], ACT.Copy)
                        m.then_inc(took.sem, 1)
                        wait(act, took.after(turn))
                        h = bass.ds(p - 1, 1)
                        act.dma_start(dst[0:4 * P, h, :].rearrange("(c p) h d -> p c (h d)", p=P), rows[:]).then_inc(out.sem, 16)
                        act.dma_start(dst[4 * P:PROMPT, h, :].rearrange("t h d -> t (h d)"), rows2[0:QN[4], 0]).then_inc(out.sem, 16)
                        act.dma_start(dst2[:, h, :].rearrange("t h d -> t (h d)"), rows2[0:SAMPLE, 1]).then_inc(out.sem, 16)
                    elif what == "kcache":
                        wait(act, kc_turned.after(turn))
                        if again:
                            wait(act, scored.after(turn, 5, ago=1))
                        for e in range(2):
                            m = nc.scalar.activation(kcT[:, 512 * e:512 * e + 512], E[e][:, :], ACT.Copy)
                        m.then_inc(kc_took.sem, 1)
                    elif what == "fetchk":
                        if turn.behind:
                            wait(act, kc_turned.after(turn))
                        act.dma_start(kc[:], cache_k[:, :, bass.ds(p, 1), :].rearrange("p c h d -> p c (h d)")).then_inc(kc_in.sem, 16)
                    elif what == "fetch":
                        if turn.behind:
                            wait(act, summed.after(turn, 5))
                            wait(act, biased.after(turn, 5))
                        act.dma_start(vc[:], cache_v[:, :, bass.ds(p, 1), :].rearrange("p c h d -> p c (h d)")).then_inc(vc_in.sem, 16)
                        act.dma_start(fbp[:], scratch["FP"][bass.ds(p, 1), :].broadcast_to([P, PROMPT])).then_inc(fb_in.sem, 16)
                        act.dma_start(fbs[:], scratch["FS"][bass.ds(p, 1), :].broadcast_to([SAMPLE, PAST + SAMPLE])
                                      ).then_inc(fb_in.sem, 16)
                    elif what == "score":
                        i, = a
                        q = slice(0, QN[i])
                        wait(act, maxed.after(turn, i))
                        nc.scalar.activation(pr[q, i % 2, 0:KN[i]], pr[q, i % 2, 0:KN[i]], ACT.Exp, bias=stat[q, i % 2, 1:2],
                                             accum_out=stat[q, i % 2, 2:3]).then_inc(expd.sem, 1)
                    elif what == "turn":
                        i, = a
                        wait(act, p_turned.after(turn, i))
                        wait(act, summed.after(turn, i, back=2))
                        nb, tail = key_blocks(i)
                        full = nb if tail == P else nb - 1
                        m = nc.scalar.activation(pt[:, i % 2, 0:QN[i] * full], E[0][:, 0:QN[i] * full], ACT.Copy)
                        if tail < P:
                            c = slice(QN[i] * full, QN[i] * nb)
                            m = nc.scalar.activation(pt[0:tail, i % 2, c], E[0][0:tail, c], ACT.Copy)
                        m.then_inc(pt_made.sem, 1)
                    elif what == "put":
                        wait(act, gated.after(turn, 5))
                        act.dma_start(scratch["fo"][bass.ds(p - 1, 1)].rearrange("k p t -> p (k t)"), fo[:]).then_inc(fo_out.sem, 16)
            turns(act, body)
            act.wait_ge(k_out.sem, 48 * FH)
            act.wait_ge(v_out.sem, 48 * FH)
            act.wait_ge(fo_out.sem, 16 * FH)

        @block.vector
        def _(dve):
            nc.vector.memset(eps[:], EPS).then_inc(start, 1)

            def body(turn):
                p = turn.p
                again = not (turn.fixed and p == 1)
                for step in turn.steps():
                    what, *a = step
                    if what == "scale":
                        n, = a
                        dve.wait_ge(w_in[n % raw_ring], 16 * (SUBS_B // raw_ring * p + n // raw_ring + 1))
                        g0 = (16 if n % SUBS_B < 4 else 32) + KSUB * (n % 2)
                        nc.vector.tensor_tensor(w_raw[:, n % raw_ring], w_raw[:, n % raw_ring],
                                                vec[:, g0:g0 + KSUB, None].broadcast_to([P, KSUB, P]), ALU.mult).then_inc(scaled, 1)
                    elif what == "split":
                        n, = a
                        dve.wait_ge(hi_made, SUBS_B * p + n + 1)
                        nc.vector.tensor_tensor(w_lo[:, n % split_ring], w_raw[:, n % raw_ring],
                                                w_hi[:, n % split_ring].bitcast(F32), ALU.subtract).then_inc(lo_made, 1)
                    elif what == "gate":
                        wait(dve, kept.after(turn, 3))
                        if turn.behind:
                            wait(dve, moved.after(turn))
                        b = main[2:4]
                        for e in range(2):
                            s = slice(e * HALF, (e + 1) * HALF)
                            m = nc.vector.scalar_tensor_tensor(out=znew[:, s], in0=zt[:, s], scalar=1.0, in1=b[e][:, 0:HALF],
                                                               op0=ALU.add, op1=ALU.mult)
                        m.then_inc(gate.sem, 1)
                    elif what == "recip":
                        t, e = a
                        wait(dve, rooted.after(turn, t))
                        if turn.behind:
                            wait(dve, kq_made.after(turn))
                        s = slice(e * HALF, (e + 1) * HALF)
                        nc.vector.reciprocal(rr[:, t // 2, s], root[:, s]).then_inc(inverted.sem, 1)
                    elif what == "tab":
                        wait(dve, inverted.after(turn, 2, 1, ago=1))
                        if again:
                            wait(dve, scored.after(turn, 5, ago=1))
                            wait(dve, k_turned.after(turn, ago=1))
                        for out, t, g in ((kT, 0, 49), (qT, 2, 50)):
                            nc.vector.scalar_tensor_tensor(out=out[:], in0=raw[:, t], scalar=vec[:, g:g + 1], in1=rr[:, t // 2],
                                                           op0=ALU.mult, op1=ALU.mult).then_inc(kq_made.sem, 1)
                        if again:
                            wait(dve, biased.after(turn, 5, ago=1))
                        nc.vector.tensor_copy(fq[:, None, :], keep["fcol"][:, bass.ds(p - 1, 1), :]).then_inc(kq_made.sem, 1)
                        wait(dve, kq_made.after(turn))
                    elif what == "score":
                        i, = a
                        q, slot = slice(0, QN[i]), i % 2
                        wait(dve, scored.after(turn, i))
                        if i == 0:
                            wait(dve, fb_in.after(turn, ago=1))
                        wait(dve, p_turned.after(turn, i, back=2))
                        fb = fbp if i < 5 else fbs
                        for _, b, k0, n in score_banks(i):
                            m = nc.vector.scalar_tensor_tensor(out=pr[q, slot, k0:k0 + n], in0=b[q, 0:n], scalar=fq[q, i:i + 1],
                                                               in1=fb[q, k0:k0 + n], op0=ALU.add, op1=ALU.subtract)
                        m.then_inc(biased.sem, 1)
                        wait(dve, biased.after(turn, i))
                        diag = pr[q, slot, KN[i] - QN[i]:KN[i]]
                        nc.vector.tensor_tensor(diag, diag, causal[q, q], ALU.add).then_inc(masked.sem, 1)
                        wait(dve, masked.after(turn, i))
                        nc.vector.tensor_reduce(stat[q, slot, 0:1], pr[q, slot, 0:KN[i]], AX.X, ALU.max).then_inc(maxed.sem, 1)
                        wait(dve, maxed.after(turn, i, n=1))
                        nc.vector.tensor_scalar(stat[q, slot, 1:2], stat[q, slot, 0:1], -1.0, None, ALU.mult).then_inc(maxed.sem, 1)
                    elif what == "prob":
                        i, = a
                        q, slot = slice(0, QN[i]), i % 2
                        wait(dve, expd.after(turn, i))
                        nc.vector.reciprocal(stat[q, slot, 3:4], stat[q, slot, 2:3]).then_inc(inv_sum.sem, 1)
                        wait(dve, inv_sum.after(turn, i))
                        nc.vector.tensor_scalar(pr[q, slot, 0:KN[i]], pr[q, slot, 0:KN[i]], stat[q, slot, 3:4], None, ALU.mult
                                                ).then_inc(prob.sem, 1)
                    elif what == "value":
                        i, = a
                        wait(dve, summed.after(turn, i))
                        if i == 0:
                            wait(dve, moved.after(turn))
                            if again:
                                wait(dve, fo_out.after(turn, ago=1))
                        c = slice(Q0[i], Q0[i] + QN[i])
                        nc.vector.scalar_tensor_tensor(out=fo[:, c], in0=E[1][:, 0:QN[i]], scalar=0.5, in1=zs[:, c],
                                                       op0=ALU.mult, op1=ALU.mult).then_inc(gated.sem, 1)
            turns(dve, body)


INPUTS = ["x_prompt", "x_sample", "cache_k", "cache_v", "cache_logf", "state_delta", "state_conv", "meta_tokens",
          "a_norm_g", "a_w_in", "a_conv_w", "a_a_log", "a_dt_bias", "a_out_norm_g", "a_w_out", "kv_norm_g", "kv_w",
          "kv_f_bias", "kv_k_norm_g", "b_norm_g", "b_w_in", "b_q_norm_g", "b_w_out"]
OUTPUTS = [("y_prompt", (1, SEQ, D)), ("y_sample", (1, SAMPLE, D)), ("delta_p", (1, 1, VH, HD, HD)),
           ("conv_p", (1, 1, HIST, CONV_DIM)), ("k_p", (1, PROMPT, FH, HD)), ("v_p", (1, PROMPT, FH, HD)),
           ("logf_p", (1, PROMPT, FH)), ("delta_s", (1, 1, VH, HD, HD)), ("conv_s", (1, 1, HIST, CONV_DIM)),
           ("k_s", (1, SAMPLE, FH, HD)), ("v_s", (1, SAMPLE, FH, HD)), ("logf_s", (1, SAMPLE, FH))]


def trunk(nc, io):
    with ExitStack() as top:
        def sb(name, shape, dt=F32):
            return top.enter_context(nc.sbuf_tensor(name, shape, dt))

        def dram(name, shape):
            return nc.dram_tensor(name, shape, F32, kind="Internal").ap()

        const_all = sb("const_all", [P, NCONST])
        keep = {"const_all": const_all, "const": {n: const_all[:, lo:hi] for n, (lo, hi) in CONST.items()},
                "vec": sb("vec", [P, 51]), "hist": sb("hist", [P, HIST, CONV_TILES]),
                "cw": sb("cw", [P, CONV_W, CONV_TILES]), "cout": sb("cout", [P, 2, HIST, CONV_TILES]),
                "fcol": sb("fcol", [P, FH, BLOCKS])}
        scratch = {"h0": dram("h0", (KT, P, NTOK)), "G": dram("G", (VH, NPAD)), "beta": dram("beta", (VH, NPAD)),
                   "o": dram("o", (VH, P, NTOK)), "FP": dram("FP", (FH, PROMPT)), "FS": dram("FS", (FH, PAST + SAMPLE)),
                   "fo": dram("fo", (FH, P, NTOK))}
        io["h1"] = dram("h1", (KT, P, NTOK))
        sems = Semaphores(nc)
        with ExitStack() as part:
            keep["tabs"] = part.enter_context(nc.sbuf_tensor("tabs", [P, PAIRS, 70], F32))
            for n in ("xh", "xl"):
                keep[n] = part.enter_context(nc.sbuf_tensor(n, [P, KT, NTOK], F32R))
            norm_and_gates(nc, sems, io, keep, scratch)
            delta_layer(nc, sems, io, keep, scratch)
        sems.retire()
        with ExitStack() as part:
            keep["r"] = part.enter_context(nc.sbuf_tensor("r", [P, NTOK], F32))
            project_back(nc, sems, io, keep, "a_", VH, scratch["o"], io["a_w_out"].rearrange("l (k p) n -> p (l k) n", p=P),
                         scratch["h0"])
            for n in ("xh_b", "xl_b"):
                keep[n] = part.enter_context(nc.sbuf_tensor(n, [P, KT, NTOK], F32R))
            forget_gates(nc, sems, io, keep, scratch)
            attention_layer(nc, sems, io, keep, scratch)
        project_back(nc, sems, io, keep, "y_", FH, scratch["fo"], io["b_w_out"].rearrange("l (k p) n -> p (l k) n", p=P),
                     io["h1"], (io["y_prompt"], io["y_sample"]))


def kernel(**inputs):
    import numpy as np
    import concourse.bacc as bacc
    from concourse.bass_utils import run_bass_kernel_spmd as run

    nc = bacc.Bacc("TRN2", target_bir_lowering=False, num_devices=1, dynamic_dma_scratch_size=4096)
    arrays = {"in_" + n: np.ascontiguousarray(inputs[n]) for n in INPUTS}
    arrays["in_consts"] = constants()
    io = {n[3:]: nc.dram_tensor(n, a.shape, F32, kind="ExternalInput").ap() for n, a in arrays.items()}
    for n, shape in OUTPUTS:
        io[n] = nc.dram_tensor("out_" + n, shape, F32, kind="ExternalOutput").ap()
    trunk(nc, io)
    r = run(nc, [arrays], core_ids=[0])
    return tuple(r.results[0]["out_" + n] for n, _ in OUTPUTS)
```
